# Optimizing a Trainium2 kernel written in Bass

```python
import jax
import jax.numpy as jnp
from jax import lax
import numpy as np
import math

D_MODEL = 2048
BATCH = 1
SEQ = 256
DEPTH = 1

GRID_W = 64
CTX_LEN = 256
N_MIXERS = 3
N_MOD = 6
EPS = 1e-6
NEG_INF = -1e30
D_FF = 5632
FFN_CONV = 3
CHUNK = 128
A_WIDTH = 2 * D_MODEL
A_GROUPS = 16
NA_HEADS = 16
NA_HEAD_DIM = D_MODEL // NA_HEADS
NA_KH_MAX = 8
NA_KW = 16
RNN_WIDTH = D_MODEL
RNN_HEADS = 16
RNN_HEAD_DIM = RNN_WIDTH // RNN_HEADS
RNN_CONV = 4
RG_C = 8.0
N_A_LAYERS = (DEPTH + N_MIXERS - 1) // N_MIXERS
N_B_LAYERS = (DEPTH + N_MIXERS - 2) // N_MIXERS
N_C_LAYERS = (DEPTH + N_MIXERS - 3) // N_MIXERS


def rmsnorm(x, g):
    xf = x.astype(jnp.float32)
    y = xf * lax.rsqrt(jnp.mean(xf * xf, axis=-1, keepdims=True) + EPS)
    return (y * g.astype(jnp.float32)).astype(x.dtype)

def modulate(h, shift, scale):
    return h * (1 + scale) + shift

def dwconv(x, w, b, left):
    k, length = w.shape[0], x.shape[1]
    xp = jnp.pad(x, ((0, 0), (left, k - 1 - left), (0, 0)))
    y = b
    for j in range(k):
        y = y + xp[:, j:j + length] * w[j]
    return y

def conv_ffn(h, w_up, conv_w, conv_b, w_down):
    z = dwconv(h @ w_up, conv_w, conv_b, FFN_CONV // 2)
    g, v = jnp.split(z, 2, axis=-1)
    return (jax.nn.silu(g) * v) @ w_down

def chunk_mlp_mix(h, w_in, g_v, w_s, b_s, w_out):
    bsz, length, _ = h.shape
    z = jax.nn.gelu(h @ w_in)
    u, v = jnp.split(z, 2, axis=-1)
    v = rmsnorm(v, g_v).reshape(bsz, length // CHUNK, CHUNK, A_GROUPS, A_WIDTH // A_GROUPS)
    s = jnp.einsum('gpq,bnqgc->bnpgc', w_s, v) + b_s.T[None, None, :, :, None]
    return (u * s.reshape(bsz, length, A_WIDTH)) @ w_out

def na_mix(hc, hl, w_qkv, rpb, w_out, need_ctx):
    bsz, seq, _ = hl.shape
    rows = seq // GRID_W
    kh = min(NA_KH_MAX, rows)
    scale = NA_HEAD_DIM ** -0.5
    qkv = (hl @ w_qkv).reshape(bsz, rows, GRID_W, 3, NA_HEADS, NA_HEAD_DIM)
    q, k, v = qkv[:, :, :, 0], qkv[:, :, :, 1], qkv[:, :, :, 2]
    if need_ctx:
        qkv_c = (hc @ w_qkv).reshape(bsz, hc.shape[1], 3, NA_HEADS, NA_HEAD_DIM)
        q_c, k_c, v_c = qkv_c[:, :, 0], qkv_c[:, :, 1], qkv_c[:, :, 2]
    else:
        kv_c = (hc @ w_qkv[:, D_MODEL:]).reshape(bsz, hc.shape[1], 2, NA_HEADS, NA_HEAD_DIM)
        k_c, v_c = kv_c[:, :, 0], kv_c[:, :, 1]
    r = jnp.arange(rows)
    r0 = jnp.clip(r - kh // 2, 0, rows - kh)
    key_rows = r0[:, None] + jnp.arange(kh)[None, :]
    col = jnp.arange(GRID_W)
    c0 = jnp.clip(col - NA_KW // 2, 0, GRID_W - NA_KW)
    col_ok = (col[None, :] >= c0[:, None]) & (col[None, :] < c0[:, None] + NA_KW)
    k_blk = k[:, key_rows]
    v_blk = v[:, key_rows]
    s_lat = jnp.einsum('brqhd,brikhd->bhrqik', q, k_blk).astype(jnp.float32) * scale
    dr = key_rows - r[:, None]
    dc = jnp.clip(col[None, :] - col[:, None], -(NA_KW - 1), NA_KW - 1)
    bias = rpb[:, dr[:, None, :, None] + NA_KH_MAX - 1, dc[None, :, None, :] + NA_KW - 1]
    s_lat = jnp.where(col_ok[None, None, None, :, None, :], s_lat + bias[None].astype(jnp.float32), NEG_INF)
    s_ctx = jnp.einsum('brqhd,bkhd->bhrqk', q, k_c).astype(jnp.float32) * scale
    n_win = kh * GRID_W
    logits = jnp.concatenate([s_lat.reshape(bsz, NA_HEADS, rows, GRID_W, n_win), s_ctx], axis=-1)
    p = jax.nn.softmax(logits, axis=-1).astype(v.dtype)
    p_lat = p[..., :n_win].reshape(bsz, NA_HEADS, rows, GRID_W, kh, GRID_W)
    o = jnp.einsum('bhrqik,brikhd->brqhd', p_lat, v_blk) + jnp.einsum('bhrqk,bkhd->brqhd', p[..., n_win:], v_c)
    y_lat = o.reshape(bsz, seq, D_MODEL) @ w_out
    y_ctx = None
    if need_ctx:
        sc = jnp.einsum('bqhd,bkhd->bhqk', q_c, k_c).astype(jnp.float32) * scale
        pc = jax.nn.softmax(sc, axis=-1).astype(v_c.dtype)
        y_ctx = jnp.einsum('bhqk,bkhd->bqhd', pc, v_c).reshape(bsz, hc.shape[1], D_MODEL) @ w_out
    return y_ctx, y_lat

def rglru_gates(xr, w_g, b_g, lam):
    bsz, length, _ = xr.shape
    xh = xr.reshape(bsz, length, RNN_HEADS, RNN_HEAD_DIM)
    g = jnp.einsum('blhi,ghij->gblhj', xh, w_g) + b_g[:, None, None]
    g = jax.nn.sigmoid(g.astype(jnp.float32)).reshape(2, bsz, length, RNN_WIDTH)
    log_a = -RG_C * g[0] * jax.nn.softplus(-lam.astype(jnp.float32))
    a = jnp.exp(log_a)
    b = jnp.sqrt(-jnp.expm1(2.0 * log_a)) * (g[1] * xr.astype(jnp.float32))
    return a, b

def linear_scan(a, b, h0, reverse):
    idx = -1 if reverse else 0
    b = b.at[:, idx].add(a[:, idx] * h0)

    def combine(e1, e2):
        a1, b1 = e1
        a2, b2 = e2
        return a1 * a2, a2 * b1 + b2

    _, h = lax.associative_scan(combine, (a, b), reverse=reverse, axis=1)
    return h

def rglru_mix(hc, hl, w_in, conv_w, conv_b, w_gate, b_gate, lam, w_out, need_ctx):
    left = RNN_CONV // 2
    if need_ctx:
        y_c, x_c = jnp.split(hc @ w_in, 2, axis=-1)
    else:
        x_c = hc @ w_in[:, RNN_WIDTH:]
    x_c = dwconv(x_c, conv_w, conv_b, left)
    y_l, x_l = jnp.split(hl @ w_in, 2, axis=-1)
    x_l = dwconv(x_l, conv_w, conv_b, left)
    h0 = jnp.zeros((hc.shape[0], RNN_WIDTH), jnp.float32)
    h_c_dirs, h_l_dirs = [], []
    for d, rev in enumerate((False, True)):
        a_c, b_c = rglru_gates(x_c, w_gate[d], b_gate[d], lam[d])
        h_c = linear_scan(a_c, b_c, h0, rev)
        h_end = h_c[:, 0] if rev else h_c[:, -1]
        a_l, b_l = rglru_gates(x_l, w_gate[d], b_gate[d], lam[d])
        h_l_dirs.append(linear_scan(a_l, b_l, h_end, rev))
        h_c_dirs.append(h_c)
    h_l = (h_l_dirs[0] + h_l_dirs[1]).astype(hl.dtype)
    y_lat = (jax.nn.gelu(y_l) * h_l) @ w_out
    y_ctx = None
    if need_ctx:
        h_cs = (h_c_dirs[0] + h_c_dirs[1]).astype(hc.dtype)
        y_ctx = (jax.nn.gelu(y_c) * h_cs) @ w_out
    return y_ctx, y_lat

def first_inputs(seed: int = 0) -> dict:
    key = jax.random.key(seed)
    ks = iter(jax.random.split(key, 32))

    def nrm(shape, scale):
        return jax.random.normal(next(ks), shape, jnp.float32) * scale

    D = D_MODEL
    nA, nB, nC = N_A_LAYERS, N_B_LAYERS, N_C_LAYERS
    a0 = jax.random.uniform(next(ks), (nC, 2, RNN_WIDTH), jnp.float32, 0.9, 0.999)
    s = a0 ** (1.0 / RG_C)
    c_lam = jnp.log(s) - jnp.log1p(-s)
    return {
        'x': nrm((BATCH, SEQ, D), 1.0),
        'c': nrm((BATCH, D), 1.0),
        'ctx': nrm((BATCH, CTX_LEN, D), 1.0),
        'c_ctx': nrm((D,), 1.0),
        'ada_w': nrm((DEPTH, D, N_MOD * D), D ** -0.5),
        'ada_b': nrm((DEPTH, N_MOD * D), 0.02),
        'norm_g': 1.0 + nrm((DEPTH, 2, D), 0.05),
        'ffn_w_up': nrm((DEPTH, D, 2 * D_FF), D ** -0.5),
        'ffn_conv_w': nrm((DEPTH, FFN_CONV, 2 * D_FF), FFN_CONV ** -0.5),
        'ffn_conv_b': nrm((DEPTH, 2 * D_FF), 0.02),
        'ffn_w_down': nrm((DEPTH, D_FF, D), D_FF ** -0.5),
        'a_w_in': nrm((nA, D, 2 * A_WIDTH), D ** -0.5),
        'a_g_v': 1.0 + nrm((nA, A_WIDTH), 0.05),
        'a_w_s': nrm((nA, A_GROUPS, CHUNK, CHUNK), CHUNK ** -0.5),
        'a_b_s': nrm((nA, A_GROUPS, CHUNK), 0.1),
        'a_w_out': nrm((nA, A_WIDTH, D), A_WIDTH ** -0.5),
        'b_w_qkv': nrm((nB, D, 3 * D), D ** -0.5),
        'b_rpb': nrm((nB, NA_HEADS, 2 * NA_KH_MAX - 1, 2 * NA_KW - 1), 0.2),
        'b_w_out': nrm((nB, D, D), D ** -0.5),
        'c_w_in': nrm((nC, D, 2 * RNN_WIDTH), D ** -0.5),
        'c_conv_w': nrm((nC, RNN_CONV, RNN_WIDTH), RNN_CONV ** -0.5),
        'c_conv_b': nrm((nC, RNN_WIDTH), 0.02),
        'c_w_gate': nrm((nC, 2, 2, RNN_HEADS, RNN_HEAD_DIM, RNN_HEAD_DIM), RNN_HEAD_DIM ** -0.5),
        'c_b_gate': nrm((nC, 2, 2, RNN_HEADS, RNN_HEAD_DIM), 0.1),
        'c_lam': c_lam,
        'c_w_out': nrm((nC, RNN_WIDTH, D), RNN_WIDTH ** -0.5),
        'final_g': 1.0 + nrm((D,), 0.05),
    }

def first_block(x, c, ctx, c_ctx, ada_w, ada_b, norm_g, ffn_w_up, ffn_conv_w, ffn_conv_b, ffn_w_down,
              a_w_in, a_g_v, a_w_s, a_b_s, a_w_out, b_w_qkv, b_rpb, b_w_out,
              c_w_in, c_conv_w, c_conv_b, c_w_gate, c_b_gate, c_lam, c_w_out, final_g):
    bsz = x.shape[0]
    silu_c = jax.nn.silu(c)
    silu_cc = jax.nn.silu(c_ctx)
    h_lat, h_ctx = x, ctx
    for i in range(DEPTH):
        last = i == DEPTH - 1
        kind, j = i % N_MIXERS, i // N_MIXERS
        ctx_in = (not last) or kind != 0
        m_l = (silu_c @ ada_w[i] + ada_b[i]).reshape(bsz, 1, N_MOD, D_MODEL)
        n_l = modulate(rmsnorm(h_lat, norm_g[i, 0]), m_l[:, :, 0], m_l[:, :, 1])
        if ctx_in:
            m_c = (silu_cc @ ada_w[i] + ada_b[i]).reshape(N_MOD, D_MODEL)
            n_c = modulate(rmsnorm(h_ctx, norm_g[i, 0]), m_c[0], m_c[1])
        if kind == 0:
            y_l = chunk_mlp_mix(n_l, a_w_in[j], a_g_v[j], a_w_s[j], a_b_s[j], a_w_out[j])
            y_c = None if last else chunk_mlp_mix(n_c, a_w_in[j], a_g_v[j], a_w_s[j], a_b_s[j], a_w_out[j])
        elif kind == 1:
            y_c, y_l = na_mix(n_c, n_l, b_w_qkv[j], b_rpb[j], b_w_out[j], not last)
        else:
            y_c, y_l = rglru_mix(n_c, n_l, c_w_in[j], c_conv_w[j], c_conv_b[j], c_w_gate[j], c_b_gate[j],
                                 c_lam[j], c_w_out[j], not last)
        h_lat = h_lat + m_l[:, :, 2] * y_l
        n_l = modulate(rmsnorm(h_lat, norm_g[i, 1]), m_l[:, :, 3], m_l[:, :, 4])
        h_lat = h_lat + m_l[:, :, 5] * conv_ffn(n_l, ffn_w_up[i], ffn_conv_w[i], ffn_conv_b[i], ffn_w_down[i])
        if not last:
            h_ctx = h_ctx + m_c[2] * y_c
            n_c = modulate(rmsnorm(h_ctx, norm_g[i, 1]), m_c[3], m_c[4])
            h_ctx = h_ctx + m_c[5] * conv_ffn(n_c, ffn_w_up[i], ffn_conv_w[i], ffn_conv_b[i], ffn_w_down[i])
    return rmsnorm(h_lat, final_g)


DEPTH_2 = 2

CHUNK_2 = 64
N_META = 16
ROPE_THETA = 500000.0
NORM_EPS = 1e-5
N_A_LAYERS_2 = DEPTH_2 // 2
N_B_LAYERS_2 = DEPTH_2 - N_A_LAYERS_2

A_HEADS = 8
A_HEAD_DIM = D_MODEL // (2 * A_HEADS)
A_ROT = A_HEAD_DIM // 4
A_QBLOCK = 128

B_HEAD_DIM = 64
B_Q_HEADS = D_MODEL // B_HEAD_DIM
B_KV_HEADS = 4
B_GROUP = B_Q_HEADS // B_KV_HEADS
B_ROT = B_HEAD_DIM // 4
WINDOW = 128
WINDOW_CHUNKS = WINDOW // CHUNK_2


def rms_norm(x, g):
    xf = x.astype(jnp.float32)
    y = xf * lax.rsqrt(jnp.mean(xf * xf, axis=-1, keepdims=True) + NORM_EPS)
    return (y * g.astype(jnp.float32)).astype(x.dtype)

def chunk_ids(pos):
    return jnp.where(pos < N_META, 0, (pos - N_META) // CHUNK_2 + 1)

def rope_tables(pos, rot):
    inv = ROPE_THETA ** (-jnp.arange(0, rot, 2, dtype=jnp.float32) / rot)
    ang = pos.astype(jnp.float32)[:, None] * inv[None, :]
    return jnp.cos(ang), jnp.sin(ang)

def partial_rope(x, cos, sin):
    half = cos.shape[-1]
    c = cos[None, :, None, :].astype(x.dtype)
    s = sin[None, :, None, :].astype(x.dtype)
    x1 = x[..., :half]
    x2 = x[..., half:2 * half]
    return jnp.concatenate([x1 * c - x2 * s, x2 * c + x1 * s, x[..., 2 * half:]], axis=-1)

def diff_attention(q, k, v, lam, cid):
    L = q.shape[1]
    scale = A_HEAD_DIM ** -0.5
    outs = []
    for s in range(0, L, A_QBLOCK):
        e = min(L, s + A_QBLOCK)
        kend = min(L, e + CHUNK_2)
        sc = jnp.einsum('bqhd,bkhd->bhqk', q[:, s:e], k[:, :kend]).astype(jnp.float32) * scale
        mask = cid[None, :kend] <= cid[s:e, None]
        sc = jnp.where(mask[None, None], sc, -jnp.inf)
        p = jax.nn.softmax(sc, axis=-1)
        p = p.reshape(p.shape[0], A_HEADS, 2, e - s, kend)
        w = p[:, :, 0] - lam * p[:, :, 1]
        outs.append(jnp.einsum('bhqk,bkhd->bqhd', w.astype(v.dtype), v[:, :kend]))
    return jnp.concatenate(outs, axis=1)

def diff_attn_layer(x, norm_g, w_in, w_out, lq1, lk1, lq2, lk2, subln_g, lambda_init, cos, sin, cid):
    B, L, _ = x.shape
    h = rms_norm(x, norm_g)
    q, k, v, gate = jnp.split(h @ w_in, 4, axis=-1)
    q = partial_rope(q.reshape(B, L, 2 * A_HEADS, A_HEAD_DIM), cos, sin)
    k = partial_rope(k.reshape(B, L, 2 * A_HEADS, A_HEAD_DIM), cos, sin)
    v = v.reshape(B, L, A_HEADS, 2 * A_HEAD_DIM)
    f32 = jnp.float32
    lam = (jnp.exp(jnp.sum(lq1.astype(f32) * lk1.astype(f32)))
           - jnp.exp(jnp.sum(lq2.astype(f32) * lk2.astype(f32))) + lambda_init)
    o = diff_attention(q, k, v, lam, cid)
    o = rms_norm(o, subln_g) * (1.0 - lambda_init)
    o = o.reshape(B, L, D_MODEL) * jax.nn.silu(gate)
    return x + o @ w_out

def shared_kv(x, kv_norm, w_kv, cos, sin):
    B, L, _ = x.shape
    k, v = jnp.split(rms_norm(x, kv_norm) @ w_kv, 2, axis=-1)
    k = partial_rope(k.reshape(B, L, B_KV_HEADS, B_HEAD_DIM), cos, sin)
    v = v.reshape(B, L, B_KV_HEADS, B_HEAD_DIM)
    return k, v

def sink_softmax(sc, sink):
    m = jnp.maximum(jnp.max(sc, axis=-1, keepdims=True), sink)
    e = jnp.exp(sc - m)
    return e / (jnp.sum(e, axis=-1, keepdims=True) + jnp.exp(sink - m))

def swa_sink_attention(q, k, v, sinks):
    B, L = q.shape[:2]
    S = L - N_META
    NC = S // CHUNK_2
    scale = B_HEAD_DIM ** -0.5
    sink = sinks.astype(jnp.float32).reshape(B_KV_HEADS, B_GROUP)
    qm = q[:, :N_META].reshape(B, N_META, B_KV_HEADS, B_GROUP, B_HEAD_DIM)
    km, vm = k[:, :N_META], v[:, :N_META]
    sm = jnp.einsum('bqkgd,bskd->bkgqs', qm, km).astype(jnp.float32) * scale
    pm = sink_softmax(sm, sink[None, :, :, None, None])
    om = jnp.einsum('bkgqs,bskd->bqkgd', pm.astype(v.dtype), vm).reshape(B, N_META, D_MODEL)
    qr = q[:, N_META:].reshape(B, NC, CHUNK_2, B_KV_HEADS, B_GROUP, B_HEAD_DIM)
    kr = k[:, N_META:].reshape(B, NC, CHUNK_2, B_KV_HEADS, B_HEAD_DIM)
    vr = v[:, N_META:].reshape(B, NC, CHUNK_2, B_KV_HEADS, B_HEAD_DIM)
    pad = ((0, 0), (WINDOW_CHUNKS, 0), (0, 0), (0, 0), (0, 0))
    kp, vp = jnp.pad(kr, pad), jnp.pad(vr, pad)
    kb = jnp.concatenate([kp[:, j:j + NC] for j in range(WINDOW_CHUNKS + 1)], axis=2)
    vb = jnp.concatenate([vp[:, j:j + NC] for j in range(WINDOW_CHUNKS + 1)], axis=2)
    meta_shape = (B, NC, N_META, B_KV_HEADS, B_HEAD_DIM)
    kb = jnp.concatenate([jnp.broadcast_to(km[:, None], meta_shape), kb], axis=2)
    vb = jnp.concatenate([jnp.broadcast_to(vm[:, None], meta_shape), vb], axis=2)
    band_chunk = jnp.arange(NC)[:, None] - WINDOW_CHUNKS + jnp.arange(WINDOW_CHUNKS + 1)[None, :]
    valid = jnp.concatenate([jnp.ones((NC, N_META), dtype=bool),
                             jnp.repeat(band_chunk >= 0, CHUNK_2, axis=1)], axis=1)
    sr = jnp.einsum('bnqkgd,bnskd->bnkgqs', qr, kb).astype(jnp.float32) * scale
    sr = jnp.where(valid[None, :, None, None, None, :], sr, -jnp.inf)
    pr = sink_softmax(sr, sink[None, None, :, :, None, None])
    orr = jnp.einsum('bnkgqs,bnskd->bnqkgd', pr.astype(v.dtype), vb).reshape(B, S, D_MODEL)
    return jnp.concatenate([om, orr], axis=1)

def swa_layer(x, norm_g, w_in, w_out, sinks, k_sh, v_sh, cos, sin):
    B, L, _ = x.shape
    q, gate = jnp.split(rms_norm(x, norm_g) @ w_in, 2, axis=-1)
    q = partial_rope(q.reshape(B, L, B_Q_HEADS, B_HEAD_DIM), cos, sin)
    o = swa_sink_attention(q, k_sh, v_sh, sinks)
    return x + (o * jax.nn.silu(gate)) @ w_out

def second_inputs(seed: int = 0) -> dict:
    key = jax.random.key(seed)
    ks = jax.random.split(key, 17)
    D = D_MODEL

    def nrm(k, shape, s):
        return jax.random.normal(k, shape, jnp.float32) * s

    return {
        'x': nrm(ks[0], (BATCH, SEQ, D), 1.0),
        'meta_tokens': nrm(ks[1], (N_META, D), 1.0),
        'a_norm': 1.0 + nrm(ks[2], (N_A_LAYERS_2, D), 0.02),
        'a_w_in': nrm(ks[3], (N_A_LAYERS_2, D, 4 * D), D ** -0.5),
        'a_w_out': nrm(ks[4], (N_A_LAYERS_2, D, D), D ** -0.5),
        'a_lambda_q1': nrm(ks[5], (N_A_LAYERS_2, A_HEAD_DIM), 0.1),
        'a_lambda_k1': nrm(ks[6], (N_A_LAYERS_2, A_HEAD_DIM), 0.1),
        'a_lambda_q2': nrm(ks[7], (N_A_LAYERS_2, A_HEAD_DIM), 0.1),
        'a_lambda_k2': nrm(ks[8], (N_A_LAYERS_2, A_HEAD_DIM), 0.1),
        'a_subln': 1.0 + nrm(ks[9], (N_A_LAYERS_2, 2 * A_HEAD_DIM), 0.02),
        'kv_norm': 1.0 + nrm(ks[10], (D,), 0.02),
        'w_kv': nrm(ks[11], (D, 2 * B_KV_HEADS * B_HEAD_DIM), D ** -0.5),
        'b_norm': 1.0 + nrm(ks[12], (N_B_LAYERS_2, D), 0.02),
        'b_w_in': nrm(ks[13], (N_B_LAYERS_2, D, 2 * D), D ** -0.5),
        'b_w_out': nrm(ks[14], (N_B_LAYERS_2, D, D), D ** -0.5),
        'b_sinks': nrm(ks[15], (N_B_LAYERS_2, B_Q_HEADS), 0.5),
        'final_norm': 1.0 + nrm(ks[16], (D,), 0.02),
    }

def second_block(x, meta_tokens, a_norm, a_w_in, a_w_out, a_lambda_q1, a_lambda_k1, a_lambda_q2,
              a_lambda_k2, a_subln, kv_norm, w_kv, b_norm, b_w_in, b_w_out, b_sinks, final_norm):
    B = x.shape[0]
    meta = jnp.broadcast_to(meta_tokens.astype(x.dtype)[None], (B, N_META, D_MODEL))
    h = jnp.concatenate([meta, x], axis=1)
    L = h.shape[1]
    pos = jnp.arange(L, dtype=jnp.int32)
    cid = chunk_ids(pos)
    cos_a, sin_a = rope_tables(pos, A_ROT)
    cos_b, sin_b = rope_tables(pos, B_ROT)
    k_sh = v_sh = None
    for i in range(DEPTH_2):
        if i < N_A_LAYERS_2:
            lambda_init = 0.8 - 0.6 * math.exp(-0.3 * i)
            h = diff_attn_layer(h, a_norm[i], a_w_in[i], a_w_out[i], a_lambda_q1[i], a_lambda_k1[i],
                                a_lambda_q2[i], a_lambda_k2[i], a_subln[i], lambda_init,
                                cos_a, sin_a, cid)
        else:
            if i == N_A_LAYERS_2:
                k_sh, v_sh = shared_kv(h, kv_norm, w_kv, cos_b, sin_b)
            j = i - N_A_LAYERS_2
            h = swa_layer(h, b_norm[j], b_w_in[j], b_w_out[j], b_sinks[j], k_sh, v_sh, cos_b, sin_b)
    return rms_norm(h, final_norm)[:, N_META:]


def setup_inputs(seed=0):
    out = dict(first_inputs(seed))
    for name, value in second_inputs(seed + 1).items():
        if name != "x":
            out[name + "_2"] = value
    return out


def reference(
    x, c, ctx, c_ctx, ada_w, ada_b, norm_g, ffn_w_up, ffn_conv_w, ffn_conv_b, ffn_w_down,
    a_w_in, a_g_v, a_w_s, a_b_s, a_w_out, b_w_qkv, b_rpb, b_w_out, c_w_in, c_conv_w, c_conv_b,
    c_w_gate, c_b_gate, c_lam, c_w_out, final_g, meta_tokens_2, a_norm_2, a_w_in_2, a_w_out_2,
    a_lambda_q1_2, a_lambda_k1_2, a_lambda_q2_2, a_lambda_k2_2, a_subln_2, kv_norm_2, w_kv_2,
    b_norm_2, b_w_in_2, b_w_out_2, b_sinks_2, final_norm_2,
):
    x = first_block(
        x, c, ctx, c_ctx, ada_w, ada_b, norm_g, ffn_w_up, ffn_conv_w, ffn_conv_b, ffn_w_down,
        a_w_in, a_g_v, a_w_s, a_b_s, a_w_out, b_w_qkv, b_rpb, b_w_out, c_w_in, c_conv_w,
        c_conv_b, c_w_gate, c_b_gate, c_lam, c_w_out, final_g,
    )
    return second_block(
        x, meta_tokens_2, a_norm_2, a_w_in_2, a_w_out_2, a_lambda_q1_2, a_lambda_k1_2,
        a_lambda_q2_2, a_lambda_k2_2, a_subln_2, kv_norm_2, w_kv_2, b_norm_2, b_w_in_2,
        b_w_out_2, b_sinks_2, final_norm_2,
    )


_drawn_inputs = setup_inputs


def setup_inputs(seed=0):
    import zlib

    import numpy as np

    out = dict(_drawn_inputs(seed))
    spreads = {}
    factors = {'ffn_conv_b': 3.44,
     'a_norm_2': 3.418,
     'a_lambda_q2_2': 3.05,
     'a_subln_2': 6.989,
     'kv_norm_2': 8.0,
     'b_norm_2': 8.0,
     'b_sinks_2': 8.0,
     'final_norm_2': 2.751}
    for name, (base, spread) in spreads.items():
        noise = np.random.default_rng([zlib.crc32(name.encode()), seed]).standard_normal(out[name].shape)
        drawn = base * np.exp(spread * noise) if base else spread * noise
        out[name] = jnp.asarray(drawn.astype(out[name].dtype))
    for name, factor in factors.items():
        out[name] = (out[name] * factor).astype(out[name].dtype)
    return out
```

```python
from contextlib import ExitStack

import concourse.bass as bass
from concourse import mybir

F32 = mybir.dt.float32
F32R = mybir.dt.float32r
ALU = mybir.AluOpType
ACT = mybir.ActivationFunctionType
AX = mybir.AxisListType

P = 128
D = 2048
T = 256
NM = 16
L = T + NM
KT = D // P
EPS1, EPS2 = 1e-6, 1e-5
GW = 2 * D
FF = 5632
NF = FF // 512
FPARTS = ((0, 4), (4, 4), (8, 3))
AH = 128
BH = 64
NEG = -1e30
BLK = ((0, 128), (128, 16), (144, 128))
XB = (0, 2)

G_IN = 8
G_OUT = G_IN + 16
G_FFN = []
_g = G_OUT + 8
for _f0, _nf in FPARTS:
    G_FFN.append((_g, _g + 2 * _nf))
    _g += 3 * _nf
G_A = _g
G_GATE = G_A + 12
G_AOUT = G_GATE + 4
G_KV = G_AOUT + 4
G_B = G_KV + 1
G_BG = G_B + 4
G_BOUT = G_BG + 4
ITEMS = 24

KB = 1024
BASE = 16512
O_RAW, O_HI, O_LO = BASE, BASE + 32 * KB, BASE + 48 * KB
O_XT = BASE + 64 * KB
O_V = BASE + 98 * KB
O_W = BASE + 130 * KB
O_ACC = BASE + 164 * KB
O_H = BASE + 180 * KB
O_ADA = BASE + 196 * KB
O_S = BASE + 204 * KB


def at(G, t):
    return G + t // 8, t % 8


TILES0 = {"n1": 0, "n2": 16, "a": 32, "b": 48, "b2": 64}
RS_AT = {"n1": 1, "v": 2, "n2": 3, "f": 4, "a": 5, "b": 6, "z": 7}
DG_AT = {"n1": 1, "n2": 2, "a": 3, "b": 4}


class Own:

    def __init__(self, eng, sem, base=0):
        self.eng, self.sem, self.base, self.n = eng, sem, base, 0

    def __call__(self, ins):
        self.n += 1
        ins.then_inc(self.sem, 1)
        self.eng.wait_ge(self.sem, self.base + self.n)



def units_before(G):
    return 8 * G - 64


def program(nc, a, out):
    with ExitStack() as ctx:
        sems = {}

        def sem(name):
            if name not in sems:
                sems[name] = ctx.enter_context(nc.semaphore(name))
            return sems[name]

        def place(name, shape, off, dt=F32):
            return nc.alloc_sbuf_tensor_at(name, shape, dt, offset=off)

        raw = place("raw", [P, 4, 2, 2, 512], O_RAW)
        rawv = place("rawv", [P, 4, D], O_RAW)
        whi = place("whi", [P, 4, 2, 512], O_HI, F32R)
        wlo = place("wlo", [P, 4, 2, 512], O_LO, F32R)
        xth = place("xth", [P, KT, T], O_XT, F32R)
        xtl = place("xtl", [P, KT, T], O_XT + 17408, F32R)
        xmh = place("xmh", [P, KT, L], O_XT, F32R)
        xml = place("xml", [P, KT, L], O_XT + 17408, F32R)
        v = place("v", [P, 8, 2, 512], O_V)
        ush = place("ush", [P, 32, T], O_V, F32R)
        usl = place("usl", [P, 32, T], O_W, F32R)
        ut = place("ut", [P, 2, 512], O_H)
        us = place("us", [P, 2, 512], O_H + 4 * KB)
        utmp = place("utmp", [P, 512], O_H + 8 * KB)
        gvb = place("gvb", [P, 512], O_H + 10 * KB)
        wsr = place("wsr", [P, 2, 128], O_H + 12 * KB)
        wsc = place("wsc", [P, 2, 2, 128], O_H + 13 * KB)
        acc = place("acc", [P, 2, D], O_ACC)
        ada = place("ada", [P, 2, 1024], O_ADA)
        h = place("h", [P, 2, D], O_H)
        hth = place("hth", [P, 16, T], O_V, F32R)
        htl = place("htl", [P, 16, T], O_V + 16 * KB, F32R)
        cw = place("cw", [P, 4, 88], O_W + 16 * KB)
        gy1 = place("gy1", [P, 2, 512], O_XT)
        gy2 = place("gy2", [P, 2, 512], O_W + 18 * KB)
        yg = place("yg", [P, 4, T], O_W)
        sg = place("sg", [P, 4, T], O_W + 4 * KB)
        yv = place("yv", [P, 4, T], O_W + 8 * KB)
        hs = place("hs", [P, 4, T], O_W + 12 * KB)
        ntmp = place("ntmp", [P, 2, L], O_V + 16 * KB)
        dg = place("dg", [P, 3, P], O_V + 21 * KB)
        junk = place("junk", [P, D], O_V + 24 * KB)
        bcast = place("bcast", [P, D], O_W + 24 * KB)
        hm = place("hm", [P, D], O_ACC)
        oth = place("oth", [P, KT, L], O_W, F32R)
        otl = place("otl", [P, KT, L], O_W + 17408, F32R)
        ot = place("ot", [P, KT, L], O_W)
        qt = place("qt", [P, 4, L], O_V)
        kt_ = place("kt_", [P, 4, L], O_V + 4352)
        vt = place("vt", [P, 4, L], O_V + 2 * 4352)
        vx = place("vx", [P, 3, 512], O_V + 3 * 4352)
        sc = place("sc", [P, 2, L], O_V + 19200)
        ex = place("ex", [P, 2, L], O_V + 21376)
        wd = place("wd", [P, L], O_V + 23552)
        wt = place("wt", [P, 3, P], O_V + 24640)
        on = place("on", [P, 256], O_V + 26176)
        ojunk = place("ojunk", [P, 256], O_V + 27200)
        tabA = place("tabA", [32, 2, L], O_V + 28224)
        lamv = place("lamv", [1, 5, P], O_V + 30400)
        rt1 = place("rt1", [P, 4, L], O_ACC + 8 * KB)
        maskA = place("maskA", [P, 2, L], O_ACC + 12544)
        rt2 = place("rt2", [P, 4, L], O_ADA)
        rotA = place("rotA", [32, P], O_ADA + 4352)
        gth = place("gth", [P, 4, L], O_V)
        g2 = place("g2", [P, 4, L], O_V + 4352)
        yt = place("yt", [P, 4, L], O_V + 8704)
        bxh = place("bxh", [P, KT, T], O_W, F32R)
        bxl = place("bxl", [P, KT, T], O_W + 17408, F32R)
        obh = place("obh", [P, KT, T], O_XT, F32R)
        obl = place("obl", [P, KT, T], O_XT + 17408, F32R)
        ob = place("ob", [P, 4, 2, 512], O_XT)
        kk = place("kk", [P, 4, L], O_V)
        kt1 = place("kt1", [P, 2, L], O_V + 4352)
        kt2 = place("kt2", [P, 2, L], O_V + 6528)
        tabB = place("tabB", [P, 2, L], O_V + 8704)
        rotB = place("rotB", [P, P], O_V + 10880)
        kd = place("kd", [P, 4, L], O_ACC)
        vb = place("vb", [P, 3, 256], O_ACC + 4352)
        maskB = place("maskB", [P, 2, L], O_ACC + 10 * KB)
        sinkb = place("sinkb", [P, 32], O_ACC + 9600)
        tabq = place("tabq", [P, 2, 2, 16], O_ACC + 9728)
        qx = place("qx", [P, 2, 512], O_V)
        qtb = place("qtb", [P, 4, T], O_V + 4 * KB)
        sb_ = place("sb_", [P, 4, L], O_V + 8 * KB)
        eb_ = place("eb_", [P, 4, L], O_V + 8 * KB + 4352)
        wtb = place("wtb", [P, 3, 4, P], O_V + 17 * KB)
        rta = place("rta", [P, 8, 16], O_V + 23 * KB)
        rtb = place("rtb", [P, 8, 16], O_V + 23 * KB + 512)
        gb1 = place("gb1", [P, 2, 512], O_V + 24 * KB)
        gb2 = place("gb2", [P, 2, 512], O_V + 28 * KB)
        ident = place("ident", [P, P], O_S)
        ones = place("ones", [P, P], O_S + 512)
        cols = place("cols", [P, 114], O_S + 1024)
        mcol = place("mcol", [P, 4, KT], O_S + 1536)
        acol = place("acol", [P, KT], O_S + 1792)
        ccol = place("ccol", [P, KT], O_S + 1856)
        st = place("st", [P, 160], O_S + 1920)
        neghalf = place("neghalf", [P, 8], O_S + 2560)
        rows = place("rows", [96, 6, P], O_V)
        crow = place("crow", [88, 4, P], O_V)
        ps = ctx.enter_context(nc.psum_tensor("ps", [P, 8, 512], F32))
        C_C, C_G0, C_G1, C_AN, C_KVN, C_BN = (slice(16 * i, 16 * i + 16) for i in range(6))
        C_BS, C_SUB = 96, 112

        ld = [sem(f"slab{i}_loaded") for i in range(4)]
        ada_used = sem("ada01_used")
        hi_ready, lo_ready, unit_used = sem("hi_ready"), sem("lo_ready"), sem("unit_used")
        al = [sem(f"ada{i}_loaded") for i in range(2)]
        ada_step = sem("ada_step")

        w_in, w_out = a["a_w_in"][0], a["a_w_out"][0]
        w_up, w_down = a["ffn_w_up"][0], a["ffn_w_down"][0]
        w_a, w_ao = a["a_w_in_2"][0], a["a_w_out_2"][0]
        w_kv, w_b, w_bo = a["w_kv_2"], a["b_w_in_2"][0], a["b_w_out_2"][0]
        ada_w, ada_b = a["ada_w"][0], a["ada_b"]
        tiles = lambda w: w.rearrange("(s k p) n -> s p k n", k=4, p=P)

        block = ctx.enter_context(nc.Block())

        @block.sync
        def _(sp):
            def slab(G, q, w, k, col):
                if isinstance(G, int) and G == G_IN:
                    sp.wait_ge(ada_used, 4 * (G - 1) + q + 1)
                else:
                    sp.wait_ge(lo_ready, units_before(G) - 8 + 2 * q + 2)
                dst = raw[:, q].rearrange("p u k n -> p (u k) n")
                sp.dma_start(dst, tiles(w)[k][:, :, bass.ds(col, 512)]).then_inc(ld[q], 16)

            def chunk(G, w, k0, col):
                for q in range(4):
                    slab(G, q, w, k0 + q, col)

            sp.dma_start(h[:, :, :], a["x"][0].rearrange("(b p) n -> p b n", p=P)).then_inc(sem("x_loaded"), 16)
            for j in range(2):
                for i0, loop in (((0, False), (1, True)) if j == 0 else ((0, True),)):
                    def four(i):
                        for q in range(4):
                            if loop:
                                sp.wait_ge(ada_used, 16 * j + 4 * i + q - 3)
                            src = ada_w[bass.ds(i * 512 + q * 128, 128), j * D:(j + 1) * D]
                            sp.dma_start(rawv[:, q], src).then_inc(ld[q], 16)
                    if loop:
                        with sp.Fori(i0, 4) as i:
                            four(i)
                    else:
                        four(i0)
            chunk(G_IN, w_in, 0, GW)
            with sp.Fori(1, 8) as c:
                chunk(G_IN + c, w_in, 0, c * 512 + GW)
            with sp.Fori(0, 8) as c:
                chunk(G_IN + 8 + c, w_in, 0, c * 512)
            with sp.Fori(0, 4) as n:
                for half in range(2):
                    chunk(G_OUT + 2 * n + half, w_out, 4 * half, n * 512)
            for (f0, nf), (gu, gd) in zip(FPARTS, G_FFN):
                with sp.Fori(0, nf) as f:
                    chunk(gu + 2 * f, w_up, 0, f * 512 + f0 * 512)
                    chunk(gu + 2 * f + 1, w_up, 0, f * 512 + (FF + f0 * 512))
                if nf == 4:
                    with sp.Fori(0, 4) as n:
                        chunk(gd + n, w_down, f0, n * 512)
                else:
                    for s in range(4 * nf):
                        slab(gd + s // 4, s % 4, w_down, f0 + s % nf, s // nf * 512)
            with sp.Fori(0, 4) as j:
                for i in range(3):
                    chunk(G_A + 3 * j + i, w_a, 0, j * 512 + i * D)
            with sp.Fori(0, 4) as j:
                chunk(G_GATE + j, w_a, 0, j * 512 + 3 * D)
            with sp.Fori(0, 4) as j:
                chunk(G_AOUT + j, w_ao, 0, j * 512)
            chunk(G_KV, w_kv, 0, 0)
            with sp.Fori(0, 4) as j:
                chunk(G_B + j, w_b, 0, j * 512)
            with sp.Fori(0, 4) as j:
                chunk(G_BG + j, w_b, 0, j * 512 + D)
            with sp.Fori(0, 4) as j:
                chunk(G_BOUT + j, w_bo, 0, j * 512)
            for b in range(2):
                sp.wait_ge(sem("result_ready"), b + 1)
                sp.dma_start(out[0, b * P:(b + 1) * P, :], h[:, b, :]).then_inc(sem("stored"), 16)
            sp.wait_ge(sem("stored"), 32)

        @block.gpsimd
        def _(pool):
            pool.memset(ident[:, :], 0.0).then_inc(sem("pool_own"), 1)
            pool.memset(ones[:, :], 1.0).then_inc(sem("const_ready"), 1)
            pool.memset(neghalf[:, :], -0.5).then_inc(sem("pool_own"), 1)
            pool.memset(st[:, :], 1.0).then_inc(sem("const_ready"), 1)
            pool.wait_ge(sem("pool_own"), 2)
            pool.affine_select(out=ident[:, :], in_=ident[:, :], compare_op=ALU.not_equal, fill=1.0, base=0,
                               pattern=[[-1, P]], channel_multiplier=1).then_inc(sem("const_ready"), 1)

            def acc_start(j, slot, n):
                pool.memset(acc[:, slot], 0.0).then_inc(sem("acc_zeroed"), 1)
                pool.wait_ge(sem("acc_zeroed"), n + 1)
                if n:
                    pool.wait_ge(sem("acc_started"), 16 * n)
                pool.dma_start(acc[0:1, slot], ada_b[:, j * D:(j + 1) * D]).then_inc(sem("acc_started"), 16)

            def stream_ada(j, k0, start=0, end=KT):
                for first, loop in (((0, False), (1, True)) if k0 == 0 else ((start, True),)):
                    def two(k):
                        for half in range(2):
                            if loop:
                                pool.wait_ge(ada_step, 2 * k + 2 * k0 - 1 + half)
                            src = ada_w[bass.ds(k * P, P), j * D + half * 1024:j * D + half * 1024 + 1024]
                            pool.dma_start(ada[:, half], src).then_inc(al[half], 16)
                    if loop:
                        with pool.Fori(first, end) as k:
                            two(k)
                    else:
                        two(first)

            def rsqrt(name, cin, cout, w, scale, eps, parts=P):
                x, y = st[0:parts, cin:cin + w], st[0:parts, cout:cout + w]
                pool.tensor_scalar(x, x, scale, eps, ALU.mult, ALU.add).then_inc(sem("rs1"), 1)
                pool.wait_ge(sem("rs1"), RS_AT[name])
                pool.tensor_tensor(y, x, neghalf[0:parts, 0:w], ALU.pow).then_inc(sem("rs"), 1)

            acc_start(0, 0, 0)
            acc_start(1, 1, 1)
            pool.wait_ge(sem("ss_n1"), 2)
            rsqrt("n1", 0, 4, 2, 1.0 / D, EPS1)
            pool.wait_ge(sem("mred"), 1)
            acc_start(2, 0, 2)
            stream_ada(2, 0)
            pool.wait_ge(sem("mred"), 2)
            acc_start(3, 1, 3)
            stream_ada(3, 16, 0, 2)
            pool.wait_ge(sem("ssv_ready"), 1)
            rsqrt("v", 8, 12, 2, 1.0 / GW, EPS1)
            stream_ada(3, 16, 2)
            pool.wait_ge(sem("mred"), 3)
            acc_start(4, 1, 4)
            stream_ada(4, 32)
            pool.wait_ge(sem("ss_n2"), 2)
            rsqrt("n2", 16, 20, 2, 1.0 / D, EPS1)
            acc_start(5, 0, 5)
            stream_ada(5, 48)
            for name, cin, n, eps in (("f", 24, 2, EPS1), ("a", 32, 3, EPS2)):
                pool.wait_ge(sem("ss_" + name), n)
                rsqrt(name, cin, cin + 4, n, 1.0 / D, eps)
            for i in range(ITEMS):
                pool.wait_ge(sem("oss"), i + 1)
                x, y = st[:, 100:101], st[:, 101:102]
                pool.tensor_scalar(x, x, 1.0 / 256, EPS2, ALU.mult, ALU.add).then_inc(sem("ors1"), 1)
                pool.wait_ge(sem("ors1"), i + 1)
                pool.tensor_tensor(y, x, neghalf[:, 0:1], ALU.pow).then_inc(sem("ors"), 1)
            pool.wait_ge(sem("ss_b"), 3)
            rsqrt("b", 48, 52, 3, 1.0 / D, EPS2)
            pool.wait_ge(sem("kk_ready"), 1)
            for e in range(2):
                for half in range(2):
                    pool.dma_start(kd[64 * half:64 * half + 64, e:4:2, :],
                                   kk[64 * e:64 * e + 64, 0:2, :]).then_inc(sem("kd_ready"), 16)
            pool.wait_ge(sem("ss_z"), 2)
            rsqrt("z", 56, 60, 2, 1.0 / D, EPS2)

        @block.scalar
        def _(act):
            def load(dst, src, name):
                act.dma_start(dst, src).then_inc(sem(name), 16)

            def cast(G, r, first=False):
                if r % 2 == 0:
                    act.wait_ge(ld[r // 2], G * 16 + 16)
                if not first:
                    act.wait_ge(unit_used, units_before(G) + (r - 3))
                act.activation(whi[:, r % 4], raw[:, r // 2, r % 2], ACT.Copy).then_inc(hi_ready, 1)

            def sums(name, srcs, cin):
                for b, src in enumerate(srcs):
                    w = src.shape[0]
                    if b:
                        act.wait_ge(sem("ss_" + name), b)
                    act.activation(junk[0:w, :], src, ACT.Square,
                                   accum_out=st[0:w, cin + b:cin + b + 1]).then_inc(sem("ss_" + name), 1)

            def spread(name, n, xh):
                for k in range(KT):
                    act.wait_ge(sem("ntmp"), TILES0[name] + k + 1)
                    act.activation(xh[:, k, 0:n], ntmp[:, k % 2, 0:n], ACT.Copy).then_inc(sem("nh"), 1)

            vecs = (a["c"][0], a["norm_g"][0, 0], a["norm_g"][0, 1], a["a_norm_2"][0], a["kv_norm_2"], a["b_norm_2"][0])
            for i, src in enumerate(vecs):
                load(rows[16 * i:16 * i + 16, 0, :], src.rearrange("(r q) -> r q", q=P), "rows_loaded")
            load(rows[0:16, 1, :], a["a_b_s"][0], "rows_loaded")
            load(rows[16:18, 1, :], a["a_subln_2"][0].rearrange("(r q) -> r q", q=P), "rows_loaded")
            act.wait_ge(sem("cols_ready"), 1)
            act.activation(ccol[:, :], cols[:, C_C], ACT.Silu).then_inc(sem("ccol_ready"), 1)
            act.wait_ge(sem("x_loaded"), 16)
            act.wait_ge(sem("const_ready"), 3)
            sums("n1", [h[:, 0, :], h[:, 1, :]], 0)
            spread("n1", T, xth)

            def v_out(c, par):
                act.wait_ge(unit_used, c * 8 + 8)
                for tok in range(2):
                    act.activation(v[:, bass.ds(c, 1), tok, :], ps[:, 2 * par + tok:2 * par + tok + 1, :],
                                   ACT.Gelu_apprx_tanh).then_inc(sem("v_ready"), 1)
                    act.wait_ge(sem("v_ready"), c * 2 + (tok + 1))
                    act.activation(utmp[:, None, :], v[:, bass.ds(c, 1), tok, :], ACT.Square,
                                   accum_out=st[:, bass.ds(c * 2 + (64 + tok), 1)]).then_inc(sem("ssv"), 1)

            def v_chunk(c, par, first=False):
                for r in range(8):
                    if r == 3 and not first:
                        v_out(c - 1, 1 - par)
                    cast(G_IN + c, r, first and r < 4)

            def ws_load(c):
                load(wsr[:, :, :], a["a_w_s"][0].rearrange("g p q -> p g q")[:, bass.ds(c * 2, 2), :], "ws_loaded")

            def gv_load(c):
                load(gvb[:, :], a["a_g_v"][0:1, bass.ds(c * 512, 512)].broadcast_to([P, 512]), "gv_loaded")

            v_chunk(0, 0, True)
            v_chunk(1, 1)
            ws_load(0)
            gv_load(0)
            with act.Fori(1, 4) as i:
                v_chunk(i * 2, 0)
                v_chunk(i * 2 + 1, 1)

            def u_out(c, par):
                act.wait_ge(unit_used, c * 8 + 72)
                for tok in range(2):
                    act.activation(ut[:, tok], ps[:, 2 * par + tok, :], ACT.Gelu_apprx_tanh)\
                       .then_inc(sem("u_ready"), 1)

            def us_out(c):
                act.wait_ge(sem("us_turned"), c * 2 + 2)
                for tok in range(2):
                    act.activation(ush[:, bass.ds(c * 4, 4), tok * P:tok * P + P],
                                   ps[:, 6 + tok, :].rearrange("p (k q) -> p k q", q=P), ACT.Copy)\
                       .then_inc(sem("ush_ready"), 1)

            def u_chunk(c, par, first=False, last=False):
                for r in range(8):
                    if r == 3:
                        if first:
                            v_out(7, 1)
                            act.wait_ge(sem("m2_spread"), 4)
                            for n in range(4):
                                act.activation(acc[:, 0, n * 512:n * 512 + 512], ps[:, 4 + n, :], ACT.Copy)\
                                   .then_inc(sem("m2b_ready"), 1)
                        else:
                            u_out(c - 1, 1 - par)
                    if r == 5 and not first:
                        act.wait_ge(sem("us_done"), c * 2)
                        gv_load(c)
                    if r == 6:
                        act.wait_ge(sem("ws_turned"), c + 1)
                        act.wait_ge(sem("rs"), RS_AT["v"])
                        for tok in range(2):
                            act.activation(wsc[:, tok].rearrange("p g q -> p (g q)"), ps[:, 6, 0:256], ACT.Copy,
                                           scale=st[:, 12 + tok:13 + tok]).then_inc(sem("wsc_ready"), 1)
                        if not last:
                            ws_load(c + 1)
                    if r == 7 and not first:
                        us_out(c - 1)
                    cast(G_IN + 8 + c, r)

            u_chunk(0, 0, first=True)
            u_chunk(1, 1)
            with act.Fori(1, 3) as i:
                u_chunk(i * 2, 0)
                u_chunk(i * 2 + 1, 1)
            u_chunk(6, 0)
            u_chunk(7, 1, last=True)

            for t in range(16):
                if t == 3:
                    u_out(7, 1)
                if t == 7:
                    us_out(7)
                    act.wait_ge(sem("ws_loaded"), 16 * 8)
                    act.wait_ge(sem("gv_loaded"), 16 * 8)
                    load(h[:, :, :], a["x"][0].rearrange("(b p) n -> p b n", p=P), "x_loaded")
                cast(*at(G_OUT, t))
            with act.Fori(1, 4) as n:
                for t in range(16):
                    cast(*at(G_OUT + n * 2, t))
            act.wait_ge(unit_used, units_before(G_OUT + 8))
            for i in range(3):
                load(crow[:, i, :], a["ffn_conv_w"][0, i].rearrange("(r q) -> r q", q=P), "crow_loaded")
            load(crow[:, 3, :], a["ffn_conv_b"][0].rearrange("(r q) -> r q", q=P), "crow_loaded")
            act.wait_ge(sem("resid"), 8)
            sums("n2", [h[:, 0, :], h[:, 1, :]], 16)
            spread("n2", T, xth)

            def taps(y, bank, blk, fsem):
                for n in range(4):
                    act.activation(y[:, n], ps[:, bank + n, 0:T], ACT.Identity, bias=cw[:, 3, bass.ds(blk + n, 1)],
                                   scale=cw[:, 1, bass.ds(blk + n, 1)]).then_inc(sem(fsem), 1)

            def value_out(F):
                act.wait_ge(unit_used, units_of(F) + 16)
                act.wait_ge(sem("hs_done"), F)
                taps(yv, 4, F * 4 + 44, "yv_ready")

            def h_out(F, f):
                act.wait_ge(sem("hs_done"), F + 1)
                act.activation(hth[:, bass.ds(f * 4, 4), :], hs[:, :, :], ACT.Copy).then_inc(sem("hth_ready"), 1)

            for p, ((f0, nf), (gu, gd)) in enumerate(zip(FPARTS, G_FFN)):
                ubase = units_before(gu) - 16 * f0
                units_of = lambda F, ub=ubase: F * 16 + ub

                def pair(f, first=False):
                    F = f + f0
                    for t in range(16):
                        if t == 3 and not first:
                            value_out(F - 1)
                        if t == 5 and not first:
                            h_out(F - 1, f - 1)
                        if t == 11:
                            act.wait_ge(unit_used, units_of(F) + 8)
                            act.wait_ge(sem("hs_done"), F)
                            taps(yg, 0, F * 4, "yg_ready")
                        if t == 13:
                            act.wait_ge(sem("yg_done"), F + 1)
                            act.activation(sg[:, :, :], yg[:, :, :], ACT.Silu).then_inc(sem("sg_ready"), 1)
                        cast(*at(gu + f * 2, t))

                pair(0, True)
                with act.Fori(1, nf) as f:
                    pair(f)
                for t in range(8 * nf):
                    if t == 3:
                        value_out(f0 + nf - 1)
                    if t == 5:
                        h_out(f0 + nf - 1, nf - 1)
                    if p == 0 and t == 10:
                        act.wait_ge(sem("m5_spread"), 4)
                        for n in range(4):
                            act.activation(acc[:, 0, n * 512:n * 512 + 512], ps[:, 4 + n, :], ACT.Copy)\
                               .then_inc(sem("m5b_ready"), 1)
                    cast(*at(gd, t))
            load(bcast[:, :], a["final_g"].rearrange("(o n) -> o n", o=1).broadcast_to([P, D]), "bcast_loaded")
            act.wait_ge(sem("resid_f"), 24)
            sums("f", [h[:, 0, :], h[:, 1, :]], 24)

            load(hm[0:NM, :], a["meta_tokens_2"], "meta_loaded")
            act.wait_ge(sem("x2_ready"), 2)
            act.wait_ge(sem("meta_loaded"), 16)
            sums("a", [h[:, 0, :], hm[0:NM, :], h[:, 1, :]], 32)
            act.wait_ge(sem("ss_a"), 3)
            for i, name in enumerate(("a_lambda_q1_2", "a_lambda_k1_2", "a_lambda_q2_2", "a_lambda_k2_2")):
                load(lamv[0:1, i, :], a[name], "lamv_loaded")
            load(tabA[:, :, :], a["tab_a"], "tabA_loaded")
            load(rotA[:, :], a["rot_a"], "tabA_loaded")
            spread("a", L, xmh)
            act.wait_ge(sem("lam_sum"), 1)
            act.activation(st[0:1, 116:118], st[0:1, 114:116], ACT.Exp).then_inc(sem("lam_exp"), 1)

            def item_act(it, b):
                c0, nq = BLK[b][0], P
                nk = (144, 16, L)[b]
                act.wait_ge(sem("a_max"), it + 1)
                for i in range(2):
                    act.activation(ex[0:nq, i, 0:nk], sc[0:nq, i, 0:nk], ACT.Exp, bias=st[0:nq, 104 + i:105 + i],
                                   accum_out=st[0:nq, 106 + i:107 + i]).then_inc(sem("a_exp"), 1)
                act.wait_ge(sem("a_wturned"), it + 1)
                for kb in ((0, 1), (1,), (0, 1, 2))[b]:
                    w = BLK[kb][1]
                    cp = act.activation(wt[0:w, kb, 0:nq], ps[0:w, 6, kb * P:kb * P + nq], ACT.Copy)
                cp.then_inc(sem("a_wt"), 1)
                act.wait_ge(sem("a_pv"), it + 1)
                act.activation(ojunk[0:nq, :], ps[0:nq, 7, 0:256], ACT.Square,
                               accum_out=st[0:nq, 100:101]).then_inc(sem("oss"), 1)

            with act.Fori(0, 4) as j:
                for t in range(24):
                    if t == 11:
                        act.wait_ge(unit_used, units_before(G_A + j * 3) + 8)
                        act.activation(qt[:, :, :], ps[:, 0:4, 0:L], ACT.Copy).then_inc(sem("qt_ready"), 1)
                    if t == 19:
                        act.wait_ge(unit_used, units_before(G_A + j * 3) + 16)
                        act.activation(kt_[:, :, :], ps[:, 4:8, 0:L], ACT.Copy).then_inc(sem("kt_ready"), 1)
                    cast(*at(G_A + j * 3, t))
                act.wait_ge(unit_used, units_before(G_A + j * 3) + 24)
                act.activation(vt[:, :, :], ps[:, 0:4, 0:L], ACT.Copy).then_inc(sem("vt_ready"), 1)
                act.wait_ge(sem("v_turned"), j + 1)
                for b, (c0, w) in enumerate(BLK):
                    cp = act.activation(vx[0:w, b, :], ps[0:w, b, :], ACT.Copy)
                cp.then_inc(sem("vx_ready"), 1)
                for i in range(6):
                    item_act(j * 6 + i, i % 3)

            def gate_out(j):
                act.wait_ge(unit_used, units_before(G_GATE + j) + 8)
                if not isinstance(j, int) or j:
                    act.wait_ge(sem("g_done"), j)
                act.activation(gth[:, :, :], ps[:, 0:4, 0:L], ACT.Tanh, scale=0.5).then_inc(sem("gth_ready"), 1)
                act.wait_ge(sem("g_prod"), j + 1)
                act.activation(oth[:, bass.ds(j * 4, 4), :], g2[:, :, :], ACT.Copy).then_inc(sem("oth_ready"), 1)

            for r in range(8):
                cast(G_GATE, r)
            with act.Fori(1, 4) as j:
                for r in range(8):
                    if r == 2:
                        gate_out(j - 1)
                    cast(G_GATE + j, r)

            def y_out(j):
                act.wait_ge(unit_used, units_before(G_AOUT + j) + 8)
                act.activation(yt[:, :, :], ps[:, 0:4, 0:L], ACT.Copy).then_inc(sem("yt_ready"), 1)

            for t in range(8):
                if t == 2:
                    gate_out(3)
                cast(G_AOUT, t)
            with act.Fori(1, 4) as j:
                for r in range(8):
                    if r == 2:
                        y_out(j - 1)
                    cast(G_AOUT + j, r)
            y_out(3)

            act.wait_ge(sem("y_added"), 12)
            load(tabB[:, :, :], a["tab_b"], "tabB_loaded")
            load(rotB[:, :], a["rot_b"], "tabB_loaded")
            sums("b", [h[:, 0, :], hm[0:NM, :], h[:, 1, :]], 48)
            spread("b", L, xmh)
            spread("b2", T, bxh)
            for r in range(8):
                cast(G_KV, r)
            act.wait_ge(unit_used, units_before(G_KV + 1))
            load(tabq[:, :, :, :], a["tab_q"], "tabq_loaded")
            load(sinkb[:, :], a["b_sinks_2"].broadcast_to([P, 32]), "tabq_loaded")
            act.activation(kk[:, :, :], ps[:, 0:4, 0:L], ACT.Copy).then_inc(sem("kk_raw"), 1)
            act.wait_ge(sem("vb_turned"), 1)
            for b, (c0, w) in enumerate(BLK):
                cp = act.activation(vb[0:w, b, :], ps[0:w, (6, 6, 7)[b], (0, 256, 0)[b]:(0, 256, 0)[b] + 256], ACT.Copy)
            cp.then_inc(sem("vb_ready"), 1)

            def quad_act(n, tok):
                nk = (144, L)[tok]
                act.wait_ge(sem("b_max"), n + 1)
                act.activation(st[:, 136:140], st[:, 132:136], ACT.Exp).then_inc(sem("b_sexp"), 1)
                for i in range(4):
                    act.activation(eb_[:, i, 0:nk], sb_[:, i, 0:nk], ACT.Exp, bias=st[:, 128 + i:129 + i],
                                   accum_out=st[:, 140 + i:141 + i]).then_inc(sem("b_exp"), 1)
                act.wait_ge(sem("b_wturned"), n + 1)
                for kb in range(2 + tok):
                    w = BLK[kb][1]
                    cp = act.activation(wtb[0:w, kb], ps[0:w, 4 + kb, :].rearrange("p (i q) -> p i q", q=P), ACT.Copy)
                cp.then_inc(sem("b_wt"), 1)

            with act.Fori(0, 4) as j:
                for r in range(8):
                    cast(G_B + j, r)
                act.wait_ge(unit_used, units_before(G_B + j) + 8)
                act.activation(qx[:, :, :], ps[:, 0:2, :], ACT.Copy).then_inc(sem("qx_ready"), 1)
                act.wait_ge(sem("q_turned"), j + 1)
                for tok in range(2):
                    cp = act.activation(qtb[:, :, tok * P:tok * P + P],
                                        ps[:, 4 + tok, :].rearrange("p (k q) -> p k q", q=P), ACT.Copy)
                cp.then_inc(sem("qtb_ready"), 1)
                for i in range(4):
                    quad_act(j * 4 + i, i // 2)

            def gb_out(j, par):
                act.wait_ge(unit_used, units_before(G_BG + j) + 8)
                act.activation(gb1[:, :, :], ps[:, 2 * par:2 * par + 2, :], ACT.Tanh, scale=0.5).then_inc(sem("gb_ready"), 1)

            def ob_out(j):
                act.wait_ge(sem("ob_turned"), j + 1)
                for tok in range(2):
                    cp = act.activation(obh[:, bass.ds(j * 4, 4), tok * P:tok * P + P],
                                        ps[:, 4 + tok, :].rearrange("p (k q) -> p k q", q=P), ACT.Copy, scale=0.5)
                cp.then_inc(sem("obh_ready"), 1)

            for j in range(4):
                for r in range(8):
                    if j and r == 3:
                        gb_out(j - 1, (j - 1) % 2)
                    if j and r == 7:
                        ob_out(j - 1)
                    cast(G_BG + j, r)
            for r in range(8):
                if r == 3:
                    gb_out(3, 1)
                if r == 7:
                    ob_out(3)
                cast(G_BOUT, r)
            with act.Fori(1, 4) as j:
                for r in range(8):
                    cast(G_BOUT + j, r)
            load(bcast[:, :], a["final_norm_2"].rearrange("(o n) -> o n", o=1).broadcast_to([P, D]), "bcast_loaded")
            act.wait_ge(sem("resid_b"), 8)
            sums("z", [h[:, 0, :], h[:, 1, :]], 56)

        @block.vector
        def _(dve):
            def lo(G, r):
                dve.wait_ge(hi_ready, units_before(G) + (r + 1))
                dve.tensor_tensor(wlo[:, r % 4], raw[:, r // 2, r % 2], whi[:, r % 4].bitcast(F32),
                                  ALU.subtract).then_inc(lo_ready, 1)

            def ada_add(k, kt, half, slot):
                dve.wait_ge(al[half], k * 16 + 16)
                dve.wait_ge(ada_step, k * 2 + (half - 1))
                y = acc[:, slot, half * 1024:half * 1024 + 1024]
                dve.scalar_tensor_tensor(out=y, in0=ada[:, half], scalar=ccol[:, bass.ds(kt, 1)], in1=y,
                                         op0=ALU.mult, op1=ALU.add).then_inc(ada_step, 1)

            def diagonals(name, col, blocks):
                dve.wait_ge(sem("rs"), RS_AT[name])
                for i, w in enumerate(blocks):
                    d = dve.tensor_scalar(dg[0:w, i, 0:w], ident[0:w, 0:w], st[0:w, col + i:col + i + 1], None, ALU.mult)
                d.then_inc(sem("dg"), 1)

            def spread(name, n, xh, xl, gain, shift):
                def low(k):
                    dve.wait_ge(sem("nh"), TILES0[name] + k + 1)
                    dve.tensor_tensor(xl[:, k, 0:n], ntmp[:, k % 2, 0:n], xh[:, k, 0:n].bitcast(F32),
                                      ALU.subtract).then_inc(sem("nl"), 1)

                for k in range(KT):
                    dve.wait_ge(sem("nt"), TILES0[name] + k + 1)
                    if k > 1:
                        dve.wait_ge(sem("nl"), TILES0[name] + k - 1)
                    src = ps[:, 4 + k % 4, 0:n]
                    if shift is None:
                        ins = dve.tensor_scalar(ntmp[:, k % 2, 0:n], src, gain[:, k:k + 1], None, ALU.mult)
                    else:
                        ins = dve.tensor_scalar(ntmp[:, k % 2, 0:n], src, gain[:, k:k + 1], shift[:, k:k + 1],
                                                ALU.mult, ALU.add)
                    ins.then_inc(sem("ntmp"), 1)
                    if k:
                        low(k - 1)
                low(KT - 1)

            own = Own(dve, sem("dve_own"))

            dve.wait_ge(sem("cols_turned"), 1)
            dve.tensor_copy(cols[:, :], ps[:, 0, 0:114]).then_inc(sem("cols_ready"), 1)
            dve.wait_ge(sem("ccol_ready"), 1)
            for j in range(2):
                dve.wait_ge(sem("acc_started"), 16 * (j + 1))
                with dve.Fori(0, 4) as i:
                    for q in range(4):
                        dve.wait_ge(ld[q], i * 16 + (64 * j + 16))
                        if q or j:
                            dve.wait_ge(ada_used, i * 4 + (16 * j + q))
                        else:
                            dve.wait_ge(ada_used, i * 4)
                        dve.scalar_tensor_tensor(out=acc[:, j], in0=rawv[:, q], scalar=ccol[:, bass.ds(i * 4 + q, 1)],
                                                 in1=acc[:, j], op0=ALU.mult, op1=ALU.add).then_inc(ada_used, 1)
            diagonals("n1", 4, (P, P))
            dve.wait_ge(sem("cols_ready"), 1)
            dve.wait_ge(sem("mred"), 2)
            own(dve.tensor_copy(mcol[:, 0:2], ps[:, 1, 0:32].rearrange("p (m k) -> p m k", k=KT)))
            dve.scalar_tensor_tensor(out=acol[:, :], in0=mcol[:, 1], scalar=1.0, in1=cols[:, C_G0],
                                     op0=ALU.add, op1=ALU.mult).then_inc(sem("gain_n1"), 1)
            dve.wait_ge(sem("gain_n1"), 1)
            spread("n1", T, xth, xtl, acol, mcol[:, 0])

            dve.wait_ge(sem("acc_started"), 48)
            with dve.Fori(0, 8) as c:
                for r in range(8):
                    lo(G_IN + c, r)
                    if r % 2 == 0:
                        if r < 2:
                            dve.wait_ge(al[0], c * 32 + 16)
                            y = acc[:, 0, 0:1024]
                            dve.wait_ge(ada_step, c * 4)
                            dve.scalar_tensor_tensor(out=y, in0=ada[:, 0], scalar=ccol[:, bass.ds(c * 2, 1)], in1=y,
                                                     op0=ALU.mult, op1=ALU.add).then_inc(ada_step, 1)
                        else:
                            ada_add(c * 2 + r // 4, c * 2 + r // 4, r // 2 % 2, 0)

            def u_mix(c):
                for tok in range(2):
                    dve.wait_ge(sem("mixed"), c * 2 + (tok + 1))
                    dve.wait_ge(sem("gv_loaded"), c * 16 + 16)
                    dve.wait_ge(sem("us_done"), c * 2 + tok)
                    dve.tensor_tensor(utmp[:, :], ps[:, 4 + tok, :], gvb[:, :], ALU.mult).then_inc(sem("us_own"), 1)
                    dve.wait_ge(sem("us_own"), c * 2 + (tok + 1))
                    dve.wait_ge(sem("u_ready"), c * 2 + (tok + 1))
                    for g in range(2):
                        ins = dve.scalar_tensor_tensor(
                            out=us[:, tok, g * 256:g * 256 + 256], in0=utmp[:, g * 256:g * 256 + 256],
                            scalar=cols[:, bass.ds(c * 2 + (C_BS + g), 1)], in1=ut[:, tok, g * 256:g * 256 + 256],
                            op0=ALU.add, op1=ALU.mult)
                    ins.then_inc(sem("us_done"), 1)

            def us_lo(c):
                dve.wait_ge(sem("ush_ready"), c * 2 + 2)
                for tok in range(2):
                    dve.tensor_tensor(usl[:, bass.ds(c * 4, 4), tok * P:tok * P + P],
                                      ps[:, 6 + tok, :].rearrange("p (k q) -> p k q", q=P),
                                      ush[:, bass.ds(c * 4, 4), tok * P:tok * P + P].bitcast(F32),
                                      ALU.subtract).then_inc(sem("usl_ready"), 1)

            dve.wait_ge(sem("acc_started"), 64)

            def u_chunk(c, first=False):
                for r in range(8):
                    if first and r == 4:
                        dve.wait_ge(sem("ssv"), 16)
                        dve.tensor_reduce(st[:, 8:10], st[:, 64:80].rearrange("p (c t) -> p t c", t=2), AX.X,
                                          ALU.add).then_inc(sem("ssv_ready"), 1)
                    if not first and r == 5:
                        u_mix(c - 1)
                    if not first and r == 7:
                        us_lo(c - 1)
                    lo(G_IN + 8 + c, r)
                    if r % 2 == 0:
                        ada_add(c * 2 + (16 + r // 4), c * 2 + r // 4, r // 2 % 2, 1)

            u_chunk(0, True)
            with dve.Fori(1, 8) as c:
                u_chunk(c)

            def residual(n, par, gate, s, base):
                gy = gy1 if s == "resid" else gy2
                for tok in range(2):
                    y = ps[:, 2 * par + tok, :]
                    hc = h[:, tok, bass.ds(n * 512, 512)]
                    if gate is not None:
                        dve.tensor_tensor(gy[:, tok], y, gate[:, bass.ds(n * 512, 512)], ALU.mult)\
                           .then_inc(sem("gated_" + s), 1)
                        dve.wait_ge(sem("gated_" + s), n * 2 + (base + tok + 1))
                        y = gy[:, tok]
                    dve.tensor_tensor(hc, hc, y, ALU.add).then_inc(sem(s), 1)

            for n in range(4):
                for t in range(16):
                    if n == 0 and t == 5:
                        u_mix(7)
                    if n == 0 and t == 7:
                        us_lo(7)
                    if n == 0 and t == 12:
                        dve.wait_ge(sem("mred"), 3)
                        dve.tensor_copy(mcol[:, 2], ps[:, 4, 0:KT]).then_inc(sem("mcol3"), 1)
                    if n and t == 3:
                        dve.wait_ge(unit_used, units_before(G_OUT) + 16 * n)
                        dve.wait_ge(sem("x_loaded"), 32)
                        if n == 1:
                            dve.wait_ge(sem("m2b_ready"), 4)
                        residual(n - 1, (n - 1) % 2, acc[:, 0], "resid", 0)
                    lo(*at(G_OUT, 16 * n + t))
                    step = t - t // 4
                    if n == 1 and t == 0:
                        dve.wait_ge(sem("acc_started"), 80)
                    if n in (1, 2) and t % 4 != 3:
                        ada_add(32 + 6 * (n - 1) + step // 2, 6 * (n - 1) + step // 2, step % 2, 1)
                    if n == 3 and t < 8:
                        ada_add(32 + 12 + t // 2, 12 + t // 2, t % 2, 1)
            dve.wait_ge(unit_used, units_before(G_OUT + 8))
            residual(3, 1, acc[:, 0], "resid", 0)

            dve.wait_ge(sem("conv_turned"), 1)
            dve.tensor_copy(cw[:, :, :].rearrange("p i b -> p (i b)"), ps[:, 0, 0:352]).then_inc(sem("cw_ready"), 1)
            diagonals("n2", 20, (P, P))
            dve.wait_ge(sem("mred"), 4)
            own(dve.tensor_copy(mcol[:, 3], ps[:, 1, 0:KT]))
            dve.scalar_tensor_tensor(out=acol[:, :], in0=mcol[:, 3], scalar=1.0, in1=cols[:, C_G1],
                                     op0=ALU.add, op1=ALU.mult).then_inc(sem("gain_n2"), 1)
            dve.wait_ge(sem("gain_n2"), 1)
            spread("n2", T, xth, xtl, acol, mcol[:, 2])
            dve.wait_ge(sem("acc_started"), 96)

            def side_taps(y, bank, blk, ysem, F, done):
                dve.wait_ge(sem(ysem), F * 4 + 4)
                for n in range(4):
                    dve.scalar_tensor_tensor(out=y[:, n, 1:T], in0=ps[:, bank + n, 0:T - 1],
                                             scalar=cw[:, 0, bass.ds(blk + n, 1)], in1=y[:, n, 1:T],
                                             op0=ALU.mult, op1=ALU.add).then_inc(sem("tap_" + ysem), 1)
                for n in range(4):
                    dve.wait_ge(sem("tap_" + ysem), F * 4 + (n + 1))
                    ins = dve.scalar_tensor_tensor(out=y[:, n, 0:T - 1], in0=ps[:, bank + n, 1:T],
                                                   scalar=cw[:, 2, bass.ds(blk + n, 1)], in1=y[:, n, 0:T - 1],
                                                   op0=ALU.mult, op1=ALU.add)
                ins.then_inc(sem(done), 1)

            def value_done(F):
                side_taps(yv, 4, F * 4 + 44, "yv_ready", F, "yv_done")
                dve.wait_ge(sem("yv_done"), F + 1)
                dve.wait_ge(sem("sg_ready"), F + 1)
                dve.tensor_tensor(hs[:, :, :], sg[:, :, :], yv[:, :, :], ALU.mult).then_inc(sem("hs_done"), 1)

            def h_lo(F, f):
                dve.wait_ge(sem("hth_ready"), F + 1)
                dve.tensor_tensor(htl[:, bass.ds(f * 4, 4), :], hs[:, :, :], hth[:, bass.ds(f * 4, 4), :].bitcast(F32),
                                  ALU.subtract).then_inc(sem("htl_ready"), 1)

            for p, ((f0, nf), (gu, gd)) in enumerate(zip(FPARTS, G_FFN)):
                def pair(f, first=False):
                    F = f + f0
                    for t in range(16):
                        if first and p and t == 3:
                            dve.wait_ge(unit_used, units_before(gu))
                            residual(3, 1, acc[:, 0], "resid_f", 8 * (p - 1))
                        if t == 3 and not first:
                            value_done(F - 1)
                        if t == 6 and not first:
                            h_lo(F - 1, f - 1)
                        if t == 11:
                            side_taps(yg, 0, F * 4, "yg_ready", F, "yg_done")
                        lo(*at(gu + f * 2, t))
                        if p == 0 and t % 2 == 0:
                            ada_add(f * 4 + (48 + t // 4), f * 4 + t // 4, t // 2 % 2, 0)

                pair(0, True)
                with dve.Fori(1, nf) as f:
                    pair(f)
                for t in range(8 * nf):
                    n, r = t // (2 * nf), t % (2 * nf)
                    if t == 3:
                        value_done(f0 + nf - 1)
                    if t == 6 and nf > 3 or t == 5 and nf == 3:
                        h_lo(f0 + nf - 1, nf - 1)
                    if n and r == 3:
                        dve.wait_ge(unit_used, units_before(gd) + 2 * nf * n)
                        if p == 0 and n == 1:
                            dve.wait_ge(sem("m5b_ready"), 4)
                        residual(n - 1, (n - 1) % 2, acc[:, 0], "resid_f", 8 * p)
                    lo(*at(gd, t))
            dve.wait_ge(unit_used, units_before(G_A))
            residual(3, 1, acc[:, 0], "resid_f", 16)

            dve.wait_ge(sem("rs"), RS_AT["f"])
            dve.wait_ge(sem("bcast_loaded"), 16)
            for b in range(2):
                dve.scalar_tensor_tensor(out=h[:, b, :], in0=h[:, b, :], scalar=st[:, 28 + b:29 + b], in1=bcast[:, :],
                                         op0=ALU.mult, op1=ALU.mult).then_inc(sem("x2_ready"), 1)
            for t, rects in ((maskA, ((0, 64, 64, 128, 0), (0, 64, 208, L, 1))),):
                own(dve.memset(t[:, :, :], 0.0))
                for p0, p1, c0, c1, b in rects:
                    own(dve.memset(t[p0:p1, b, c0:c1], NEG))
            dve.wait_ge(sem("lamv_loaded"), 64)
            for i in range(2):
                own(dve.tensor_tensor(lamv[0:1, 4, :], lamv[0:1, 2 * i, :], lamv[0:1, 2 * i + 1, :], ALU.mult))
                own(dve.tensor_reduce(st[0:1, 114 + i:115 + i], lamv[0:1, 4, :], AX.X, ALU.add))
            dve.tensor_scalar(st[:, 112:114], cols[:, C_SUB:C_SUB + 2], 0.4, None, ALU.mult).then_inc(sem("lam_sum"), 1)
            diagonals("a", 36, (P, NM, P))
            spread("a", L, xmh, xml, cols[:, C_AN], None)
            dve.wait_ge(sem("lam_exp"), 1)
            dve.wait_ge(sem("lam_sum"), 1)
            own(dve.tensor_tensor(st[0:1, 118:119], st[0:1, 117:118], st[0:1, 116:117], ALU.subtract))
            dve.tensor_scalar(st[0:1, 119:120], st[0:1, 118:119], -0.2, None, ALU.add).then_inc(sem("nlam"), 1)
            dve.wait_ge(sem("nlam_ps"), 1)
            own(dve.tensor_copy(st[:, 111:112], ps[:, 4, 0:1]))

            def rope(t, nth, j, ready):
                dve.wait_ge(sem(ready), j + 1)
                dve.wait_ge(sem("tabA_loaded"), 32)
                own2 = Own(dve, sem("rope_own"), j * 6 + nth * 3)
                dve.tensor_tensor(rt1[0:32], t[0:32, :, :], tabA[:, 0:1, :].broadcast_to([32, 4, L]), ALU.mult)\
                   .then_inc(sem("rope_own"), 1)
                own2.n += 1
                dve.wait_ge(sem("rot"), j * 2 + (nth + 1))
                own2(dve.tensor_tensor(rt2[0:32], ps[0:32, 4:8, 0:L], tabA[:, 1:2, :].broadcast_to([32, 4, L]), ALU.mult))
                own2(dve.tensor_tensor(t[0:32, :, :], rt1[0:32], rt2[0:32], ALU.add))

            def item_dve(it, j, pair, b):
                c0, nq = BLK[b][0], P
                nk = (144, 16, L)[b]
                own3 = Own(dve, sem("item_own"), it * 5)
                dve.wait_ge(sem("a_scores"), it + 1)
                s = sc[0:nq, :, 0:nk]
                if b == 1:
                    own3(dve.tensor_scalar(s, ps[0:nq, 4:6, 0:nk], AH ** -0.5, None, ALU.mult))
                else:
                    own3(dve.scalar_tensor_tensor(out=s, in0=ps[0:nq, 4:6, 0:nk], scalar=AH ** -0.5,
                                                  in1=maskA[0:nq, b // 2:b // 2 + 1, 0:nk].broadcast_to([nq, 2, nk]),
                                                  op0=ALU.mult, op1=ALU.add))
                own3(dve.tensor_reduce(st[0:nq, 102:104], s, AX.X, ALU.max))
                dve.tensor_scalar(st[0:nq, 104:106], st[0:nq, 102:104], -1.0, None, ALU.mult).then_inc(sem("a_max"), 1)
                dve.wait_ge(sem("a_exp"), it * 2 + 2)
                own3(dve.reciprocal(st[0:nq, 108:110], st[0:nq, 106:108]))
                own3(dve.tensor_scalar(st[0:nq, 110:111], st[0:nq, 109:110], st[0:nq, 111:112], None, ALU.mult))
                own3(dve.tensor_scalar(wd[0:nq, 0:nk], ex[0:nq, 0, 0:nk], st[0:nq, 108:109], None, ALU.mult))
                dve.scalar_tensor_tensor(out=wd[0:nq, 0:nk], in0=ex[0:nq, 1, 0:nk], scalar=st[0:nq, 110:111],
                                         in1=wd[0:nq, 0:nk], op0=ALU.mult, op1=ALU.add).then_inc(sem("a_w"), 1)
                dve.wait_ge(sem("ors"), it + 1)
                dve.tensor_scalar(on[0:nq, :], ps[0:nq, 7, 0:256], st[0:nq, 101:102], None, ALU.mult).then_inc(sem("a_on"), 1)
                dve.wait_ge(sem("a_oturned"), it + 1)
                for d in range(2):
                    dve.tensor_scalar(ot[:, bass.ds(j * 4 + (2 * pair + d), 1), c0:c0 + BLK[b][1]],
                                      ps[:, 4:5, d * P:d * P + BLK[b][1]], st[:, 112 + d:113 + d], None,
                                      ALU.mult).then_inc(sem("a_ot"), 1)

            with dve.Fori(0, 4) as j:
                for t in range(24):
                    lo(*at(G_A + j * 3, t))
                rope(qt, 0, j, "qt_ready")
                rope(kt_, 1, j, "kt_ready")
                for i in range(6):
                    item_dve(j * 6 + i, j, i // 3, i % 3)

            def gate(j):
                dve.wait_ge(sem("gth_ready"), j + 1)
                dve.scalar_tensor_tensor(out=g2[:, :, :], in0=gth[:, :, :], scalar=1.0, in1=ps[:, 0:4, 0:L],
                                         op0=ALU.add, op1=ALU.mult).then_inc(sem("g_silu"), 1)
                dve.wait_ge(sem("g_silu"), j + 1)
                dve.tensor_tensor(g2[:, :, :], g2[:, :, :], ot[:, bass.ds(j * 4, 4), :], ALU.mult).then_inc(sem("g_prod"), 1)
                dve.wait_ge(sem("oth_ready"), j + 1)
                dve.tensor_tensor(otl[:, bass.ds(j * 4, 4), :], g2[:, :, :], oth[:, bass.ds(j * 4, 4), :].bitcast(F32),
                                  ALU.subtract).then_inc(sem("g_done"), 1)

            def y_add(j):
                dve.wait_ge(sem("y_turned"), j + 1)
                for b, (c0, w) in enumerate(BLK):
                    hb = (h[:, 0], hm[0:NM], h[:, 1])[b]
                    hc = hb[:, bass.ds(j * 512, 512)]
                    dve.tensor_tensor(hc, hc, ps[0:w, 4 + b, :], ALU.add).then_inc(sem("y_added"), 1)

            for r in range(8):
                lo(G_GATE, r)
            with dve.Fori(1, 4) as j:
                for r in range(8):
                    if r == 2:
                        gate(j - 1)
                    lo(G_GATE + j, r)
            for r in range(8):
                if r == 2:
                    gate(3)
                lo(G_AOUT, r)
            with dve.Fori(1, 4) as j:
                for r in range(8):
                    if r == 6:
                        y_add(j - 1)
                    lo(G_AOUT + j, r)
            y_add(3)

            own4 = Own(dve, sem("dve_own_b"))
            diagonals("b", 52, (P, NM, P))
            spread("b", L, xmh, xml, cols[:, C_KVN], None)
            own4(dve.memset(maskB[:, :, :], 0.0))
            for p0, p1, c0, c1, b in ((0, 64, 64, 128, 0), (0, 64, 208, L, 1), (64, 128, 0, 64, 1)):
                own4(dve.memset(maskB[p0:p1, b, c0:c1], NEG))
            spread("b2", T, bxh, bxl, cols[:, C_BN], None)
            for r in range(8):
                lo(G_KV, r)
            dve.wait_ge(sem("kk_raw"), 1)
            dve.wait_ge(sem("tabB_loaded"), 32)
            own4(dve.tensor_tensor(kt1[:, :, :], kk[:, 0:2, :], tabB[:, 0:1, :].broadcast_to([P, 2, L]), ALU.mult))
            dve.wait_ge(sem("rotb"), 1)
            own4(dve.tensor_tensor(kt2[:, :, :], ps[:, 4:6, 0:L], tabB[:, 1:2, :].broadcast_to([P, 2, L]), ALU.mult))
            dve.tensor_tensor(kk[:, 0:2, :], kt1[:, :, :], kt2[:, :, :], ALU.add).then_inc(sem("kk_ready"), 1)
            dve.wait_ge(sem("tabq_loaded"), 32)

            qv = qx[:, :, :].rearrange("p t (h d) -> p t h d", d=BH)

            def quad_dve(n, j, tok, half):
                own6 = Own(dve, sem("quad_own"), n * 6)
                nk = (144, L)[tok]
                dve.wait_ge(sem("b_scores"), n + 1)
                s = sb_[:, :, 0:nk]
                sink = sinkb[:, bass.ds(j * 8 + 4 * half, 4)]
                own6(dve.scalar_tensor_tensor(out=s, in0=ps[:, 4:8, 0:nk], scalar=BH ** -0.5,
                                              in1=maskB[:, tok:tok + 1, 0:nk].broadcast_to([P, 4, nk]),
                                              op0=ALU.mult, op1=ALU.add))
                own6(dve.tensor_reduce(st[:, 120:124], s, AX.X, ALU.max))
                own6(dve.tensor_tensor(st[:, 124:128], st[:, 120:124], sink, ALU.max))
                own6(dve.tensor_scalar(st[:, 128:132], st[:, 124:128], -1.0, None, ALU.mult))
                dve.tensor_tensor(st[:, 132:136], sink, st[:, 124:128], ALU.subtract).then_inc(sem("b_max"), 1)
                dve.wait_ge(sem("b_exp"), n * 4 + 4)
                own6(dve.tensor_tensor(st[:, 144:148], st[:, 140:144], st[:, 136:140], ALU.add))
                own6(dve.reciprocal(st[:, 148:152], st[:, 144:148]))
                dve.wait_ge(sem("b_pv"), n + 1)
                dve.tensor_tensor(ob[:, bass.ds(j, 1), tok, half * 256:half * 256 + 256].rearrange("p o (i d) -> p (o i) d", d=BH),
                                  ps[:, 7, 0:256].rearrange("p (i d) -> p i d", d=BH),
                                  st[:, 148:152].unsqueeze(2).broadcast_to([P, 4, BH]), ALU.mult).then_inc(sem("b_o"), 1)

            with dve.Fori(0, 4) as j:
                for r in range(8):
                    lo(G_B + j, r)
                dve.wait_ge(sem("qx_ready"), j + 1)
                own5 = Own(dve, sem("qrope_own"), j * 6)
                for tok in range(2):
                    own5(dve.tensor_tensor(rta[:, :, :], qv[:, tok, :, 0:16],
                                           tabq[:, tok, 0:1, :].broadcast_to([P, 8, 16]), ALU.mult))
                    dve.tensor_tensor(rtb[:, :, 0:8], qv[:, tok, :, 8:16],
                                      tabq[:, tok, 1:2, 0:8].broadcast_to([P, 8, 8]), ALU.mult)
                    own5(dve.tensor_tensor(rtb[:, :, 8:16], qv[:, tok, :, 0:8],
                                           tabq[:, tok, 1:2, 8:16].broadcast_to([P, 8, 8]), ALU.mult))
                    own5(dve.tensor_tensor(qv[:, tok, :, 0:16], rta[:, :, :], rtb[:, :, :], ALU.add))
                for i in range(4):
                    quad_dve(j * 4 + i, j, i // 2, i % 2)

            def gb(j, par):
                dve.wait_ge(sem("gb_ready"), j + 1)
                dve.scalar_tensor_tensor(out=gb2[:, :, :], in0=gb1[:, :, :], scalar=1.0, in1=ps[:, 2 * par:2 * par + 2, :],
                                         op0=ALU.add, op1=ALU.mult).then_inc(sem("gb_silu"), 1)
                dve.wait_ge(sem("gb_silu"), j + 1)
                dve.tensor_tensor(gb2[:, :, :], gb2[:, :, :], ob[:, j, :, :], ALU.mult).then_inc(sem("gb_prod"), 1)

            def ob_lo(j):
                dve.wait_ge(sem("obh_ready"), j + 1)
                for tok in range(2):
                    ins = dve.scalar_tensor_tensor(
                        out=obl[:, 4 * j:4 * j + 4, tok * P:tok * P + P],
                        in0=ps[:, 4 + tok, :].rearrange("p (k q) -> p k q", q=P), scalar=0.5,
                        in1=obh[:, 4 * j:4 * j + 4, tok * P:tok * P + P].bitcast(F32), op0=ALU.mult, op1=ALU.subtract)
                ins.then_inc(sem("obl_ready"), 1)

            for j in range(4):
                for r in range(8):
                    if j and r == 4:
                        gb(j - 1, (j - 1) % 2)
                    if j and r == 7:
                        ob_lo(j - 1)
                    lo(G_BG + j, r)
            for j in range(4):
                for r in range(8):
                    if j == 0 and r == 4:
                        gb(3, 1)
                    if j == 0 and r == 7:
                        ob_lo(3)
                    if j and r == 3:
                        dve.wait_ge(unit_used, units_before(G_BOUT + j))
                        residual(j - 1, (j - 1) % 2, None, "resid_b", 0)
                    lo(G_BOUT + j, r)
            dve.wait_ge(unit_used, units_before(G_BOUT + 4))
            residual(3, 1, None, "resid_b", 0)
            dve.wait_ge(sem("rs"), RS_AT["z"])
            dve.wait_ge(sem("bcast_loaded"), 32)
            for b in range(2):
                dve.scalar_tensor_tensor(out=h[:, b, :], in0=h[:, b, :], scalar=st[:, 60 + b:61 + b], in1=bcast[:, :],
                                         op0=ALU.mult, op1=ALU.mult).then_inc(sem("result_ready"), 1)

        @block.tensor
        def _(pe):
            def tok_unit(G, r, xh, xl, k0, bank, first, last):
                pe.wait_ge(lo_ready, units_before(G) + (r + 1))
                for tok in range(2):
                    for i in range(2):
                        xs = [x[:, k0 + i, tok * P:tok * P + P] for x in (xh, xl)]
                        for n, (x, w) in enumerate(((0, whi), (0, wlo), (1, whi))):
                            mm = pe.matmul(ps[:, bank + tok, :], xs[x], w[:, r % 4, i, :],
                                           start=first and i == 0 and n == 0, stop=last and i == 1 and n == 2)
                mm.then_inc(unit_used, 1)

            def chan_unit(G, r, xh, xl, n_tok, bank, first, last, before=None):
                pe.wait_ge(lo_ready, units_before(G) + (r + 1))
                for c in range(4):
                    for i in range(2):
                        ws = [w[:, r % 4, i, c * P:c * P + P] for w in (whi, wlo)]
                        for n, (w, x) in enumerate(((0, xh), (0, xl), (1, xh))):
                            mm = pe.matmul(ps[:, bank + c, 0:n_tok], ws[w], x[:, 2 * r + i, 0:n_tok],
                                           start=first and i == 0 and n == 0, stop=last and i == 1 and n == 2)
                mm.then_inc(unit_used, 1)

            def turned_norm(name, srcs, n, xnl):
                pe.wait_ge(sem("dg"), DG_AT[name])
                for k in range(KT):
                    if k >= 4:
                        pe.wait_ge(sem("ntmp"), TILES0[xnl] + k - 3)
                    for i, (src, c0, w, d) in enumerate(srcs):
                        mm = pe.matmul(ps[:, 4 + k % 4, c0:c0 + w], src[0:w, k * P:k * P + P], dg[0:w, d, 0:w],
                                       start=True, stop=True)
                    mm.then_inc(sem("nt"), 1)

            def column(slot, bank, c0):
                for b in range(KT):
                    mm = pe.matmul(ps[:, bank, c0 + b:c0 + b + 1], acc[:, slot, b * P:b * P + P], ones[:, 0:1],
                                   start=True, stop=True)
                mm.then_inc(sem("mred"), 1)

            def row_all(slot, done):
                for n in range(4):
                    pe.matmul(ps[:, 4 + n, :], ones[:, :], acc[:, slot, n * 512:n * 512 + 512],
                              start=True, stop=True).then_inc(sem(done), 1)

            pe.wait_ge(sem("const_ready"), 3)
            pe.wait_ge(sem("rows_loaded"), 16 * 8)
            pe.transpose(ps[:, 0, 0:96], rows[0:96, 0, :], ident[0:96, 0:96])
            pe.transpose(ps[:, 0, 96:114], rows[0:18, 1, :], ident[0:18, 0:18]).then_inc(sem("cols_turned"), 1)
            pe.wait_ge(ada_used, 16)
            column(0, 1, 0)
            pe.wait_ge(ada_used, 32)
            column(1, 1, 16)
            turned_norm("n1", [(h[:, 0], 0, P, 0), (h[:, 1], P, P, 1)], T, "n1")

            def v_chunk(c, par, first=False):
                if not first:
                    pe.wait_ge(sem("v_ready"), c * 2 - 2)
                for r in range(8):
                    if first and par == 0:
                        pe.wait_ge(sem("nl"), TILES0["n1"] + 2 * r + 2)
                    tok_unit(G_IN + c, r, xth, xtl, 2 * r, 2 * par, r == 0, r == 7)

            v_chunk(0, 0, True)
            v_chunk(1, 1, True)
            with pe.Fori(1, 4) as i:
                v_chunk(i * 2, 0)
                v_chunk(i * 2 + 1, 1)

            def mix(c):
                pe.wait_ge(sem("wsc_ready"), c * 2 + 2)
                pe.wait_ge(sem("v_ready"), 16)
                for tok in range(2):
                    for g in range(2):
                        mm = pe.matmul(ps[:, 4 + tok, g * 256:g * 256 + 256], wsc[:, tok, g, :],
                                       v[:, bass.ds(c, 1), tok, g * 256:g * 256 + 256].rearrange("p o n -> p (o n)"),
                                       start=True, stop=True)
                    mm.then_inc(sem("mixed"), 1)

            def us_turn(c):
                for tok in range(2):
                    pe.wait_ge(sem("us_done"), c * 2 + (tok + 1))
                    for k in range(4):
                        mm = pe.transpose(ps[:, 6 + tok, k * P:k * P + P], us[:, tok, k * P:k * P + P], ident[:, :])
                    mm.then_inc(sem("us_turned"), 1)

            def u_chunk(c, par, first=False):
                if first:
                    pe.wait_ge(sem("v_ready"), 14)
                    pe.wait_ge(ada_step, 32)
                    row_all(0, "m2_spread")
                else:
                    pe.wait_ge(sem("u_ready"), c * 2 - 2)
                for r in range(8):
                    if r == 1:
                        pe.wait_ge(sem("ws_loaded"), c * 16 + 16)
                        if first:
                            pe.wait_ge(sem("m2b_ready"), 4)
                        else:
                            pe.wait_ge(sem("usl_ready"), c * 2 - 2)
                        for g in range(2):
                            mm = pe.transpose(ps[:, 6, g * P:g * P + P], wsr[:, g, :], ident[:, :])
                        mm.then_inc(sem("ws_turned"), 1)
                    if r == 4 and not first:
                        pe.wait_ge(sem("wsc_ready"), c * 2 + 2)
                        us_turn(c - 1)
                    if r == 5:
                        mix(c)
                    tok_unit(G_IN + 8 + c, r, xth, xtl, 2 * r, 2 * par, r == 0, r == 7)

            u_chunk(0, 0, True)
            pe.wait_ge(sem("v_ready"), 16)
            u_chunk(1, 1)
            with pe.Fori(1, 4) as i:
                u_chunk(i * 2, 0)
                u_chunk(i * 2 + 1, 1)

            for n in range(4):
                if n == 0:
                    pe.wait_ge(sem("u_ready"), 14)
                elif n == 1:
                    pe.wait_ge(sem("u_ready"), 16)
                else:
                    pe.wait_ge(sem("resid"), 2 * n - 2)
                for t in range(16):
                    if n == 0 and t == 4:
                        pe.wait_ge(sem("wsc_ready"), 16)
                        us_turn(7)
                    if n == 0 and t == 8:
                        pe.wait_ge(ada_step, 64)
                        column(1, 4, 0)
                    if n == 0 and t % 2 == 0:
                        pe.wait_ge(sem("usl_ready"), t + 2)
                    tok_unit(*at(G_OUT, 16 * n + t), ush, usl, 2 * t, 2 * (n % 2), t == 0, t == 15)

            pe.wait_ge(sem("crow_loaded"), 64)
            for i in range(4):
                mm = pe.transpose(ps[:, 0, 88 * i:88 * i + 88], crow[:, i, :], ident[0:88, 0:88])
            mm.then_inc(sem("conv_turned"), 1)
            pe.wait_ge(ada_step, 96)
            column(1, 1, 0)
            turned_norm("n2", [(h[:, 0], 0, P, 0), (h[:, 1], P, P, 1)], T, "n2")
            pe.wait_ge(sem("cw_ready"), 1)
            for p, ((f0, nf), (gu, gd)) in enumerate(zip(FPARTS, G_FFN)):
                def pair(f, first=False):
                    F = f + f0
                    if first:
                        if p == 0:
                            pe.wait_ge(sem("gain_n2"), 1)
                        else:
                            pe.wait_ge(sem("resid_f"), 8 * p)
                    else:
                        pe.wait_ge(sem("yg_done"), F)
                    for r in range(8):
                        if first and p == 0:
                            pe.wait_ge(sem("nl"), TILES0["n2"] + 2 * r + 2)
                        chan_unit(gu + f * 2, r, xth, xtl, T, 0, r == 0, r == 7)
                    if first and p == 0:
                        pass
                    elif first and p == 1:
                        pe.wait_ge(sem("m5b_ready"), 4)
                        pe.wait_ge(sem("yv_done"), F)
                    else:
                        pe.wait_ge(sem("yv_done"), F)
                    for r in range(8):
                        chan_unit(gu + f * 2 + 1, r, xth, xtl, T, 4, r == 0, r == 7)

                pair(0, True)
                with pe.Fori(1, nf) as f:
                    pair(f)
                for t in range(8 * nf):
                    n, r = t // (2 * nf), t % (2 * nf)
                    if r == 0 and n < 2:
                        pe.wait_ge(sem("yg_done"), f0 + nf)
                    elif r == 0:
                        pe.wait_ge(sem("resid_f"), 8 * p + 2 * n - 2)
                    if p == 0 and t == 6:
                        pe.wait_ge(sem("yv_done"), nf)
                        pe.wait_ge(ada_step, 128)
                        row_all(0, "m5_spread")
                    if n == 0 and r % 2 == 0:
                        pe.wait_ge(sem("htl_ready"), f0 + r // 2 + 1)
                    tok_unit(*at(gd, t), hth, htl, 2 * r, 2 * (n % 2), r == 0, r == 2 * nf - 1)

            pe.wait_ge(sem("x2_ready"), 2)
            pe.wait_ge(sem("meta_loaded"), 16)
            turned_norm("a", [(h[:, 0], 0, P, 0), (hm[:, :], P, NM, 1), (h[:, 1], P + NM, P, 2)], L, "a")
            pe.wait_ge(sem("nlam"), 1)
            pe.wait_ge(sem("nl"), TILES0["a"] + 13)
            pe.matmul(ps[:, 4, 0:1], ones[0:1, :], st[0:1, 119:120], start=True, stop=True).then_inc(sem("nlam_ps"), 1)
            pe.wait_ge(sem("nl"), TILES0["a"] + 16)
            pe.wait_ge(sem("tabA_loaded"), 32)

            def item_pe(it, j, pair, b):
                c0, nq = BLK[b][0], P
                k0, nk = ((0, 144), (P, 16), (0, L))[b]
                for i in range(2):
                    mm = pe.matmul(ps[0:nq, 4 + i, 0:nk], qt[:, 2 * pair + i, c0:c0 + nq],
                                   kt_[:, 2 * pair + i, k0:k0 + nk], start=True, stop=True)
                mm.then_inc(sem("a_scores"), 1)
                pe.wait_ge(sem("a_w"), it + 1)
                kbs = ((0, 1), (1,), (0, 1, 2))[b]
                for kb in kbs:
                    kc, w = BLK[kb]
                    mm = pe.transpose(ps[0:w, 6, kb * P:kb * P + nq], wd[0:nq, kc - k0:kc - k0 + w], ident[0:nq, 0:nq])
                mm.then_inc(sem("a_wturned"), 1)
                pe.wait_ge(sem("a_wt"), it + 1)
                for kb in kbs:
                    w = BLK[kb][1]
                    mm = pe.matmul(ps[0:nq, 7, 0:256], wt[0:w, kb, 0:nq], vx[0:w, kb, pair * 256:pair * 256 + 256],
                                   start=kb == kbs[0], stop=kb == kbs[-1])
                mm.then_inc(sem("a_pv"), 1)
                pe.wait_ge(sem("a_on"), it + 1)
                for d in range(2):
                    mm = pe.transpose(ps[:, 4, d * P:d * P + nq], on[0:nq, d * P:d * P + P], ident[0:nq, 0:nq])
                mm.then_inc(sem("a_oturned"), 1)
                pe.wait_ge(sem("a_ot"), it * 2 + 2)

            with pe.Fori(0, 4) as j:
                pe.wait_ge(sem("resid_f"), 24)
                for i in range(3):
                    if i == 2:
                        pe.wait_ge(sem("qt_ready"), j + 1)
                    for r in range(8):
                        chan_unit(G_A + j * 3 + i, r, xmh, xml, L, 4 * (i % 2), r == 0, r == 7)
                for nth, (t, ready) in enumerate(((qt, "qt_ready"), (kt_, "kt_ready"))):
                    pe.wait_ge(sem("kt_ready"), j + 1)
                    if nth:
                        pe.wait_ge(sem("rope_own"), j * 6 + 2)
                    for i in range(4):
                        mm = pe.matmul(ps[:, 4 + i, 0:L], rotA[:, :], t[0:32, i, :], start=True, stop=True)
                    mm.then_inc(sem("rot"), 1)
                pe.wait_ge(sem("vt_ready"), j + 1)
                for b, (c0, w) in enumerate(BLK):
                    for i in range(4):
                        mm = pe.transpose(ps[0:w, b, i * P:i * P + P], vt[:, i, c0:c0 + w], ident[:, :])
                mm.then_inc(sem("v_turned"), 1)
                pe.wait_ge(sem("vx_ready"), j + 1)
                pe.wait_ge(sem("rope_own"), j * 6 + 6)
                for i in range(6):
                    item_pe(j * 6 + i, j, i // 3, i % 3)

            for r in range(8):
                chan_unit(G_GATE, r, xmh, xml, L, 0, r == 0, r == 7)
            with pe.Fori(1, 4) as j:
                pe.wait_ge(sem("g_silu"), j)
                for r in range(8):
                    chan_unit(G_GATE + j, r, xmh, xml, L, 0, r == 0, r == 7)

            def y_turn(j):
                pe.wait_ge(sem("yt_ready"), j + 1)
                for b, (c0, w) in enumerate(BLK):
                    for i in range(4):
                        mm = pe.transpose(ps[0:w, 4 + b, i * P:i * P + P], yt[:, i, c0:c0 + w], ident[:, :])
                mm.then_inc(sem("y_turned"), 1)

            pe.wait_ge(sem("g_silu"), 4)
            for r in range(8):
                if r % 2 == 0:
                    pe.wait_ge(sem("g_done"), r // 2 + 1)
                chan_unit(G_AOUT, r, oth, otl, L, 0, r == 0, r == 7)
            with pe.Fori(1, 4) as j:
                pe.wait_ge(sem("yt_ready"), j)
                for r in range(8):
                    if r == 3:
                        pe.wait_ge(sem("y_added"), j * 3 - 3)
                        y_turn(j - 1)
                    chan_unit(G_AOUT + j, r, oth, otl, L, 0, r == 0, r == 7)
            pe.wait_ge(sem("y_added"), 9)
            y_turn(3)

            pe.wait_ge(sem("y_added"), 12)
            turned_norm("b", [(h[:, 0], 0, P, 0), (hm[:, :], P, NM, 1), (h[:, 1], P + NM, P, 2)], L, "b")
            pe.wait_ge(sem("nl"), TILES0["b"] + 16)
            turned_norm("b", [(h[:, 0], 0, P, 0), (h[:, 1], P, P, 2)], T, "b2")
            for r in range(8):
                chan_unit(G_KV, r, xmh, xml, L, 0, r == 0, r == 7)
            pe.wait_ge(sem("kk_raw"), 1)
            pe.wait_ge(sem("tabB_loaded"), 32)
            pe.wait_ge(sem("nl"), TILES0["b2"] + 16)
            for i in range(2):
                mm = pe.matmul(ps[:, 4 + i, 0:L], rotB[:, :], kk[:, i, :], start=True, stop=True)
            mm.then_inc(sem("rotb"), 1)
            for b, (c0, w) in enumerate(BLK):
                bank, col = ((6, 0), (6, 256), (7, 0))[b]
                for i in range(2):
                    mm = pe.transpose(ps[0:w, bank, col + i * P:col + i * P + P], kk[:, 2 + i, c0:c0 + w], ident[:, :])
            mm.then_inc(sem("vb_turned"), 1)
            pe.wait_ge(sem("vb_ready"), 1)
            pe.wait_ge(sem("kd_ready"), 64)

            def quad_pe(n, j, tok, half):
                nk = (144, L)[tok]
                for i in range(4):
                    p0 = 64 * (i % 2)
                    mm = pe.matmul(ps[:, 4 + i, 0:nk], qtb[p0:p0 + 64, 2 * half + i // 2, tok * P:tok * P + P],
                                   kd[p0:p0 + 64, j, 0:nk], start=True, stop=True)
                mm.then_inc(sem("b_scores"), 1)
                pe.wait_ge(sem("b_exp"), n * 4 + 4)
                for kb in range(2 + tok):
                    kc, w = BLK[kb]
                    for i in range(4):
                        mm = pe.transpose(ps[0:w, 4 + kb, i * P:i * P + P], eb_[:, i, kc:kc + w], ident[:, :])
                mm.then_inc(sem("b_wturned"), 1)
                pe.wait_ge(sem("b_wt"), n + 1)
                for i in range(4):
                    for kb in range(2 + tok):
                        w = BLK[kb][1]
                        mm = pe.matmul(ps[:, 7, i * BH:i * BH + BH], wtb[0:w, kb, i, :],
                                       vb[0:w, kb, j * BH:j * BH + BH], start=kb == 0, stop=kb == 1 + tok)
                mm.then_inc(sem("b_pv"), 1)
                pe.wait_ge(sem("b_o"), n + 1)

            for j in range(4):
                for r in range(8):
                    tok_unit(G_B + j, r, bxh, bxl, 2 * r, 0, r == 0, r == 7)
                pe.wait_ge(sem("qrope_own"), j * 6 + 6)
                for tok in range(2):
                    for i in range(4):
                        mm = pe.transpose(ps[:, 4 + tok, i * P:i * P + P], qx[:, tok, i * P:i * P + P], ident[:, :])
                mm.then_inc(sem("q_turned"), 1)
                pe.wait_ge(sem("qtb_ready"), j + 1)
                for i in range(4):
                    quad_pe(j * 4 + i, j, i // 2, i % 2)

            def ob_turn(j):
                pe.wait_ge(sem("gb_prod"), j + 1)
                if j:
                    pe.wait_ge(sem("obl_ready"), j)
                for tok in range(2):
                    for i in range(4):
                        mm = pe.transpose(ps[:, 4 + tok, i * P:i * P + P], gb2[:, tok, i * P:i * P + P], ident[:, :])
                mm.then_inc(sem("ob_turned"), 1)

            for j in range(4):
                if j > 1:
                    pe.wait_ge(sem("gb_silu"), j - 1)
                for r in range(8):
                    if j and r == 4:
                        ob_turn(j - 1)
                    tok_unit(G_BG + j, r, bxh, bxl, 2 * r, 2 * (j % 2), r == 0, r == 7)
            for j in range(4):
                if j < 2:
                    pe.wait_ge(sem("gb_silu"), j + 3)
                else:
                    pe.wait_ge(sem("resid_b"), 2 * j - 2)
                for r in range(8):
                    if j == 0 and r == 4:
                        ob_turn(3)
                    if j == 0 and r % 2 == 0:
                        pe.wait_ge(sem("obl_ready"), r // 2 + 1)
                    tok_unit(G_BOUT + j, r, obh, obl, 2 * r, 2 * (j % 2), r == 0, r == 7)


USED = ("x", "c", "ada_w", "ada_b", "norm_g", "ffn_w_up", "ffn_conv_w", "ffn_conv_b", "ffn_w_down", "a_w_in",
        "a_g_v", "a_w_s", "a_b_s", "a_w_out", "final_g", "meta_tokens_2", "a_norm_2", "a_w_in_2", "a_w_out_2",
        "a_lambda_q1_2", "a_lambda_k1_2", "a_lambda_q2_2", "a_lambda_k2_2", "a_subln_2", "kv_norm_2", "w_kv_2",
        "b_norm_2", "b_w_in_2", "b_w_out_2", "b_sinks_2", "final_norm_2")


def rope_constants():
    import numpy as np

    pos = np.concatenate([NM + np.arange(P), np.arange(NM), NM + P + np.arange(P)])
    out = {}

    def angles(rot):
        inv = (500000.0 ** (-np.arange(0, rot, 2, dtype=np.float32) / rot)).astype(np.float32)
        return pos.astype(np.float32)[None, :] * inv[:, None]

    ang = angles(AH // 4)
    half = AH // 8
    out["tab_a"] = np.stack([np.concatenate([np.cos(ang)] * 2), np.concatenate([-np.sin(ang), np.sin(ang)])], 1)
    out["rot_a"] = np.pad(np.roll(np.eye(2 * half), half, 1), ((0, 0), (0, P - 2 * half)))
    ang = angles(BH // 4)
    half = BH // 8
    tab = np.zeros((P, 2, L))
    tab[:, 0] = 1.0
    rot = np.zeros((P, P))
    for h0 in (0, BH):
        tab[h0:h0 + 2 * half, 0] = np.concatenate([np.cos(ang)] * 2)
        tab[h0:h0 + 2 * half, 1] = np.concatenate([-np.sin(ang), np.sin(ang)])
        rot[h0:h0 + 2 * half, h0:h0 + 2 * half] = np.roll(np.eye(2 * half), half, 1)
    out["tab_b"], out["rot_b"] = tab, rot
    tabq = np.zeros((P, 2, 2, 2 * half))
    for i, b in enumerate(XB):
        c0 = BLK[b][0]
        tabq[:, i] = tab[0:2 * half, :, c0:c0 + P].transpose(2, 1, 0)
    out["tab_q"] = tabq
    return {k: np.ascontiguousarray(x.astype(np.float32)) for k, x in out.items()}


def kernel(**inputs):
    import numpy as np
    import concourse.bacc as bacc
    from concourse.bass_utils import run_bass_kernel_spmd

    nc = bacc.Bacc("TRN2", target_bir_lowering=False, num_devices=1)
    arrays, aps = {}, {}
    for name, x in [(n, inputs[n]) for n in USED] + list(rope_constants().items()):
        x = np.ascontiguousarray(x)
        arrays[f"in_{name}"] = x
        aps[name] = nc.dram_tensor(f"in_{name}", x.shape, mybir.dt.from_np(x.dtype), kind="ExternalInput").ap()
    out = nc.dram_tensor("out", (1, T, D), F32, kind="ExternalOutput").ap()
    program(nc, aps, out)
    r = run_bass_kernel_spmd(nc, [arrays], core_ids=[0])
    return r.results[0]["out"]
```

```python
from contextlib import ExitStack

import concourse.bass as bass
from concourse import mybir

F32 = mybir.dt.float32
F32R = mybir.dt.float32r
ALU = mybir.AluOpType
ACT = mybir.ActivationFunctionType
AX = mybir.AxisListType

P = 128
D = 2048
T = 256
NM = 16
L = T + NM
KT = D // P
EPS1, EPS2 = 1e-6, 1e-5
GW = 2 * D
FF = 5632
NF = FF // 512
FPARTS = ((0, 4), (4, 4), (8, 3))
AH = 128
BH = 64
NEG = -1e30
BLK = ((0, 128), (128, 16), (144, 128))
XB = (0, 2)
ITEM_KEYS = ((0, 144), (P, 16), (0, L))
ITEM_BLOCKS = ((0, 1), (1,), (0, 1, 2))

G_IN = 8
G_OUT = G_IN + 16
G_FFN = []
_g = G_OUT + 8
for _f0, _nf in FPARTS:
    G_FFN.append((_g, _g + 2 * _nf))
    _g += 3 * _nf
G_A = _g
G_GATE = G_A + 12
G_AOUT = G_GATE + 4
G_KV = G_AOUT + 4
G_B = G_KV + 1
G_BG = G_B + 4
G_BOUT = G_BG + 4
ITEMS = 24
ITEM_AT = (3, 7, 11, 14, 18, 21)
ROPE_AT = (9, 13, 17, 20)


QUAD_AT = tuple(12 + 3 * n for n in range(16))
Q_TURN_AT = (10, 20, 26, 35)
O_TURN_AT = (44, 50, 59, 66)
TURN_BANK = (2, 3, 4)


def quads(t, step):
    return [n for n, a in enumerate(QUAD_AT) if a + step == t]


def due(t, step, items=True, before=True):
    out = []
    for i, a in enumerate(ITEM_AT):
        if items and a + step == t:
            out.append((i, 1))
        if before and a + step == t + 24:
            out.append((i, 2))
    return out

KB = 1024
BASE = 16512
O_RAW, O_HI, O_LO = BASE, BASE + 32 * KB, BASE + 48 * KB
O_XT = BASE + 64 * KB
O_V = BASE + 98 * KB
O_W = BASE + 130 * KB
O_ACC = BASE + 164 * KB
O_H = BASE + 180 * KB
O_ADA = BASE + 196 * KB
O_S = BASE + 204 * KB


def at(G, t):
    return G + t // 8, t % 8


TILES0 = {"n1": 0, "n2": 16, "a": 32, "b": 48, "b2": 64}
RS_AT = {"n1": 1, "v": 2, "n2": 3, "f": 4, "a": 5, "b": 6, "z": 7}
DG_AT = {"n1": 1, "n2": 2, "a": 3, "b": 4}


class Own:

    def __init__(self, eng, sem, base=0):
        self.eng, self.sem, self.base, self.n = eng, sem, base, 0

    def __call__(self, ins):
        self.n += 1
        ins.then_inc(self.sem, 1)
        self.eng.wait_ge(self.sem, self.base + self.n)



def units_before(G):
    return 8 * G - 64


def program(nc, a, out):
    with ExitStack() as ctx:
        sems = {}

        def sem(name):
            if name not in sems:
                sems[name] = ctx.enter_context(nc.semaphore(name))
            return sems[name]

        def place(name, shape, off, dt=F32):
            return nc.alloc_sbuf_tensor_at(name, shape, dt, offset=off)

        raw = place("raw", [P, 4, 2, 2, 512], O_RAW)
        rawv = place("rawv", [P, 4, D], O_RAW)
        whi = place("whi", [P, 4, 2, 512], O_HI, F32R)
        wlo = place("wlo", [P, 4, 2, 512], O_LO, F32R)
        xth = place("xth", [P, KT, T], O_XT, F32R)
        xtl = place("xtl", [P, KT, T], O_XT + 17408, F32R)
        xmh = place("xmh", [P, KT, L], O_XT, F32R)
        xml = place("xml", [P, KT, L], O_XT + 17408, F32R)
        v = place("v", [P, 8, 2, 512], O_V)
        ush = place("ush", [P, 32, T], O_V, F32R)
        usl = place("usl", [P, 32, T], O_W, F32R)
        ut = place("ut", [P, 2, 512], O_H)
        us = place("us", [P, 2, 512], O_H + 4 * KB)
        utmp = place("utmp", [P, 512], O_H + 8 * KB)
        gvb = place("gvb", [P, 512], O_H + 10 * KB)
        wsr = place("wsr", [P, 2, 128], O_H + 12 * KB)
        wsc = place("wsc", [P, 2, 2, 128], O_H + 13 * KB)
        acc = place("acc", [P, 2, D], O_ACC)
        ada = place("ada", [P, 2, 1024], O_ADA)
        h = place("h", [P, 2, D], O_H)
        hth = place("hth", [P, 16, T], O_V, F32R)
        htl = place("htl", [P, 16, T], O_V + 16 * KB, F32R)
        cw = place("cw", [P, 4, 88], O_W + 16 * KB)
        gy1 = place("gy1", [P, 2, 512], O_XT)
        gy2 = place("gy2", [P, 2, 512], O_W + 18 * KB)
        yg = place("yg", [P, 4, T], O_W)
        sg = place("sg", [P, 4, T], O_W + 4 * KB)
        yv = place("yv", [P, 4, T], O_W + 8 * KB)
        hs = place("hs", [P, 4, T], O_W + 12 * KB)
        ntmp = place("ntmp", [P, 2, L], O_V + 16 * KB)
        dg = place("dg", [P, 3, P], O_V + 21 * KB)
        junk = place("junk", [P, D], O_V + 24 * KB)
        bcast = place("bcast", [P, D], O_W + 24 * KB)
        hm = place("hm", [P, D], O_ACC)
        oth = place("oth", [P, KT, L], O_W, F32R)
        otl = place("otl", [P, KT, L], O_W + 17408, F32R)
        ot = place("ot", [P, KT, L], O_W)
        qt = place("qt", [P, 4, L], O_V)
        kt_ = place("kt_", [P, 4, L], O_V + 4352)
        qs = place("qs", [P, 4, L], O_V + 2 * 4352)
        ks = place("ks", [P, 4, L], O_ACC + 8 * KB)
        vx = place("vx", [P, 3, 512], O_V + 3 * 4352)
        sc = place("sc", [P, 2, L], O_V + 19200)
        ex = place("ex", [P, 2, L], O_V + 21376)
        wd = place("wd", [P, L], O_V + 23552)
        wt = place("wt", [P, 3, P], O_V + 24640)
        on = place("on", [P, 256], O_V + 26176)
        ojunk = place("ojunk", [P, 256], O_V + 27200)
        tabA = place("tabA", [32, 2, L], O_V + 28224)
        lamv = place("lamv", [1, 5, P], O_V + 30400)
        maskA = place("maskA", [P, 2, L], O_ACC + 12544)
        rt2 = place("rt2", [32, 2, L], O_ADA)
        rotA = place("rotA", [32, P], O_ADA + 4352)
        gth = place("gth", [P, 4, L], O_V + 8704)
        g2 = place("g2", [P, 4, L], O_ACC + 8 * KB)
        yt = place("yt", [P, 4, L], O_V)
        bxh = place("bxh", [P, KT, T], O_W, F32R)
        bxl = place("bxl", [P, KT, T], O_W + 17408, F32R)
        obh = place("obh", [P, KT, T], O_XT, F32R)
        obl = place("obl", [P, KT, T], O_XT + 17408, F32R)
        ob = place("ob", [P, 4, 2, 512], O_XT)
        kk = place("kk", [P, 4, L], O_V)
        kt1 = place("kt1", [P, 2, L], O_V + 4352)
        kt2 = place("kt2", [P, 2, L], O_V + 6528)
        tabB = place("tabB", [P, 2, L], O_V + 8704)
        rotB = place("rotB", [P, P], O_V + 10880)
        kd = place("kd", [P, 4, L], O_ACC)
        vb = place("vb", [P, 3, 256], O_ACC + 4352)
        maskB = place("maskB", [P, 2, L], O_ACC + 10 * KB)
        sinkb = place("sinkb", [P, 32], O_ACC + 9600)
        tabq = place("tabq", [P, 2, 2, 16], O_ACC + 9728)
        qx = place("qx", [P, 2, 512], O_V)
        qtb = place("qtb", [P, 4, 4, T], O_XT + 17408)
        sb_ = place("sb_", [P, 4, L], O_V + 8 * KB)
        eb_ = place("eb_", [P, 4, L], O_V + 8 * KB + 4352)
        wtb = place("wtb", [P, 3, 4, P], O_V + 17 * KB)
        rta = place("rta", [P, 8, 16], O_V + 23 * KB)
        rtb = place("rtb", [P, 8, 16], O_V + 23 * KB + 512)
        gb1 = place("gb1", [P, 2, 512], O_V + 24 * KB)
        gb2 = place("gb2", [P, 2, 512], O_V + 28 * KB)
        ident = place("ident", [P, P], O_S)
        ones = place("ones", [P, P], O_S + 512)
        cols = place("cols", [P, 114], O_S + 1024)
        mcol = place("mcol", [P, 4, KT], O_S + 1536)
        acol = place("acol", [P, KT], O_S + 1792)
        ccol = place("ccol", [P, KT], O_S + 1856)
        st = place("st", [P, 160], O_S + 1920)
        neghalf = place("neghalf", [P, 8], O_S + 2560)
        rows = place("rows", [96, 6, P], O_V)
        crow = place("crow", [88, 4, P], O_V)
        ps = ctx.enter_context(nc.psum_tensor("ps", [P, 8, 512], F32))
        C_C, C_G0, C_G1, C_AN, C_KVN, C_BN = (slice(16 * i, 16 * i + 16) for i in range(6))
        C_BS, C_SUB = 96, 112

        ld = [sem(f"slab{i}_loaded") for i in range(4)]
        ada_used = sem("ada01_used")
        hi_ready, lo_ready, unit_used = sem("hi_ready"), sem("lo_ready"), sem("unit_used")
        al = [sem(f"ada{i}_loaded") for i in range(2)]
        ada_step = sem("ada_step")
        bank_done = sem("bank_done")

        w_in, w_out = a["a_w_in"][0], a["a_w_out"][0]
        w_up, w_down = a["ffn_w_up"][0], a["ffn_w_down"][0]
        w_a, w_ao = a["a_w_in_2"][0], a["a_w_out_2"][0]
        w_kv, w_b, w_bo = a["w_kv_2"], a["b_w_in_2"][0], a["b_w_out_2"][0]
        ada_w, ada_b = a["ada_w"][0], a["ada_b"]
        tiles = lambda w: w.rearrange("(s k p) n -> s p k n", k=4, p=P)

        block = ctx.enter_context(nc.Block())

        @block.sync
        def _(sp):
            def slab(G, q, w, k, col):
                if isinstance(G, int) and G == G_IN:
                    sp.wait_ge(ada_used, 4 * (G - 1) + q + 1)
                else:
                    sp.wait_ge(lo_ready, units_before(G) - 8 + 2 * q + 2)
                dst = raw[:, q].rearrange("p u k n -> p (u k) n")
                sp.dma_start(dst, tiles(w)[k][:, :, bass.ds(col, 512)]).then_inc(ld[q], 16)

            def chunk(G, w, k0, col):
                for q in range(4):
                    slab(G, q, w, k0 + q, col)

            sp.dma_start(h[:, :, :], a["x"][0].rearrange("(b p) n -> p b n", p=P)).then_inc(sem("x_loaded"), 16)
            for j in range(2):
                for i0, loop in (((0, False), (1, True)) if j == 0 else ((0, True),)):
                    def four(i):
                        for q in range(4):
                            if loop:
                                sp.wait_ge(ada_used, 16 * j + 4 * i + q - 3)
                            src = ada_w[bass.ds(i * 512 + q * 128, 128), j * D:(j + 1) * D]
                            sp.dma_start(rawv[:, q], src).then_inc(ld[q], 16)
                    if loop:
                        with sp.Fori(i0, 4) as i:
                            four(i)
                    else:
                        four(i0)
            chunk(G_IN, w_in, 0, GW)
            with sp.Fori(1, 8) as c:
                chunk(G_IN + c, w_in, 0, c * 512 + GW)
            with sp.Fori(0, 8) as c:
                chunk(G_IN + 8 + c, w_in, 0, c * 512)
            with sp.Fori(0, 4) as n:
                for half in range(2):
                    chunk(G_OUT + 2 * n + half, w_out, 4 * half, n * 512)
            for (f0, nf), (gu, gd) in zip(FPARTS, G_FFN):
                with sp.Fori(0, nf) as f:
                    chunk(gu + 2 * f, w_up, 0, f * 512 + f0 * 512)
                    chunk(gu + 2 * f + 1, w_up, 0, f * 512 + (FF + f0 * 512))
                if nf == 4:
                    with sp.Fori(0, 4) as n:
                        chunk(gd + n, w_down, f0, n * 512)
                else:
                    for s in range(4 * nf):
                        slab(gd + s // 4, s % 4, w_down, f0 + s % nf, s // nf * 512)
            with sp.Fori(0, 4) as j:
                for i in range(3):
                    chunk(G_A + 3 * j + i, w_a, 0, j * 512 + i * D)
            with sp.Fori(0, 4) as j:
                chunk(G_GATE + j, w_a, 0, j * 512 + 3 * D)
            with sp.Fori(0, 4) as j:
                chunk(G_AOUT + j, w_ao, 0, j * 512)
            chunk(G_KV, w_kv, 0, 0)
            with sp.Fori(0, 4) as j:
                chunk(G_B + j, w_b, 0, j * 512)
            with sp.Fori(0, 4) as j:
                chunk(G_BG + j, w_b, 0, j * 512 + D)
            with sp.Fori(0, 4) as j:
                chunk(G_BOUT + j, w_bo, 0, j * 512)
            for b in range(2):
                sp.wait_ge(sem("result_ready"), b + 1)
                sp.dma_start(out[0, b * P:(b + 1) * P, :], h[:, b, :]).then_inc(sem("stored"), 16)
            sp.wait_ge(sem("stored"), 32)

        @block.gpsimd
        def _(pool):
            pool.memset(ident[:, :], 0.0).then_inc(sem("pool_own"), 1)
            pool.memset(ones[:, :], 1.0).then_inc(sem("const_ready"), 1)
            pool.memset(neghalf[:, :], -0.5).then_inc(sem("pool_own"), 1)
            pool.memset(st[:, :], 1.0).then_inc(sem("const_ready"), 1)
            pool.wait_ge(sem("pool_own"), 2)
            pool.affine_select(out=ident[:, :], in_=ident[:, :], compare_op=ALU.not_equal, fill=1.0, base=0,
                               pattern=[[-1, P]], channel_multiplier=1).then_inc(sem("const_ready"), 1)

            def acc_start(j, slot, n):
                pool.memset(acc[:, slot], 0.0).then_inc(sem("acc_zeroed"), 1)
                pool.wait_ge(sem("acc_zeroed"), n + 1)
                if n:
                    pool.wait_ge(sem("acc_started"), 16 * n)
                pool.dma_start(acc[0:1, slot], ada_b[:, j * D:(j + 1) * D]).then_inc(sem("acc_started"), 16)

            def stream_ada(j, k0, start=0, end=KT):
                for first, loop in (((0, False), (1, True)) if k0 == 0 else ((start, True),)):
                    def two(k):
                        for half in range(2):
                            if loop:
                                pool.wait_ge(ada_step, 2 * k + 2 * k0 - 1 + half)
                            src = ada_w[bass.ds(k * P, P), j * D + half * 1024:j * D + half * 1024 + 1024]
                            pool.dma_start(ada[:, half], src).then_inc(al[half], 16)
                    if loop:
                        with pool.Fori(first, end) as k:
                            two(k)
                    else:
                        two(first)

            def rsqrt(name, cin, cout, w, scale, eps, parts=P):
                x, y = st[0:parts, cin:cin + w], st[0:parts, cout:cout + w]
                pool.tensor_scalar(x, x, scale, eps, ALU.mult, ALU.add).then_inc(sem("rs1"), 1)
                pool.wait_ge(sem("rs1"), RS_AT[name])
                pool.tensor_tensor(y, x, neghalf[0:parts, 0:w], ALU.pow).then_inc(sem("rs"), 1)

            acc_start(0, 0, 0)
            acc_start(1, 1, 1)
            pool.wait_ge(sem("ss_n1"), 2)
            rsqrt("n1", 0, 4, 2, 1.0 / D, EPS1)
            pool.wait_ge(sem("mred"), 1)
            acc_start(2, 0, 2)
            stream_ada(2, 0)
            pool.wait_ge(sem("mred"), 2)
            acc_start(3, 1, 3)
            stream_ada(3, 16, 0, 2)
            pool.wait_ge(sem("ssv_ready"), 1)
            rsqrt("v", 8, 12, 2, 1.0 / GW, EPS1)
            stream_ada(3, 16, 2)
            pool.wait_ge(sem("mred"), 3)
            acc_start(4, 1, 4)
            stream_ada(4, 32)
            pool.wait_ge(sem("ss_n2"), 2)
            rsqrt("n2", 16, 20, 2, 1.0 / D, EPS1)
            acc_start(5, 0, 5)
            stream_ada(5, 48)
            for name, cin, n, eps in (("f", 24, 2, EPS1), ("a", 32, 3, EPS2)):
                pool.wait_ge(sem("ss_" + name), n)
                rsqrt(name, cin, cin + 4, n, 1.0 / D, eps)
            for i in range(ITEMS):
                pool.wait_ge(sem("oss"), i + 1)
                x, y = st[:, 100:101], st[:, 101:102]
                pool.tensor_scalar(x, x, 1.0 / 256, EPS2, ALU.mult, ALU.add).then_inc(sem("ors1"), 1)
                pool.wait_ge(sem("ors1"), i + 1)
                pool.tensor_tensor(y, x, neghalf[:, 0:1], ALU.pow).then_inc(sem("ors"), 1)
            pool.wait_ge(sem("ss_b"), 3)
            rsqrt("b", 48, 52, 3, 1.0 / D, EPS2)
            pool.wait_ge(sem("kk_ready"), 1)
            for e in range(2):
                for half in range(2):
                    pool.dma_start(kd[64 * half:64 * half + 64, e:4:2, :],
                                   kk[64 * e:64 * e + 64, 0:2, :]).then_inc(sem("kd_ready"), 16)
            pool.wait_ge(sem("ss_z"), 2)
            rsqrt("z", 56, 60, 2, 1.0 / D, EPS2)

        @block.scalar
        def _(act):
            def load(dst, src, name):
                act.dma_start(dst, src).then_inc(sem(name), 16)

            def cast(G, r, first=False):
                if r % 2 == 0:
                    act.wait_ge(ld[r // 2], G * 16 + 16)
                if not first:
                    act.wait_ge(unit_used, units_before(G) + (r - 3))
                act.activation(whi[:, r % 4], raw[:, r // 2, r % 2], ACT.Copy).then_inc(hi_ready, 1)

            def sums(name, srcs, cin):
                for b, src in enumerate(srcs):
                    w = src.shape[0]
                    if b:
                        act.wait_ge(sem("ss_" + name), b)
                    act.activation(junk[0:w, :], src, ACT.Square,
                                   accum_out=st[0:w, cin + b:cin + b + 1]).then_inc(sem("ss_" + name), 1)

            def spread(name, n, xh):
                for k in range(KT):
                    act.wait_ge(sem("ntmp"), TILES0[name] + k + 1)
                    act.activation(xh[:, k, 0:n], ntmp[:, k % 2, 0:n], ACT.Copy).then_inc(sem("nh"), 1)

            vecs = (a["c"][0], a["norm_g"][0, 0], a["norm_g"][0, 1], a["a_norm_2"][0], a["kv_norm_2"], a["b_norm_2"][0])
            for i, src in enumerate(vecs):
                load(rows[16 * i:16 * i + 16, 0, :], src.rearrange("(r q) -> r q", q=P), "rows_loaded")
            load(rows[0:16, 1, :], a["a_b_s"][0], "rows_loaded")
            load(rows[16:18, 1, :], a["a_subln_2"][0].rearrange("(r q) -> r q", q=P), "rows_loaded")
            act.wait_ge(sem("cols_ready"), 1)
            act.activation(ccol[:, :], cols[:, C_C], ACT.Silu).then_inc(sem("ccol_ready"), 1)
            act.wait_ge(sem("x_loaded"), 16)
            act.wait_ge(sem("const_ready"), 3)
            sums("n1", [h[:, 0, :], h[:, 1, :]], 0)
            spread("n1", T, xth)

            def v_out(c, par):
                act.wait_ge(unit_used, c * 8 + 8)
                for tok in range(2):
                    act.activation(v[:, bass.ds(c, 1), tok, :], ps[:, 2 * par + tok:2 * par + tok + 1, :],
                                   ACT.Gelu_apprx_tanh).then_inc(sem("v_ready"), 1)
                    act.wait_ge(sem("v_ready"), c * 2 + (tok + 1))
                    act.activation(utmp[:, None, :], v[:, bass.ds(c, 1), tok, :], ACT.Square,
                                   accum_out=st[:, bass.ds(c * 2 + (64 + tok), 1)]).then_inc(sem("ssv"), 1)

            def v_chunk(c, par, first=False):
                for r in range(8):
                    if r == 3 and not first:
                        v_out(c - 1, 1 - par)
                    cast(G_IN + c, r, first and r < 4)

            def ws_load(c):
                load(wsr[:, :, :], a["a_w_s"][0].rearrange("g p q -> p g q")[:, bass.ds(c * 2, 2), :], "ws_loaded")

            def gv_load(c):
                load(gvb[:, :], a["a_g_v"][0:1, bass.ds(c * 512, 512)].broadcast_to([P, 512]), "gv_loaded")

            v_chunk(0, 0, True)
            v_chunk(1, 1)
            ws_load(0)
            gv_load(0)
            with act.Fori(1, 4) as i:
                v_chunk(i * 2, 0)
                v_chunk(i * 2 + 1, 1)

            def u_out(c, par):
                act.wait_ge(unit_used, c * 8 + 72)
                for tok in range(2):
                    act.activation(ut[:, tok], ps[:, 2 * par + tok, :], ACT.Gelu_apprx_tanh)\
                       .then_inc(sem("u_ready"), 1)

            def us_out(c):
                act.wait_ge(sem("us_turned"), c * 2 + 2)
                for tok in range(2):
                    act.activation(ush[:, bass.ds(c * 4, 4), tok * P:tok * P + P],
                                   ps[:, 6 + tok, :].rearrange("p (k q) -> p k q", q=P), ACT.Copy)\
                       .then_inc(sem("ush_ready"), 1)

            def u_chunk(c, par, first=False, last=False):
                for r in range(8):
                    if r == 3:
                        if first:
                            v_out(7, 1)
                            act.wait_ge(sem("m2_spread"), 4)
                            for n in range(4):
                                act.activation(acc[:, 0, n * 512:n * 512 + 512], ps[:, 4 + n, :], ACT.Copy)\
                                   .then_inc(sem("m2b_ready"), 1)
                        else:
                            u_out(c - 1, 1 - par)
                    if r == 5 and not first:
                        act.wait_ge(sem("us_done"), c * 2)
                        gv_load(c)
                    if r == 6:
                        act.wait_ge(sem("ws_turned"), c + 1)
                        act.wait_ge(sem("rs"), RS_AT["v"])
                        for tok in range(2):
                            act.activation(wsc[:, tok].rearrange("p g q -> p (g q)"), ps[:, 6, 0:256], ACT.Copy,
                                           scale=st[:, 12 + tok:13 + tok]).then_inc(sem("wsc_ready"), 1)
                        if not last:
                            ws_load(c + 1)
                    if r == 7 and not first:
                        us_out(c - 1)
                    cast(G_IN + 8 + c, r)

            u_chunk(0, 0, first=True)
            u_chunk(1, 1)
            with act.Fori(1, 3) as i:
                u_chunk(i * 2, 0)
                u_chunk(i * 2 + 1, 1)
            u_chunk(6, 0)
            u_chunk(7, 1, last=True)

            for t in range(16):
                if t == 3:
                    u_out(7, 1)
                if t == 7:
                    us_out(7)
                    act.wait_ge(sem("ws_loaded"), 16 * 8)
                    act.wait_ge(sem("gv_loaded"), 16 * 8)
                    load(h[:, :, :], a["x"][0].rearrange("(b p) n -> p b n", p=P), "x_loaded")
                cast(*at(G_OUT, t))
            with act.Fori(1, 4) as n:
                for t in range(16):
                    cast(*at(G_OUT + n * 2, t))
            act.wait_ge(unit_used, units_before(G_OUT + 8))
            for i in range(3):
                load(crow[:, i, :], a["ffn_conv_w"][0, i].rearrange("(r q) -> r q", q=P), "crow_loaded")
            load(crow[:, 3, :], a["ffn_conv_b"][0].rearrange("(r q) -> r q", q=P), "crow_loaded")
            act.wait_ge(sem("resid"), 8)
            sums("n2", [h[:, 0, :], h[:, 1, :]], 16)
            spread("n2", T, xth)

            def taps(y, bank, blk, fsem):
                for n in range(4):
                    act.activation(y[:, n], ps[:, bank + n, 0:T], ACT.Identity, bias=cw[:, 3, bass.ds(blk + n, 1)],
                                   scale=cw[:, 1, bass.ds(blk + n, 1)]).then_inc(sem(fsem), 1)

            def value_out(F):
                act.wait_ge(unit_used, units_of(F) + 16)
                act.wait_ge(sem("hs_done"), F)
                taps(yv, 4, F * 4 + 44, "yv_ready")

            def h_out(F, f):
                act.wait_ge(sem("hs_done"), F + 1)
                act.activation(hth[:, bass.ds(f * 4, 4), :], hs[:, :, :], ACT.Copy).then_inc(sem("hth_ready"), 1)

            for p, ((f0, nf), (gu, gd)) in enumerate(zip(FPARTS, G_FFN)):
                ubase = units_before(gu) - 16 * f0
                units_of = lambda F, ub=ubase: F * 16 + ub

                def pair(f, first=False):
                    F = f + f0
                    for t in range(16):
                        if t == 3 and not first:
                            value_out(F - 1)
                        if t == 5 and not first:
                            h_out(F - 1, f - 1)
                        if t == 11:
                            act.wait_ge(unit_used, units_of(F) + 8)
                            act.wait_ge(sem("hs_done"), F)
                            taps(yg, 0, F * 4, "yg_ready")
                        if t == 13:
                            act.wait_ge(sem("yg_done"), F + 1)
                            act.activation(sg[:, :, :], yg[:, :, :], ACT.Silu).then_inc(sem("sg_ready"), 1)
                        cast(*at(gu + f * 2, t))

                pair(0, True)
                with act.Fori(1, nf) as f:
                    pair(f)
                for t in range(8 * nf):
                    if t == 3:
                        value_out(f0 + nf - 1)
                    if t == 5:
                        h_out(f0 + nf - 1, nf - 1)
                    if p == 0 and t == 10:
                        act.wait_ge(sem("m5_spread"), 4)
                        for n in range(4):
                            act.activation(acc[:, 0, n * 512:n * 512 + 512], ps[:, 4 + n, :], ACT.Copy)\
                               .then_inc(sem("m5b_ready"), 1)
                    cast(*at(gd, t))
            load(bcast[:, :], a["final_g"].rearrange("(o n) -> o n", o=1).broadcast_to([P, D]), "bcast_loaded")
            act.wait_ge(sem("resid_f"), 24)
            sums("f", [h[:, 0, :], h[:, 1, :]], 24)

            load(hm[0:NM, :], a["meta_tokens_2"], "meta_loaded")
            act.wait_ge(sem("x2_ready"), 2)
            act.wait_ge(sem("meta_loaded"), 16)
            sums("a", [h[:, 0, :], hm[0:NM, :], h[:, 1, :]], 32)
            act.wait_ge(sem("ss_a"), 3)
            for i, name in enumerate(("a_lambda_q1_2", "a_lambda_k1_2", "a_lambda_q2_2", "a_lambda_k2_2")):
                load(lamv[0:1, i, :], a[name], "lamv_loaded")
            load(tabA[:, :, :], a["tab_a"], "tabA_loaded")
            load(rotA[:, :], a["rot_a"], "tabA_loaded")
            spread("a", L, xmh)
            act.wait_ge(sem("lam_sum"), 1)
            act.activation(st[0:1, 116:118], st[0:1, 114:116], ACT.Exp).then_inc(sem("lam_exp"), 1)

            def banks_out(n, G, func, dst, done):
                for c in range(4):
                    if c < 3:
                        act.wait_ge(bank_done, n * 3 + (c + 1))
                    else:
                        act.wait_ge(unit_used, units_before(G))
                    act.activation(dst[:, c, :], ps[:, c, 0:L], func, scale=0.5 if func == ACT.Tanh else 1.0)\
                       .then_inc(sem(done), 1)

            def item_act(t, j, items=True, before=True):
                for i, back in due(t, 4, items, before):
                    it, nk = (j - back) * 6 + i, ITEM_KEYS[i % 3][1]
                    act.wait_ge(sem("a_max"), it + 1)
                    for e in range(2):
                        act.activation(ex[:, e, 0:nk], sc[:, e, 0:nk], ACT.Exp, bias=st[:, 104 + e:105 + e],
                                       accum_out=st[:, 106 + e:107 + e]).then_inc(sem("a_exp"), 1)
                for i, back in due(t, 6, items, before):
                    it = (j - back) * 6 + i
                    act.wait_ge(sem("a_wturned"), it + 1)
                    for kb in ITEM_BLOCKS[i % 3]:
                        w = BLK[kb][1]
                        cp = act.activation(wt[0:w, kb, :], ps[0:w, 6, kb * P:kb * P + P], ACT.Copy)
                    cp.then_inc(sem("a_wt"), 1)
                for i, back in due(t, 7, items, before):
                    act.wait_ge(sem("a_pv"), (j - back) * 6 + (i + 1))
                    act.activation(ojunk[:, :], ps[:, 7, 0:256], ACT.Square,
                                   accum_out=st[:, 100:101]).then_inc(sem("oss"), 1)

            def group_act(j, t, before=True):
                if t == 1:
                    act.wait_ge(sem("rope_done"), j * 4)
                    if before:
                        act.wait_ge(sem("a_scores"), (j - 1) * 6)
                    act.activation(qt[:, :, :], qs[:, :, :], ACT.Copy).then_inc(sem("qk_moved"), 1)
                    act.activation(kt_[:, :, :], ks[:, :, :], ACT.Copy).then_inc(sem("qk_moved"), 1)
                if t == 4:
                    act.wait_ge(sem("qk_moved"), j * 2)
                    banks_out(3 * j - 1, G_A + 3 * j, ACT.Copy, qs, "bank_read")
                if t == 6:
                    act.wait_ge(sem("v_turned"), j)
                    for b, (c0, w) in enumerate(BLK):
                        cp = act.activation(vx[0:w, b, :], ps[0:w, 4 + b, :], ACT.Copy)
                    cp.then_inc(sem("vx_ready"), 1)

            def heads(j, items=True, before=True):
                for t in range(24):
                    item_act(t, j, items, before)
                    if items:
                        group_act(j, t, before)
                    if t == 12:
                        banks_out(3 * j, G_A + (3 * j + 1), ACT.Copy, qs, "bank_read")
                    if t == 20:
                        banks_out(3 * j + 1, G_A + (3 * j + 2), ACT.Copy, ks, "bank_read")
                    cast(*at(G_A + j * 3, t))

            heads(0, False, False)
            heads(1, True, False)
            with act.Fori(2, 4) as j:
                heads(j)

            def gate_out(g):
                banks_out(12 + g, G_GATE + g + 1, ACT.Tanh, gth, "gth_ready")

            def oth_out(g):
                act.wait_ge(sem("g_prod"), g + 1)
                act.activation(oth[:, 4 * g:4 * g + 4, :], g2[:, :, :], ACT.Copy).then_inc(sem("oth_ready"), 1)

            for t in range(40):
                if t < 24:
                    item_act(t, 4)
                    group_act(4, t)
                else:
                    item_act(t - 24, 5, items=False)
                if t % 8 == 4 and t > 8:
                    gate_out(t // 8 - 1)
                if t % 8 == 6 and t > 8:
                    oth_out(t // 8 - 1)
                cast(*at(G_GATE, t))

            def y_out(j):
                banks_out(16 + j, G_AOUT + (j + 1), ACT.Copy, yt, "bank_read")

            with act.Fori(1, 4) as j:
                for r in range(8):
                    if r == 4:
                        y_out(j - 1)
                    cast(G_AOUT + j, r)
            y_out(3)

            act.wait_ge(sem("y_added"), 12)
            load(tabB[:, :, :], a["tab_b"], "tabB_loaded")
            load(rotB[:, :], a["rot_b"], "tabB_loaded")
            sums("b", [h[:, 0, :], hm[0:NM, :], h[:, 1, :]], 48)
            spread("b", L, xmh)
            spread("b2", T, bxh)
            for r in range(8):
                cast(G_KV, r)
            act.wait_ge(unit_used, units_before(G_KV + 1))
            load(tabq[:, :, :, :], a["tab_q"], "tabq_loaded")
            load(sinkb[:, :], a["b_sinks_2"].broadcast_to([P, 32]), "tabq_loaded")
            act.activation(kk[:, :, :], ps[:, 0:4, 0:L], ACT.Copy).then_inc(sem("kk_raw"), 1)
            act.wait_ge(sem("vb_turned"), 1)
            for b, (c0, w) in enumerate(BLK):
                cp = act.activation(vb[0:w, b, :], ps[0:w, (6, 6, 7)[b], (0, 256, 0)[b]:(0, 256, 0)[b] + 256], ACT.Copy)
            cp.then_inc(sem("vb_ready"), 1)

            def quad_act(t):
                for n in quads(t, 4):
                    nk = (144, L)[n // 2 % 2]
                    act.wait_ge(sem("b_max"), n + 1)
                    act.activation(st[:, 136:140], st[:, 132:136], ACT.Exp).then_inc(sem("b_sexp"), 1)
                    for i in range(4):
                        act.activation(eb_[:, i, 0:nk], sb_[:, i, 0:nk], ACT.Exp, bias=st[:, 128 + i:129 + i],
                                       accum_out=st[:, 140 + i:141 + i]).then_inc(sem("b_exp"), 1)
                for n in quads(t, 6):
                    act.wait_ge(sem("b_wturned"), n + 1)
                    for kb in range(2 + n // 2 % 2):
                        w = BLK[kb][1]
                        cp = act.activation(wtb[0:w, kb], ps[0:w, TURN_BANK[kb], :].rearrange("p (i q) -> p i q", q=P),
                                            ACT.Copy)
                    cp.then_inc(sem("b_wt"), 1)

            def pair_out(n, func, dst, done):
                for tok in range(2):
                    if tok == 0:
                        act.wait_ge(sem("pair_done"), n + 1)
                    else:
                        act.wait_ge(unit_used, units_before(G_B + n + 1))
                    act.activation(dst[:, tok, :], ps[:, tok, :], func, scale=0.5 if func == ACT.Tanh else 1.0)\
                       .then_inc(sem(done), 1)

            for t in range(72):
                quad_act(t)
                if t % 8 == 4 and t > 8:
                    n = t // 8 - 1
                    if n < 4:
                        pair_out(n, ACT.Copy, qx, "pair_read")
                    else:
                        pair_out(n, ACT.Tanh, gb1, "gb_ready")
                if t - 4 in Q_TURN_AT:
                    j = Q_TURN_AT.index(t - 4)
                    act.wait_ge(sem("q_turned"), j + 1)
                    for tok in range(2):
                        cp = act.activation(qtb[:, j, :, tok * P:tok * P + P],
                                            ps[:, 5 + tok, :].rearrange("p (k q) -> p k q", q=P), ACT.Copy)
                    cp.then_inc(sem("qtb_ready"), 1)
                if t - 4 in O_TURN_AT:
                    j = O_TURN_AT.index(t - 4)
                    act.wait_ge(sem("ob_turned"), j + 1)
                    for tok in range(2):
                        cp = act.activation(obh[:, 4 * j:4 * j + 4, tok * P:tok * P + P],
                                            ps[:, 5 + tok, :].rearrange("p (k q) -> p k q", q=P), ACT.Copy, scale=0.5)
                    cp.then_inc(sem("obh_ready"), 1)
                cast(*at(G_B, t))
            with act.Fori(1, 4) as j:
                for r in range(8):
                    cast(G_BOUT + j, r)
            load(bcast[:, :], a["final_norm_2"].rearrange("(o n) -> o n", o=1).broadcast_to([P, D]), "bcast_loaded")
            act.wait_ge(sem("resid_b"), 8)
            sums("z", [h[:, 0, :], h[:, 1, :]], 56)

        @block.vector
        def _(dve):
            def lo(G, r):
                dve.wait_ge(hi_ready, units_before(G) + (r + 1))
                dve.tensor_tensor(wlo[:, r % 4], raw[:, r // 2, r % 2], whi[:, r % 4].bitcast(F32),
                                  ALU.subtract).then_inc(lo_ready, 1)

            def ada_add(k, kt, half, slot):
                dve.wait_ge(al[half], k * 16 + 16)
                dve.wait_ge(ada_step, k * 2 + (half - 1))
                y = acc[:, slot, half * 1024:half * 1024 + 1024]
                dve.scalar_tensor_tensor(out=y, in0=ada[:, half], scalar=ccol[:, bass.ds(kt, 1)], in1=y,
                                         op0=ALU.mult, op1=ALU.add).then_inc(ada_step, 1)

            def diagonals(name, col, blocks):
                dve.wait_ge(sem("rs"), RS_AT[name])
                for i, w in enumerate(blocks):
                    d = dve.tensor_scalar(dg[0:w, i, 0:w], ident[0:w, 0:w], st[0:w, col + i:col + i + 1], None, ALU.mult)
                d.then_inc(sem("dg"), 1)

            def spread(name, n, xh, xl, gain, shift):
                def low(k):
                    dve.wait_ge(sem("nh"), TILES0[name] + k + 1)
                    dve.tensor_tensor(xl[:, k, 0:n], ntmp[:, k % 2, 0:n], xh[:, k, 0:n].bitcast(F32),
                                      ALU.subtract).then_inc(sem("nl"), 1)

                for k in range(KT):
                    dve.wait_ge(sem("nt"), TILES0[name] + k + 1)
                    if k > 1:
                        dve.wait_ge(sem("nl"), TILES0[name] + k - 1)
                    src = ps[:, 4 + k % 4, 0:n]
                    if shift is None:
                        ins = dve.tensor_scalar(ntmp[:, k % 2, 0:n], src, gain[:, k:k + 1], None, ALU.mult)
                    else:
                        ins = dve.tensor_scalar(ntmp[:, k % 2, 0:n], src, gain[:, k:k + 1], shift[:, k:k + 1],
                                                ALU.mult, ALU.add)
                    ins.then_inc(sem("ntmp"), 1)
                    if k:
                        low(k - 1)
                low(KT - 1)

            own = Own(dve, sem("dve_own"))

            dve.wait_ge(sem("cols_turned"), 1)
            dve.tensor_copy(cols[:, :], ps[:, 0, 0:114]).then_inc(sem("cols_ready"), 1)
            dve.wait_ge(sem("ccol_ready"), 1)
            for j in range(2):
                dve.wait_ge(sem("acc_started"), 16 * (j + 1))
                with dve.Fori(0, 4) as i:
                    for q in range(4):
                        dve.wait_ge(ld[q], i * 16 + (64 * j + 16))
                        if q or j:
                            dve.wait_ge(ada_used, i * 4 + (16 * j + q))
                        else:
                            dve.wait_ge(ada_used, i * 4)
                        dve.scalar_tensor_tensor(out=acc[:, j], in0=rawv[:, q], scalar=ccol[:, bass.ds(i * 4 + q, 1)],
                                                 in1=acc[:, j], op0=ALU.mult, op1=ALU.add).then_inc(ada_used, 1)
            diagonals("n1", 4, (P, P))
            dve.wait_ge(sem("cols_ready"), 1)
            dve.wait_ge(sem("mred"), 2)
            own(dve.tensor_copy(mcol[:, 0:2], ps[:, 1, 0:32].rearrange("p (m k) -> p m k", k=KT)))
            dve.scalar_tensor_tensor(out=acol[:, :], in0=mcol[:, 1], scalar=1.0, in1=cols[:, C_G0],
                                     op0=ALU.add, op1=ALU.mult).then_inc(sem("gain_n1"), 1)
            dve.wait_ge(sem("gain_n1"), 1)
            spread("n1", T, xth, xtl, acol, mcol[:, 0])

            dve.wait_ge(sem("acc_started"), 48)
            with dve.Fori(0, 8) as c:
                for r in range(8):
                    lo(G_IN + c, r)
                    if r % 2 == 0:
                        if r < 2:
                            dve.wait_ge(al[0], c * 32 + 16)
                            y = acc[:, 0, 0:1024]
                            dve.wait_ge(ada_step, c * 4)
                            dve.scalar_tensor_tensor(out=y, in0=ada[:, 0], scalar=ccol[:, bass.ds(c * 2, 1)], in1=y,
                                                     op0=ALU.mult, op1=ALU.add).then_inc(ada_step, 1)
                        else:
                            ada_add(c * 2 + r // 4, c * 2 + r // 4, r // 2 % 2, 0)

            def u_mix(c):
                for tok in range(2):
                    dve.wait_ge(sem("mixed"), c * 2 + (tok + 1))
                    dve.wait_ge(sem("gv_loaded"), c * 16 + 16)
                    dve.wait_ge(sem("us_done"), c * 2 + tok)
                    dve.tensor_tensor(utmp[:, :], ps[:, 4 + tok, :], gvb[:, :], ALU.mult).then_inc(sem("us_own"), 1)
                    dve.wait_ge(sem("us_own"), c * 2 + (tok + 1))
                    dve.wait_ge(sem("u_ready"), c * 2 + (tok + 1))
                    for g in range(2):
                        ins = dve.scalar_tensor_tensor(
                            out=us[:, tok, g * 256:g * 256 + 256], in0=utmp[:, g * 256:g * 256 + 256],
                            scalar=cols[:, bass.ds(c * 2 + (C_BS + g), 1)], in1=ut[:, tok, g * 256:g * 256 + 256],
                            op0=ALU.add, op1=ALU.mult)
                    ins.then_inc(sem("us_done"), 1)

            def us_lo(c):
                dve.wait_ge(sem("ush_ready"), c * 2 + 2)
                for tok in range(2):
                    dve.tensor_tensor(usl[:, bass.ds(c * 4, 4), tok * P:tok * P + P],
                                      ps[:, 6 + tok, :].rearrange("p (k q) -> p k q", q=P),
                                      ush[:, bass.ds(c * 4, 4), tok * P:tok * P + P].bitcast(F32),
                                      ALU.subtract).then_inc(sem("usl_ready"), 1)

            dve.wait_ge(sem("acc_started"), 64)

            def u_chunk(c, first=False):
                for r in range(8):
                    if first and r == 4:
                        dve.wait_ge(sem("ssv"), 16)
                        dve.tensor_reduce(st[:, 8:10], st[:, 64:80].rearrange("p (c t) -> p t c", t=2), AX.X,
                                          ALU.add).then_inc(sem("ssv_ready"), 1)
                    if not first and r == 5:
                        u_mix(c - 1)
                    if not first and r == 7:
                        us_lo(c - 1)
                    lo(G_IN + 8 + c, r)
                    if r % 2 == 0:
                        ada_add(c * 2 + (16 + r // 4), c * 2 + r // 4, r // 2 % 2, 1)

            u_chunk(0, True)
            with dve.Fori(1, 8) as c:
                u_chunk(c)

            def residual(n, par, gate, s, base):
                gy = gy1 if s == "resid" else gy2
                for tok in range(2):
                    y = ps[:, 2 * par + tok, :]
                    hc = h[:, tok, bass.ds(n * 512, 512)]
                    if gate is not None:
                        dve.tensor_tensor(gy[:, tok], y, gate[:, bass.ds(n * 512, 512)], ALU.mult)\
                           .then_inc(sem("gated_" + s), 1)
                        dve.wait_ge(sem("gated_" + s), n * 2 + (base + tok + 1))
                        y = gy[:, tok]
                    dve.tensor_tensor(hc, hc, y, ALU.add).then_inc(sem(s), 1)

            for n in range(4):
                for t in range(16):
                    if n == 0 and t == 5:
                        u_mix(7)
                    if n == 0 and t == 7:
                        us_lo(7)
                    if n == 0 and t == 12:
                        dve.wait_ge(sem("mred"), 3)
                        dve.tensor_copy(mcol[:, 2], ps[:, 4, 0:KT]).then_inc(sem("mcol3"), 1)
                    if n and t == 3:
                        dve.wait_ge(unit_used, units_before(G_OUT) + 16 * n)
                        dve.wait_ge(sem("x_loaded"), 32)
                        if n == 1:
                            dve.wait_ge(sem("m2b_ready"), 4)
                        residual(n - 1, (n - 1) % 2, acc[:, 0], "resid", 0)
                    lo(*at(G_OUT, 16 * n + t))
                    step = t - t // 4
                    if n == 1 and t == 0:
                        dve.wait_ge(sem("acc_started"), 80)
                    if n in (1, 2) and t % 4 != 3:
                        ada_add(32 + 6 * (n - 1) + step // 2, 6 * (n - 1) + step // 2, step % 2, 1)
                    if n == 3 and t < 8:
                        ada_add(32 + 12 + t // 2, 12 + t // 2, t % 2, 1)
            dve.wait_ge(unit_used, units_before(G_OUT + 8))
            residual(3, 1, acc[:, 0], "resid", 0)

            dve.wait_ge(sem("conv_turned"), 1)
            dve.tensor_copy(cw[:, :, :].rearrange("p i b -> p (i b)"), ps[:, 0, 0:352]).then_inc(sem("cw_ready"), 1)
            diagonals("n2", 20, (P, P))
            dve.wait_ge(sem("mred"), 4)
            own(dve.tensor_copy(mcol[:, 3], ps[:, 1, 0:KT]))
            dve.scalar_tensor_tensor(out=acol[:, :], in0=mcol[:, 3], scalar=1.0, in1=cols[:, C_G1],
                                     op0=ALU.add, op1=ALU.mult).then_inc(sem("gain_n2"), 1)
            dve.wait_ge(sem("gain_n2"), 1)
            spread("n2", T, xth, xtl, acol, mcol[:, 2])
            dve.wait_ge(sem("acc_started"), 96)

            def side_taps(y, bank, blk, ysem, F, done):
                dve.wait_ge(sem(ysem), F * 4 + 4)
                for n in range(4):
                    dve.scalar_tensor_tensor(out=y[:, n, 1:T], in0=ps[:, bank + n, 0:T - 1],
                                             scalar=cw[:, 0, bass.ds(blk + n, 1)], in1=y[:, n, 1:T],
                                             op0=ALU.mult, op1=ALU.add).then_inc(sem("tap_" + ysem), 1)
                for n in range(4):
                    dve.wait_ge(sem("tap_" + ysem), F * 4 + (n + 1))
                    ins = dve.scalar_tensor_tensor(out=y[:, n, 0:T - 1], in0=ps[:, bank + n, 1:T],
                                                   scalar=cw[:, 2, bass.ds(blk + n, 1)], in1=y[:, n, 0:T - 1],
                                                   op0=ALU.mult, op1=ALU.add)
                ins.then_inc(sem(done), 1)

            def value_done(F):
                side_taps(yv, 4, F * 4 + 44, "yv_ready", F, "yv_done")
                dve.wait_ge(sem("yv_done"), F + 1)
                dve.wait_ge(sem("sg_ready"), F + 1)
                dve.tensor_tensor(hs[:, :, :], sg[:, :, :], yv[:, :, :], ALU.mult).then_inc(sem("hs_done"), 1)

            def h_lo(F, f):
                dve.wait_ge(sem("hth_ready"), F + 1)
                dve.tensor_tensor(htl[:, bass.ds(f * 4, 4), :], hs[:, :, :], hth[:, bass.ds(f * 4, 4), :].bitcast(F32),
                                  ALU.subtract).then_inc(sem("htl_ready"), 1)

            for p, ((f0, nf), (gu, gd)) in enumerate(zip(FPARTS, G_FFN)):
                def pair(f, first=False):
                    F = f + f0
                    for t in range(16):
                        if first and p and t == 3:
                            dve.wait_ge(unit_used, units_before(gu))
                            residual(3, 1, acc[:, 0], "resid_f", 8 * (p - 1))
                        if t == 3 and not first:
                            value_done(F - 1)
                        if t == 6 and not first:
                            h_lo(F - 1, f - 1)
                        if t == 11:
                            side_taps(yg, 0, F * 4, "yg_ready", F, "yg_done")
                        lo(*at(gu + f * 2, t))
                        if p == 0 and t % 2 == 0:
                            ada_add(f * 4 + (48 + t // 4), f * 4 + t // 4, t // 2 % 2, 0)

                pair(0, True)
                with dve.Fori(1, nf) as f:
                    pair(f)
                for t in range(8 * nf):
                    n, r = t // (2 * nf), t % (2 * nf)
                    if t == 3:
                        value_done(f0 + nf - 1)
                    if t == 6 and nf > 3 or t == 5 and nf == 3:
                        h_lo(f0 + nf - 1, nf - 1)
                    if n and r == 3:
                        dve.wait_ge(unit_used, units_before(gd) + 2 * nf * n)
                        if p == 0 and n == 1:
                            dve.wait_ge(sem("m5b_ready"), 4)
                        residual(n - 1, (n - 1) % 2, acc[:, 0], "resid_f", 8 * p)
                    lo(*at(gd, t))
            dve.wait_ge(unit_used, units_before(G_A))
            residual(3, 1, acc[:, 0], "resid_f", 16)

            dve.wait_ge(sem("rs"), RS_AT["f"])
            dve.wait_ge(sem("bcast_loaded"), 16)
            for b in range(2):
                dve.scalar_tensor_tensor(out=h[:, b, :], in0=h[:, b, :], scalar=st[:, 28 + b:29 + b], in1=bcast[:, :],
                                         op0=ALU.mult, op1=ALU.mult).then_inc(sem("x2_ready"), 1)
            for t, rects in ((maskA, ((0, 64, 64, 128, 0), (0, 64, 208, L, 1))),):
                own(dve.memset(t[:, :, :], 0.0))
                for p0, p1, c0, c1, b in rects:
                    own(dve.memset(t[p0:p1, b, c0:c1], NEG))
            dve.wait_ge(sem("lamv_loaded"), 64)
            for i in range(2):
                own(dve.tensor_tensor(lamv[0:1, 4, :], lamv[0:1, 2 * i, :], lamv[0:1, 2 * i + 1, :], ALU.mult))
                own(dve.tensor_reduce(st[0:1, 114 + i:115 + i], lamv[0:1, 4, :], AX.X, ALU.add))
            dve.tensor_scalar(st[:, 112:114], cols[:, C_SUB:C_SUB + 2], 0.4, None, ALU.mult).then_inc(sem("lam_sum"), 1)
            diagonals("a", 36, (P, NM, P))
            spread("a", L, xmh, xml, cols[:, C_AN], None)
            dve.wait_ge(sem("lam_exp"), 1)
            dve.wait_ge(sem("lam_sum"), 1)
            own(dve.tensor_tensor(st[0:1, 118:119], st[0:1, 117:118], st[0:1, 116:117], ALU.subtract))
            dve.tensor_scalar(st[0:1, 119:120], st[0:1, 118:119], -0.2, None, ALU.add).then_inc(sem("nlam"), 1)
            dve.wait_ge(sem("nlam_ps"), 1)
            own(dve.tensor_copy(st[:, 111:112], ps[:, 4, 0:1]))

            def rope(j, q):
                x = (qs, ks)[q // 2][0:32, q % 2 * 2:q % 2 * 2 + 2, :]
                n = j * 4 + q
                dve.wait_ge(sem("rot"), n + 1)
                if not isinstance(n, int) or n:
                    dve.wait_ge(sem("rope_done"), n)
                dve.tensor_tensor(rt2[:, :, :], ps[0:32, 4:6, 0:L], tabA[:, 1:2, :].broadcast_to([32, 2, L]),
                                  ALU.mult).then_inc(sem("rope_read"), 1)
                dve.tensor_tensor(x, x, tabA[:, 0:1, :].broadcast_to([32, 2, L]), ALU.mult).then_inc(sem("rope_own"), 1)
                dve.wait_ge(sem("rope_read"), n + 1)
                dve.wait_ge(sem("rope_own"), n + 1)
                dve.tensor_tensor(x, x, rt2[:, :, :], ALU.add).then_inc(sem("rope_done"), 1)

            def item_dve(t, j, items=True, before=True):
                for i, back in due(t, 4, items, before):
                    it, b = (j - back) * 6 + i, i % 3
                    own3 = Own(dve, sem("item_own"), it * 5)
                    nk = ITEM_KEYS[b][1]
                    dve.wait_ge(sem("a_scores"), it + 1)
                    s = sc[:, :, 0:nk]
                    if b == 1:
                        own3(dve.tensor_scalar(s, ps[:, 4:6, 0:nk], AH ** -0.5, None, ALU.mult))
                    else:
                        own3(dve.scalar_tensor_tensor(out=s, in0=ps[:, 4:6, 0:nk], scalar=AH ** -0.5,
                                                      in1=maskA[:, b // 2:b // 2 + 1, 0:nk].broadcast_to([P, 2, nk]),
                                                      op0=ALU.mult, op1=ALU.add))
                    own3(dve.tensor_reduce(st[:, 102:104], s, AX.X, ALU.max))
                    dve.tensor_scalar(st[:, 104:106], st[:, 102:104], -1.0, None, ALU.mult).then_inc(sem("a_max"), 1)
                for i, back in due(t, 5, items, before):
                    it, nk = (j - back) * 6 + i, ITEM_KEYS[i % 3][1]
                    own3 = Own(dve, sem("item_own"), it * 5 + 2)
                    dve.wait_ge(sem("a_exp"), it * 2 + 2)
                    own3(dve.reciprocal(st[:, 108:110], st[:, 106:108]))
                    own3(dve.tensor_scalar(st[:, 110:111], st[:, 109:110], st[:, 111:112], None, ALU.mult))
                    own3(dve.tensor_scalar(wd[:, 0:nk], ex[:, 0, 0:nk], st[:, 108:109], None, ALU.mult))
                    dve.scalar_tensor_tensor(out=wd[:, 0:nk], in0=ex[:, 1, 0:nk], scalar=st[:, 110:111],
                                             in1=wd[:, 0:nk], op0=ALU.mult, op1=ALU.add).then_inc(sem("a_w"), 1)
                for i, back in due(t, 8, items, before):
                    dve.wait_ge(sem("ors"), (j - back) * 6 + (i + 1))
                    dve.tensor_scalar(on[:, :], ps[:, 7, 0:256], st[:, 101:102], None, ALU.mult).then_inc(sem("a_on"), 1)
                for i, back in due(t, 9, items, before):
                    c0, w = BLK[i % 3]
                    dve.wait_ge(sem("a_oturned"), (j - back) * 6 + (i + 1))
                    for d in range(2):
                        dve.tensor_scalar(ot[:, bass.ds((j - back) * 4 + (2 * (i // 3) + d), 1), c0:c0 + w],
                                          ps[:, 7:8, 256 + d * P:256 + d * P + w], st[:, 112 + d:113 + d], None,
                                          ALU.mult).then_inc(sem("a_ot"), 1)

            def heads(j, items=True, before=True):
                for t in range(24):
                    if t == 0 and items:
                        rope(j - 1, 3)
                    item_dve(t, j, items, before)
                    if t - 4 in ROPE_AT:
                        rope(j, ROPE_AT.index(t - 4))
                    lo(*at(G_A + j * 3, t))

            heads(0, False, False)
            heads(1, True, False)
            with dve.Fori(2, 4) as j:
                heads(j)

            def gate(g):
                for c in range(4):
                    dve.wait_ge(sem("gth_ready"), g * 4 + c + 1)
                    dve.scalar_tensor_tensor(out=g2[:, c, :], in0=gth[:, c, :], scalar=1.0, in1=ps[:, c, 0:L],
                                             op0=ALU.add, op1=ALU.mult).then_inc(sem("bank_read"), 1)
                dve.wait_ge(sem("bank_read"), (12 + g) * 4 + 4)
                dve.tensor_tensor(g2[:, :, :], g2[:, :, :], ot[:, 4 * g:4 * g + 4, :], ALU.mult).then_inc(sem("g_prod"), 1)

            def otl_out(g):
                dve.wait_ge(sem("oth_ready"), g + 1)
                dve.tensor_tensor(otl[:, 4 * g:4 * g + 4, :], g2[:, :, :], oth[:, 4 * g:4 * g + 4, :].bitcast(F32),
                                  ALU.subtract).then_inc(sem("g_done"), 1)

            for t in range(40):
                if t == 0:
                    rope(3, 3)
                if t < 24:
                    item_dve(t, 4)
                else:
                    item_dve(t - 24, 5, items=False)
                if t % 8 == 4 and t > 8:
                    if t > 12:
                        dve.wait_ge(sem("g_done"), t // 8 - 1)
                    gate(t // 8 - 1)
                if t % 8 == 7 and t > 8:
                    otl_out(t // 8 - 1)
                lo(*at(G_GATE, t))

            def y_add(j):
                dve.wait_ge(sem("y_turned"), j + 1)
                for b, (c0, w) in enumerate(BLK):
                    hb = (h[:, 0], hm[0:NM], h[:, 1])[b]
                    hc = hb[:, bass.ds(j * 512, 512)]
                    dve.tensor_tensor(hc, hc, ps[0:w, 4 + b, :], ALU.add).then_inc(sem("y_added"), 1)

            with dve.Fori(1, 4) as j:
                for r in range(8):
                    if r == 6:
                        y_add(j - 1)
                    lo(G_AOUT + j, r)
            y_add(3)

            own4 = Own(dve, sem("dve_own_b"))
            diagonals("b", 52, (P, NM, P))
            spread("b", L, xmh, xml, cols[:, C_KVN], None)
            own4(dve.memset(maskB[:, :, :], 0.0))
            for p0, p1, c0, c1, b in ((0, 64, 64, 128, 0), (0, 64, 208, L, 1), (64, 128, 0, 64, 1)):
                own4(dve.memset(maskB[p0:p1, b, c0:c1], NEG))
            spread("b2", T, bxh, bxl, cols[:, C_BN], None)
            for r in range(8):
                lo(G_KV, r)
            dve.wait_ge(sem("kk_raw"), 1)
            dve.wait_ge(sem("tabB_loaded"), 32)
            own4(dve.tensor_tensor(kt1[:, :, :], kk[:, 0:2, :], tabB[:, 0:1, :].broadcast_to([P, 2, L]), ALU.mult))
            dve.wait_ge(sem("rotb"), 1)
            own4(dve.tensor_tensor(kt2[:, :, :], ps[:, 4:6, 0:L], tabB[:, 1:2, :].broadcast_to([P, 2, L]), ALU.mult))
            dve.tensor_tensor(kk[:, 0:2, :], kt1[:, :, :], kt2[:, :, :], ALU.add).then_inc(sem("kk_ready"), 1)
            dve.wait_ge(sem("tabq_loaded"), 32)

            qv = qx[:, :, :].rearrange("p t (h d) -> p t h d", d=BH)

            def quad_dve(t):
                for n in quads(t, 4):
                    j, tok, half = n // 4, n // 2 % 2, n % 2
                    own6 = Own(dve, sem("quad_own"), n * 6)
                    nk = (144, L)[tok]
                    dve.wait_ge(sem("b_scores"), n + 1)
                    s = sb_[:, :, 0:nk]
                    sink = sinkb[:, j * 8 + 4 * half:j * 8 + 4 * half + 4]
                    own6(dve.scalar_tensor_tensor(out=s, in0=ps[:, 4:8, 0:nk], scalar=BH ** -0.5,
                                                  in1=maskB[:, tok:tok + 1, 0:nk].broadcast_to([P, 4, nk]),
                                                  op0=ALU.mult, op1=ALU.add))
                    own6(dve.tensor_reduce(st[:, 120:124], s, AX.X, ALU.max))
                    own6(dve.tensor_tensor(st[:, 124:128], st[:, 120:124], sink, ALU.max))
                    own6(dve.tensor_scalar(st[:, 128:132], st[:, 124:128], -1.0, None, ALU.mult))
                    dve.tensor_tensor(st[:, 132:136], sink, st[:, 124:128], ALU.subtract).then_inc(sem("b_max"), 1)
                for n in quads(t, 5):
                    own6 = Own(dve, sem("quad_own"), n * 6 + 4)
                    dve.wait_ge(sem("b_exp"), n * 4 + 4)
                    own6(dve.tensor_tensor(st[:, 144:148], st[:, 140:144], st[:, 136:140], ALU.add))
                    if n:
                        dve.wait_ge(sem("b_o"), n)
                    own6(dve.reciprocal(st[:, 148:152], st[:, 144:148]))
                for n in quads(t, 7):
                    j, tok, half = n // 4, n // 2 % 2, n % 2
                    dve.wait_ge(sem("b_pv"), n + 1)
                    dve.tensor_tensor(ob[:, j, tok, half * 256:half * 256 + 256].rearrange("p (i d) -> p i d", d=BH),
                                      ps[:, 2, 0:256].rearrange("p (i d) -> p i d", d=BH),
                                      st[:, 148:152].unsqueeze(2).broadcast_to([P, 4, BH]), ALU.mult)\
                       .then_inc(sem("b_o"), 1)

            def rope_q(j, tok):
                own5 = Own(dve, sem("qrope_own"), j * 6 + tok * 3)
                own5(dve.tensor_tensor(rta[:, :, :], qv[:, tok, :, 0:16],
                                       tabq[:, tok, 0:1, :].broadcast_to([P, 8, 16]), ALU.mult))
                dve.tensor_tensor(rtb[:, :, 0:8], qv[:, tok, :, 8:16],
                                  tabq[:, tok, 1:2, 0:8].broadcast_to([P, 8, 8]), ALU.mult)
                own5(dve.tensor_tensor(rtb[:, :, 8:16], qv[:, tok, :, 0:8],
                                       tabq[:, tok, 1:2, 8:16].broadcast_to([P, 8, 8]), ALU.mult))
                own5(dve.tensor_tensor(qv[:, tok, :, 0:16], rta[:, :, :], rtb[:, :, :], ALU.add))

            def gb(j):
                for tok in range(2):
                    dve.wait_ge(sem("gb_ready"), j * 2 + tok + 1)
                    dve.scalar_tensor_tensor(out=gb2[:, tok, :], in0=gb1[:, tok, :], scalar=1.0, in1=ps[:, tok, :],
                                             op0=ALU.add, op1=ALU.mult).then_inc(sem("pair_read"), 1)
                dve.wait_ge(sem("pair_read"), j * 2 + 10)
                dve.tensor_tensor(gb2[:, :, :], gb2[:, :, :], ob[:, j, :, :], ALU.mult).then_inc(sem("gb_prod"), 1)

            def ob_lo(j):
                dve.wait_ge(sem("obh_ready"), j + 1)
                for tok in range(2):
                    ins = dve.scalar_tensor_tensor(
                        out=obl[:, 4 * j:4 * j + 4, tok * P:tok * P + P],
                        in0=ps[:, 5 + tok, :].rearrange("p (k q) -> p k q", q=P), scalar=0.5,
                        in1=obh[:, 4 * j:4 * j + 4, tok * P:tok * P + P].bitcast(F32), op0=ALU.mult, op1=ALU.subtract)
                ins.then_inc(sem("obl_ready"), 1)

            for t in range(72):
                quad_dve(t)
                n = t // 8 - 1
                if n >= 0 and n < 4 and t % 8 in (4, 5):
                    tok = t % 8 - 4
                    dve.wait_ge(sem("pair_read"), n * 2 + tok + 1)
                    rope_q(n, tok)
                if n >= 4 and t % 8 == 4:
                    gb(n - 4)
                if t - 4 in O_TURN_AT:
                    ob_lo(O_TURN_AT.index(t - 4))
                lo(*at(G_B, t))
            for j in range(1, 4):
                for r in range(8):
                    if r == 3:
                        dve.wait_ge(unit_used, units_before(G_BOUT + j))
                        residual(j - 1, (j - 1) % 2, None, "resid_b", 0)
                    lo(G_BOUT + j, r)
            dve.wait_ge(unit_used, units_before(G_BOUT + 4))
            residual(3, 1, None, "resid_b", 0)
            dve.wait_ge(sem("rs"), RS_AT["z"])
            dve.wait_ge(sem("bcast_loaded"), 32)
            for b in range(2):
                dve.scalar_tensor_tensor(out=h[:, b, :], in0=h[:, b, :], scalar=st[:, 60 + b:61 + b], in1=bcast[:, :],
                                         op0=ALU.mult, op1=ALU.mult).then_inc(sem("result_ready"), 1)

        @block.tensor
        def _(pe):
            def tok_unit(G, r, xh, xl, k0, bank, first, last, chunk=None):
                pe.wait_ge(lo_ready, units_before(G) + (r + 1))
                for tok in range(2):
                    if first and chunk:
                        pe.wait_ge(sem("pair_read"), chunk * 2 + tok - 1)
                    for i in range(2):
                        xs = [x[:, k0 + i, tok * P:tok * P + P] for x in (xh, xl)]
                        for n, (x, w) in enumerate(((0, whi), (0, wlo), (1, whi))):
                            mm = pe.matmul(ps[:, bank + tok, :], xs[x], w[:, r % 4, i, :],
                                           start=first and i == 0 and n == 0, stop=last and i == 1 and n == 2)
                    if last and tok == 0 and chunk is not None:
                        mm.then_inc(sem("pair_done"), 1)
                mm.then_inc(unit_used, 1)

            def chan_unit(G, r, xh, xl, n_tok, bank, first, last, chunk=None, counted=False):
                pe.wait_ge(lo_ready, units_before(G) + (r + 1))
                for c in range(4):
                    if first and chunk is not None:
                        pe.wait_ge(sem("bank_read"), chunk * 4 + (c - 3))
                    for i in range(2):
                        ws = [w[:, r % 4, i, c * P:c * P + P] for w in (whi, wlo)]
                        for n, (w, x) in enumerate(((0, xh), (0, xl), (1, xh))):
                            mm = pe.matmul(ps[:, bank + c, 0:n_tok], ws[w], x[:, 2 * r + i, 0:n_tok],
                                           start=first and i == 0 and n == 0, stop=last and i == 1 and n == 2)
                    if last and c < 3 and counted:
                        mm.then_inc(bank_done, 1)
                mm.then_inc(unit_used, 1)

            def turned_norm(name, srcs, n, xnl):
                pe.wait_ge(sem("dg"), DG_AT[name])
                for k in range(KT):
                    if k >= 4:
                        pe.wait_ge(sem("ntmp"), TILES0[xnl] + k - 3)
                    for i, (src, c0, w, d) in enumerate(srcs):
                        mm = pe.matmul(ps[:, 4 + k % 4, c0:c0 + w], src[0:w, k * P:k * P + P], dg[0:w, d, 0:w],
                                       start=True, stop=True)
                    mm.then_inc(sem("nt"), 1)

            def column(slot, bank, c0):
                for b in range(KT):
                    mm = pe.matmul(ps[:, bank, c0 + b:c0 + b + 1], acc[:, slot, b * P:b * P + P], ones[:, 0:1],
                                   start=True, stop=True)
                mm.then_inc(sem("mred"), 1)

            def row_all(slot, done):
                for n in range(4):
                    pe.matmul(ps[:, 4 + n, :], ones[:, :], acc[:, slot, n * 512:n * 512 + 512],
                              start=True, stop=True).then_inc(sem(done), 1)

            pe.wait_ge(sem("const_ready"), 3)
            pe.wait_ge(sem("rows_loaded"), 16 * 8)
            pe.transpose(ps[:, 0, 0:96], rows[0:96, 0, :], ident[0:96, 0:96])
            pe.transpose(ps[:, 0, 96:114], rows[0:18, 1, :], ident[0:18, 0:18]).then_inc(sem("cols_turned"), 1)
            pe.wait_ge(ada_used, 16)
            column(0, 1, 0)
            pe.wait_ge(ada_used, 32)
            column(1, 1, 16)
            turned_norm("n1", [(h[:, 0], 0, P, 0), (h[:, 1], P, P, 1)], T, "n1")

            def v_chunk(c, par, first=False):
                if not first:
                    pe.wait_ge(sem("v_ready"), c * 2 - 2)
                for r in range(8):
                    if first and par == 0:
                        pe.wait_ge(sem("nl"), TILES0["n1"] + 2 * r + 2)
                    tok_unit(G_IN + c, r, xth, xtl, 2 * r, 2 * par, r == 0, r == 7)

            v_chunk(0, 0, True)
            v_chunk(1, 1, True)
            with pe.Fori(1, 4) as i:
                v_chunk(i * 2, 0)
                v_chunk(i * 2 + 1, 1)

            def mix(c):
                pe.wait_ge(sem("wsc_ready"), c * 2 + 2)
                pe.wait_ge(sem("v_ready"), 16)
                for tok in range(2):
                    for g in range(2):
                        mm = pe.matmul(ps[:, 4 + tok, g * 256:g * 256 + 256], wsc[:, tok, g, :],
                                       v[:, bass.ds(c, 1), tok, g * 256:g * 256 + 256].rearrange("p o n -> p (o n)"),
                                       start=True, stop=True)
                    mm.then_inc(sem("mixed"), 1)

            def us_turn(c):
                for tok in range(2):
                    pe.wait_ge(sem("us_done"), c * 2 + (tok + 1))
                    for k in range(4):
                        mm = pe.transpose(ps[:, 6 + tok, k * P:k * P + P], us[:, tok, k * P:k * P + P], ident[:, :])
                    mm.then_inc(sem("us_turned"), 1)

            def u_chunk(c, par, first=False):
                if first:
                    pe.wait_ge(sem("v_ready"), 14)
                    pe.wait_ge(ada_step, 32)
                    row_all(0, "m2_spread")
                else:
                    pe.wait_ge(sem("u_ready"), c * 2 - 2)
                for r in range(8):
                    if r == 1:
                        pe.wait_ge(sem("ws_loaded"), c * 16 + 16)
                        if first:
                            pe.wait_ge(sem("m2b_ready"), 4)
                        else:
                            pe.wait_ge(sem("usl_ready"), c * 2 - 2)
                        for g in range(2):
                            mm = pe.transpose(ps[:, 6, g * P:g * P + P], wsr[:, g, :], ident[:, :])
                        mm.then_inc(sem("ws_turned"), 1)
                    if r == 4 and not first:
                        pe.wait_ge(sem("wsc_ready"), c * 2 + 2)
                        us_turn(c - 1)
                    if r == 5:
                        mix(c)
                    tok_unit(G_IN + 8 + c, r, xth, xtl, 2 * r, 2 * par, r == 0, r == 7)

            u_chunk(0, 0, True)
            pe.wait_ge(sem("v_ready"), 16)
            u_chunk(1, 1)
            with pe.Fori(1, 4) as i:
                u_chunk(i * 2, 0)
                u_chunk(i * 2 + 1, 1)

            for n in range(4):
                if n == 0:
                    pe.wait_ge(sem("u_ready"), 14)
                elif n == 1:
                    pe.wait_ge(sem("u_ready"), 16)
                else:
                    pe.wait_ge(sem("resid"), 2 * n - 2)
                for t in range(16):
                    if n == 0 and t == 4:
                        pe.wait_ge(sem("wsc_ready"), 16)
                        us_turn(7)
                    if n == 0 and t == 8:
                        pe.wait_ge(ada_step, 64)
                        column(1, 4, 0)
                    if n == 0 and t % 2 == 0:
                        pe.wait_ge(sem("usl_ready"), t + 2)
                    tok_unit(*at(G_OUT, 16 * n + t), ush, usl, 2 * t, 2 * (n % 2), t == 0, t == 15)

            pe.wait_ge(sem("crow_loaded"), 64)
            for i in range(4):
                mm = pe.transpose(ps[:, 0, 88 * i:88 * i + 88], crow[:, i, :], ident[0:88, 0:88])
            mm.then_inc(sem("conv_turned"), 1)
            pe.wait_ge(ada_step, 96)
            column(1, 1, 0)
            turned_norm("n2", [(h[:, 0], 0, P, 0), (h[:, 1], P, P, 1)], T, "n2")
            pe.wait_ge(sem("cw_ready"), 1)
            for p, ((f0, nf), (gu, gd)) in enumerate(zip(FPARTS, G_FFN)):
                def pair(f, first=False):
                    F = f + f0
                    if first:
                        if p == 0:
                            pe.wait_ge(sem("gain_n2"), 1)
                        else:
                            pe.wait_ge(sem("resid_f"), 8 * p)
                    else:
                        pe.wait_ge(sem("yg_done"), F)
                    for r in range(8):
                        if first and p == 0:
                            pe.wait_ge(sem("nl"), TILES0["n2"] + 2 * r + 2)
                        chan_unit(gu + f * 2, r, xth, xtl, T, 0, r == 0, r == 7)
                    if first and p == 0:
                        pass
                    elif first and p == 1:
                        pe.wait_ge(sem("m5b_ready"), 4)
                        pe.wait_ge(sem("yv_done"), F)
                    else:
                        pe.wait_ge(sem("yv_done"), F)
                    for r in range(8):
                        chan_unit(gu + f * 2 + 1, r, xth, xtl, T, 4, r == 0, r == 7)

                pair(0, True)
                with pe.Fori(1, nf) as f:
                    pair(f)
                for t in range(8 * nf):
                    n, r = t // (2 * nf), t % (2 * nf)
                    if r == 0 and n < 2:
                        pe.wait_ge(sem("yg_done"), f0 + nf)
                    elif r == 0:
                        pe.wait_ge(sem("resid_f"), 8 * p + 2 * n - 2)
                    if p == 0 and t == 6:
                        pe.wait_ge(sem("yv_done"), nf)
                        pe.wait_ge(ada_step, 128)
                        row_all(0, "m5_spread")
                    if n == 0 and r % 2 == 0:
                        pe.wait_ge(sem("htl_ready"), f0 + r // 2 + 1)
                    tok_unit(*at(gd, t), hth, htl, 2 * r, 2 * (n % 2), r == 0, r == 2 * nf - 1)

            pe.wait_ge(sem("x2_ready"), 2)
            pe.wait_ge(sem("meta_loaded"), 16)
            turned_norm("a", [(h[:, 0], 0, P, 0), (hm[:, :], P, NM, 1), (h[:, 1], P + NM, P, 2)], L, "a")
            pe.wait_ge(sem("nlam"), 1)
            pe.wait_ge(sem("nl"), TILES0["a"] + 13)
            pe.matmul(ps[:, 4, 0:1], ones[0:1, :], st[0:1, 119:120], start=True, stop=True).then_inc(sem("nlam_ps"), 1)
            pe.wait_ge(sem("nl"), TILES0["a"] + 16)
            pe.wait_ge(sem("tabA_loaded"), 32)

            def item_pe(t, j, items=True, before=True):
                for i, back in due(t, 2, items, before):
                    it, b = (j - back) * 6 + i, i % 3
                    pe.wait_ge(sem("a_w"), it + 1)
                    for kb in ITEM_BLOCKS[b]:
                        kc, w = BLK[kb]
                        k0 = ITEM_KEYS[b][0]
                        mm = pe.transpose(ps[0:w, 6, kb * P:kb * P + P], wd[:, kc - k0:kc - k0 + w], ident[:, :])
                    mm.then_inc(sem("a_wturned"), 1)
                for i, back in due(t, 5, items, before):
                    pe.wait_ge(sem("a_on"), (j - back) * 6 + (i + 1))
                    for d in range(2):
                        mm = pe.transpose(ps[:, 7, 256 + d * P:256 + d * P + P], on[:, d * P:d * P + P], ident[:, :])
                    mm.then_inc(sem("a_oturned"), 1)
                for i, back in due(t, 3, items, before):
                    it, blocks = (j - back) * 6 + i, ITEM_BLOCKS[i % 3]
                    if not isinstance(it, int) or it:
                        pe.wait_ge(sem("a_ot"), it * 2)
                    pe.wait_ge(sem("a_wt"), it + 1)
                    for kb in blocks:
                        w = BLK[kb][1]
                        mm = pe.matmul(ps[:, 7, 0:256], wt[0:w, kb, :], vx[0:w, kb, i // 3 * 256:i // 3 * 256 + 256],
                                       start=kb == blocks[0], stop=kb == blocks[-1])
                    mm.then_inc(sem("a_pv"), 1)
                if items and t == 1:
                    pe.wait_ge(sem("bank_read"), j * 12)
                    pe.wait_ge(sem("rope_read"), j * 4)
                    for b, (c0, w) in enumerate(BLK):
                        for i in range(4):
                            mm = pe.transpose(ps[0:w, 4 + b, i * P:i * P + P], qs[:, i, c0:c0 + w], ident[:, :])
                    mm.then_inc(sem("v_turned"), 1)
                for i, back in due(t, 0, items, before):
                    c0, pair, (k0, nk) = BLK[i % 3][0], i // 3, ITEM_KEYS[i % 3]
                    if i == 0:
                        pe.wait_ge(sem("qk_moved"), j * 2)
                        pe.wait_ge(sem("vx_ready"), j)
                    for q in range(4):
                        if t > ROPE_AT[q] and ITEM_AT[i - 1] <= ROPE_AT[q] and rotates(j):
                            pe.wait_ge(sem("rope_read"), j * 4 + (q + 1))
                    for e in range(2):
                        mm = pe.matmul(ps[:, 4 + e, 0:nk], qt[:, 2 * pair + e, c0:c0 + P],
                                       kt_[:, 2 * pair + e, k0:k0 + nk], start=True, stop=True)
                    mm.then_inc(sem("a_scores"), 1)

            def rotates(j):
                return not isinstance(j, int) or j < 4

            def swap_halves(j, q):
                pe.wait_ge(sem("bank_read"), j * 12 + 4 * (q // 2 + 1))
                if not isinstance(j, int) or j * 4 + q:
                    pe.wait_ge(sem("rope_read"), j * 4 + q)
                for i in range(2):
                    mm = pe.matmul(ps[:, 4 + i, 0:L], rotA[:, :], (qs, ks)[q // 2][0:32, q % 2 * 2 + i, :],
                                   start=True, stop=True)
                mm.then_inc(sem("rot"), 1)

            def heads(j, items=True, before=True):
                for t in range(24):
                    item_pe(t, j, items, before)
                    if t in ROPE_AT:
                        swap_halves(j, ROPE_AT.index(t))
                    chunk = None if isinstance(j, int) and j * 3 + t // 8 == 0 else j * 3 + t // 8
                    chan_unit(*at(G_A + j * 3, t), xmh, xml, L, 0, t % 8 == 0, t % 8 == 7, chunk, True)

            pe.wait_ge(sem("resid_f"), 24)
            heads(0, False, False)
            heads(1, True, False)
            with pe.Fori(2, 4) as j:
                heads(j)

            for t in range(40):
                if t < 24:
                    item_pe(t, 4)
                else:
                    item_pe(t - 24, 5, items=False)
                if t < 32:
                    chan_unit(*at(G_GATE, t), xmh, xml, L, 0, t % 8 == 0, t % 8 == 7, 12 + t // 8, True)
                else:
                    if t % 2 == 0:
                        pe.wait_ge(sem("g_done"), (t - 32) // 2 + 1)
                    chan_unit(*at(G_GATE, t), oth, otl, L, 0, t % 8 == 0, t % 8 == 7, 12 + t // 8, True)

            def y_turn(j):
                if not isinstance(j, int) or j:
                    pe.wait_ge(sem("y_added"), j * 3)
                pe.wait_ge(sem("bank_read"), j * 4 + 68)
                for b, (c0, w) in enumerate(BLK):
                    for i in range(4):
                        mm = pe.transpose(ps[0:w, 4 + b, i * P:i * P + P], yt[:, i, c0:c0 + w], ident[:, :])
                mm.then_inc(sem("y_turned"), 1)

            def out_chunk(j):
                for r in range(8):
                    if r == 3:
                        y_turn(j - 1)
                    chan_unit(G_AOUT + j, r, oth, otl, L, 0, r == 0, r == 7, j + 16, True)

            out_chunk(1)
            with pe.Fori(2, 4) as j:
                out_chunk(j)
            y_turn(3)

            pe.wait_ge(sem("y_added"), 12)
            turned_norm("b", [(h[:, 0], 0, P, 0), (hm[:, :], P, NM, 1), (h[:, 1], P + NM, P, 2)], L, "b")
            pe.wait_ge(sem("nl"), TILES0["b"] + 16)
            turned_norm("b", [(h[:, 0], 0, P, 0), (h[:, 1], P, P, 2)], T, "b2")
            for r in range(8):
                chan_unit(G_KV, r, xmh, xml, L, 0, r == 0, r == 7)
            pe.wait_ge(sem("kk_raw"), 1)
            pe.wait_ge(sem("tabB_loaded"), 32)
            pe.wait_ge(sem("nl"), TILES0["b2"] + 16)
            for i in range(2):
                mm = pe.matmul(ps[:, 4 + i, 0:L], rotB[:, :], kk[:, i, :], start=True, stop=True)
            mm.then_inc(sem("rotb"), 1)
            for b, (c0, w) in enumerate(BLK):
                bank, col = ((6, 0), (6, 256), (7, 0))[b]
                for i in range(2):
                    mm = pe.transpose(ps[0:w, bank, col + i * P:col + i * P + P], kk[:, 2 + i, c0:c0 + w], ident[:, :])
            mm.then_inc(sem("vb_turned"), 1)
            pe.wait_ge(sem("vb_ready"), 1)
            pe.wait_ge(sem("kd_ready"), 64)

            def quad_pe(t):
                for n in quads(t, 2):
                    tok = n // 2 % 2
                    if n:
                        pe.wait_ge(sem("b_o"), n)
                    pe.wait_ge(sem("b_exp"), n * 4 + 4)
                    for kb in range(2 + tok):
                        kc, w = BLK[kb]
                        for i in range(4):
                            mm = pe.transpose(ps[0:w, TURN_BANK[kb], i * P:i * P + P], eb_[:, i, kc:kc + w], ident[:, :])
                    mm.then_inc(sem("b_wturned"), 1)
                for n in quads(t, 3):
                    j, tok = n // 4, n // 2 % 2
                    pe.wait_ge(sem("b_wt"), n + 1)
                    for i in range(4):
                        for kb in range(2 + tok):
                            w = BLK[kb][1]
                            mm = pe.matmul(ps[:, 2, i * BH:i * BH + BH], wtb[0:w, kb, i, :],
                                           vb[0:w, kb, j * BH:j * BH + BH], start=kb == 0, stop=kb == 1 + tok)
                    mm.then_inc(sem("b_pv"), 1)
                for n in quads(t, 0):
                    j, tok, half = n // 4, n // 2 % 2, n % 2
                    nk = (144, L)[tok]
                    pe.wait_ge(sem("qtb_ready"), len([x for x in Q_TURN_AT if x < t]))
                    if t > O_TURN_AT[0]:
                        pe.wait_ge(sem("obl_ready"), len([x for x in O_TURN_AT if x < t]))
                    for i in range(4):
                        p0 = 64 * (i % 2)
                        mm = pe.matmul(ps[:, 4 + i, 0:nk], qtb[p0:p0 + 64, j, 2 * half + i // 2, tok * P:tok * P + P],
                                       kd[p0:p0 + 64, j, 0:nk], start=True, stop=True)
                    mm.then_inc(sem("b_scores"), 1)

            def turn(src, done):
                for tok in range(2):
                    for i in range(4):
                        mm = pe.transpose(ps[:, 5 + tok, i * P:i * P + P], src[:, tok, i * P:i * P + P], ident[:, :])
                mm.then_inc(sem(done), 1)

            for t in range(72):
                quad_pe(t)
                if t in Q_TURN_AT:
                    pe.wait_ge(sem("qrope_own"), Q_TURN_AT.index(t) * 6 + 6)
                    turn(qx, "q_turned")
                if t in O_TURN_AT:
                    pe.wait_ge(sem("gb_prod"), O_TURN_AT.index(t) + 1)
                    turn(gb2, "ob_turned")
                if t < 64:
                    tok_unit(*at(G_B, t), bxh, bxl, 2 * (t % 8), 0, t % 8 == 0, t % 8 == 7, t // 8)
                else:
                    if t % 2 == 0:
                        pe.wait_ge(sem("obl_ready"), t % 8 // 2 + 1)
                    tok_unit(*at(G_B, t), obh, obl, 2 * (t % 8), 0, t % 8 == 0, t % 8 == 7, t // 8)
            for j in range(1, 4):
                if j > 1:
                    pe.wait_ge(sem("resid_b"), 2 * j - 2)
                for r in range(8):
                    tok_unit(G_BOUT + j, r, obh, obl, 2 * r, 2 * (j % 2), r == 0, r == 7)


USED = ("x", "c", "ada_w", "ada_b", "norm_g", "ffn_w_up", "ffn_conv_w", "ffn_conv_b", "ffn_w_down", "a_w_in",
        "a_g_v", "a_w_s", "a_b_s", "a_w_out", "final_g", "meta_tokens_2", "a_norm_2", "a_w_in_2", "a_w_out_2",
        "a_lambda_q1_2", "a_lambda_k1_2", "a_lambda_q2_2", "a_lambda_k2_2", "a_subln_2", "kv_norm_2", "w_kv_2",
        "b_norm_2", "b_w_in_2", "b_w_out_2", "b_sinks_2", "final_norm_2")


def rope_constants():
    import numpy as np

    pos = np.concatenate([NM + np.arange(P), np.arange(NM), NM + P + np.arange(P)])
    out = {}

    def angles(rot):
        inv = (500000.0 ** (-np.arange(0, rot, 2, dtype=np.float32) / rot)).astype(np.float32)
        return pos.astype(np.float32)[None, :] * inv[:, None]

    ang = angles(AH // 4)
    half = AH // 8
    out["tab_a"] = np.stack([np.concatenate([np.cos(ang)] * 2), np.concatenate([-np.sin(ang), np.sin(ang)])], 1)
    out["rot_a"] = np.pad(np.roll(np.eye(2 * half), half, 1), ((0, 0), (0, P - 2 * half)))
    ang = angles(BH // 4)
    half = BH // 8
    tab = np.zeros((P, 2, L))
    tab[:, 0] = 1.0
    rot = np.zeros((P, P))
    for h0 in (0, BH):
        tab[h0:h0 + 2 * half, 0] = np.concatenate([np.cos(ang)] * 2)
        tab[h0:h0 + 2 * half, 1] = np.concatenate([-np.sin(ang), np.sin(ang)])
        rot[h0:h0 + 2 * half, h0:h0 + 2 * half] = np.roll(np.eye(2 * half), half, 1)
    out["tab_b"], out["rot_b"] = tab, rot
    tabq = np.zeros((P, 2, 2, 2 * half))
    for i, b in enumerate(XB):
        c0 = BLK[b][0]
        tabq[:, i] = tab[0:2 * half, :, c0:c0 + P].transpose(2, 1, 0)
    out["tab_q"] = tabq
    return {k: np.ascontiguousarray(x.astype(np.float32)) for k, x in out.items()}


def kernel(**inputs):
    import numpy as np
    import concourse.bacc as bacc
    from concourse.bass_utils import run_bass_kernel_spmd

    nc = bacc.Bacc("TRN2", target_bir_lowering=False, num_devices=1)
    arrays, aps = {}, {}
    for name, x in [(n, inputs[n]) for n in USED] + list(rope_constants().items()):
        x = np.ascontiguousarray(x)
        arrays[f"in_{name}"] = x
        aps[name] = nc.dram_tensor(f"in_{name}", x.shape, mybir.dt.from_np(x.dtype), kind="ExternalInput").ap()
    out = nc.dram_tensor("out", (1, T, D), F32, kind="ExternalOutput").ap()
    program(nc, aps, out)
    r = run_bass_kernel_spmd(nc, [arrays], core_ids=[0])
    return r.results[0]["out"]
```

```python
from contextlib import ExitStack

import concourse.bass as bass
from concourse import mybir

F32 = mybir.dt.float32
F32R = mybir.dt.float32r
ALU = mybir.AluOpType
ACT = mybir.ActivationFunctionType
AX = mybir.AxisListType

P = 128
D = 2048
T = 256
NM = 16
L = T + NM
KT = D // P
EPS1, EPS2 = 1e-6, 1e-5
GW = 2 * D
FF = 5632
NF = FF // 512
FPARTS = ((0, 4), (4, 4), (8, 3))
AH = 128
BH = 64
NEG = -1e30
BLK = ((0, 128), (128, 16), (144, 128))
XB = (0, 2)
ITEM_KEYS = ((0, 144), (P, 16), (0, L))
ITEM_BLOCKS = ((0, 1), (1,), (0, 1, 2))

G_IN = 8
G_OUT = G_IN + 16
G_FFN = []
_g = G_OUT + 8
for _f0, _nf in FPARTS:
    G_FFN.append((_g, _g + 2 * _nf))
    _g += 3 * _nf
G_A = _g
G_GATE = G_A + 12
G_AOUT = G_GATE + 4
G_KV = G_AOUT + 4
G_B = G_KV + 1
G_BG = G_B + 4
G_BOUT = G_BG + 4
ITEMS = 24
ITEM_AT = (3, 7, 10, 14, 17, 21)
ROPE_AT = (9, 13, 16, 20)

QUAD_AT = tuple(12 + 3 * n for n in range(16))
Q_TURN_AT = (10, 20, 29, 38)
O_TURN_AT = (44, 53, 59, 66)
TURN_BANK = (2, 3, 4)


def quads(t, step):
    return [n for n, a in enumerate(QUAD_AT) if a + step == t]


def due(t, step, items=True, before=True):
    out = []
    for i, a in enumerate(ITEM_AT):
        if items and a + step == t:
            out.append((i, 1))
        if before and a + step == t + 24:
            out.append((i, 2))
    return out

KB = 1024
BASE = 16512
O_RAW, O_HI, O_LO = BASE, BASE + 32 * KB, BASE + 48 * KB
O_XT = BASE + 64 * KB
O_V = BASE + 98 * KB
O_W = BASE + 130 * KB
O_ACC = BASE + 164 * KB
O_H = BASE + 180 * KB
O_ADA = BASE + 196 * KB
O_S = BASE + 204 * KB


def at(G, t):
    return G + t // 8, t % 8


TILES0 = {"n1": 0, "n2": 16, "a": 32, "b": 48}
RS_AT = {"n1": 1, "v": 2, "n2": 3, "f": 4, "a": 5, "b": 6, "z": 7}
PART_AT = {"n2": 0, "f": 8, "b": 24, "z": 36}
DG_AT = {"n1": 1, "n2": 2, "a": 3, "b": 4}


def tiles_at(t, first):
    return range(6) if t == first else range(2 * t - 4, 2 * t - 2) if 4 < t < 10 else ()


class Own:

    def __init__(self, eng, sem, base=0):
        self.eng, self.sem, self.base, self.n = eng, sem, base, 0

    def __call__(self, ins):
        self.n += 1
        ins.then_inc(self.sem, 1)
        self.eng.wait_ge(self.sem, self.base + self.n)


def units_before(G):
    return 8 * G - 64


def program(nc, a, out):
    with ExitStack() as ctx:
        sems = {}

        def sem(name):
            if name not in sems:
                sems[name] = ctx.enter_context(nc.semaphore(name))
            return sems[name]

        def place(name, shape, off, dt=F32):
            return nc.alloc_sbuf_tensor_at(name, shape, dt, offset=off)

        raw = place("raw", [P, 4, 2, 2, 512], O_RAW)
        rawv = place("rawv", [P, 4, D], O_RAW)
        whi = place("whi", [P, 4, 2, 512], O_HI, F32R)
        wlo = place("wlo", [P, 4, 2, 512], O_LO, F32R)
        xth = place("xth", [P, KT, T], O_XT, F32R)
        xtl = place("xtl", [P, KT, T], O_XT + 17408, F32R)
        xmh = place("xmh", [P, KT, L], O_XT, F32R)
        xml = place("xml", [P, KT, L], O_XT + 17408, F32R)
        v = place("v", [P, 8, 2, 512], O_V)
        ush = place("ush", [P, 32, T], O_V, F32R)
        usl = place("usl", [P, 32, T], O_W, F32R)
        ut = place("ut", [P, 2, 512], O_H)
        us = place("us", [P, 2, 512], O_H + 4 * KB)
        utmp = place("utmp", [P, 512], O_H + 8 * KB)
        gvb = place("gvb", [P, 512], O_H + 10 * KB)
        wsr = place("wsr", [P, 2, 128], O_H + 12 * KB)
        wsc = place("wsc", [P, 2, 2, 128], O_H + 13 * KB)
        acc = place("acc", [P, 2, D], O_ACC)
        ada = place("ada", [P, 2, 1024], O_ADA)
        h = place("h", [P, 2, D], O_H)
        hth = place("hth", [P, 16, T], O_V, F32R)
        htl = place("htl", [P, 16, T], O_V + 16 * KB, F32R)
        cw = place("cw", [P, 4, 88], O_W + 16 * KB)
        gy1 = place("gy1", [P, 2, 512], O_XT)
        gy2 = place("gy2", [P, 2, 512], O_W + 18 * KB)
        yg = place("yg", [P, 4, T], O_W)
        sg = place("sg", [P, 4, T], O_W + 4 * KB)
        yv = place("yv", [P, 4, T], O_W + 8 * KB)
        hs = place("hs", [P, 4, T], O_W + 12 * KB)
        ntmp = place("ntmp", [P, 2, L], O_V + 16 * KB)
        dg = place("dg", [P, 3, P], O_V + 21 * KB)
        junk = place("junk", [P, D], O_V + 24 * KB)
        bcast = place("bcast", [P, D], O_W + 24 * KB)
        hm = place("hm", [P, D], O_ACC + 8 * KB)
        oth = place("oth", [P, KT, L], O_W, F32R)
        otl = place("otl", [P, KT, L], O_W + 17408, F32R)
        ot = place("ot", [P, KT, L], O_W)
        qt = place("qt", [P, 4, L], O_V)
        kt_ = place("kt_", [P, 4, L], O_V + 4352)
        qs = place("qs", [P, 4, L], O_V + 2 * 4352)
        ks = place("ks", [P, 4, L], O_ACC)
        vx = place("vx", [P, 3, 512], O_V + 3 * 4352)
        sc = place("sc", [P, 2, L], O_V + 19200)
        ex = place("ex", [P, 2, L], O_V + 21376)
        wd = place("wd", [P, L], O_V + 23552)
        wt = place("wt", [P, 3, P], O_V + 24640)
        on = place("on", [P, 256], O_V + 26176)
        ojunk = place("ojunk", [P, 256], O_V + 27200)
        tabA = place("tabA", [32, 2, L], O_V + 28224)
        lamv = place("lamv", [1, 5, P], O_V + 30400)
        maskA = place("maskA", [P, 2, L], O_ACC + 4352)
        rt2 = place("rt2", [32, 2, L], O_ADA)
        rotA = place("rotA", [32, P], O_ADA + 4352)
        gth = place("gth", [P, 4, L], O_V + 8704)
        g2 = place("g2", [P, 4, L], O_ACC)
        yt = place("yt", [P, 4, L], O_V)
        bxh = place("bxh", [P, KT, T], O_W, F32R)
        bxl = place("bxl", [P, KT, T], O_W + 17408, F32R)
        obh = place("obh", [P, KT, T], O_XT, F32R)
        obl = place("obl", [P, KT, T], O_XT + 17408, F32R)
        ob = place("ob", [P, 4, 2, 512], O_XT)
        kk = place("kk", [P, 4, L], O_V)
        kt1 = place("kt1", [P, 2, L], O_V + 4352)
        kt2 = place("kt2", [P, 2, L], O_V + 6528)
        tabB = place("tabB", [P, 2, L], O_V + 8704)
        rotB = place("rotB", [P, P], O_V + 10880)
        kd = place("kd", [P, 4, L], O_ACC)
        vb = place("vb", [P, 3, 256], O_ACC + 4352)
        maskB = place("maskB", [P, 2, L], O_ADA + 5 * KB)
        sinkb = place("sinkb", [P, 32], O_ACC + 7424)
        tabq = place("tabq", [P, 2, 2, 16], O_ACC + 7552)
        qx = place("qx", [P, 2, 512], O_V)
        qtb = place("qtb", [P, 4, 4, T], O_XT + 17408)
        sb_ = place("sb_", [P, 4, L], O_V + 8 * KB)
        eb_ = place("eb_", [P, 4, L], O_V + 8 * KB + 4352)
        wtb = place("wtb", [P, 3, 4, P], O_V + 17 * KB)
        rta = place("rta", [P, 8, 16], O_V + 23 * KB)
        rtb = place("rtb", [P, 8, 16], O_V + 23 * KB + 512)
        gb1 = place("gb1", [P, 2, 512], O_V + 24 * KB)
        gb2 = place("gb2", [P, 2, 512], O_V + 28 * KB)
        ident = place("ident", [P, P], O_S)
        ones = place("ones", [P, P], O_S + 512)
        cols = place("cols", [P, 114], O_S + 1024)
        mcol = place("mcol", [P, 4, KT], O_S + 1536)
        acol = place("acol", [P, KT], O_S + 1792)
        ccol = place("ccol", [P, KT], O_S + 1856)
        st = place("st", [P, 160], O_S + 1920)
        neghalf = place("neghalf", [P, 8], O_S + 2560)
        rows = place("rows", [96, 6, P], O_V)
        crow = place("crow", [88, 4, P], O_V)
        crows = place("crows", [16, P], O_V + 3 * KB)
        brow = place("brow", [1, 2, D], O_W)
        ps = ctx.enter_context(nc.psum_tensor("ps", [P, 8, 512], F32))
        C_C, C_G0, C_G1, C_AN, C_KVN, C_BN = (slice(16 * i, 16 * i + 16) for i in range(6))
        C_BS, C_SUB = 96, 112

        ld = [sem(f"slab{i}_loaded") for i in range(4)]
        ada_used = sem("ada01_used")
        hi_ready, lo_ready, unit_used = sem("hi_ready"), sem("lo_ready"), sem("unit_used")
        al = [sem(f"ada{i}_loaded") for i in range(2)]
        ada_step = sem("ada_step")
        bank_done = sem("bank_done")

        w_in, w_out = a["a_w_in"][0], a["a_w_out"][0]
        w_up, w_down = a["ffn_w_up"][0], a["ffn_w_down"][0]
        w_a, w_ao = a["a_w_in_2"][0], a["a_w_out_2"][0]
        w_kv, w_b, w_bo = a["w_kv_2"], a["b_w_in_2"][0], a["b_w_out_2"][0]
        ada_w, ada_b = a["ada_w"][0], a["ada_b"]
        tiles = lambda w: w.rearrange("(s k p) n -> s p k n", k=4, p=P)

        block = ctx.enter_context(nc.Block())

        @block.sync
        def _(sp):
            def slab(G, q, w, k, col):
                if isinstance(G, int) and G == G_IN:
                    sp.wait_ge(ada_used, 4 * (G - 1) + q + 1)
                else:
                    sp.wait_ge(lo_ready, units_before(G) - 8 + 2 * q + 2)
                dst = raw[:, q].rearrange("p u k n -> p (u k) n")
                sp.dma_start(dst, tiles(w)[k][:, :, bass.ds(col, 512)]).then_inc(ld[q], 16)

            def chunk(G, w, k0, col):
                for q in range(4):
                    slab(G, q, w, k0 + q, col)

            sp.dma_start(crows[:, :], a["c"][0].rearrange("(r q) -> r q", q=P)).then_inc(sem("c_loaded"), 16)
            for j in range(2):
                for i0, loop in (((0, False), (1, True)) if j == 0 else ((0, True),)):
                    def four(i):
                        for q in range(4):
                            if loop:
                                sp.wait_ge(ada_used, 16 * j + 4 * i + q - 3)
                            src = ada_w[bass.ds(i * 512 + q * 128, 128), j * D:(j + 1) * D]
                            sp.dma_start(rawv[:, q], src).then_inc(ld[q], 16)
                    if loop:
                        with sp.Fori(i0, 4) as i:
                            four(i)
                    else:
                        four(i0)
                        sp.dma_start(h[:, :, :], a["x"][0].rearrange("(b p) n -> p b n", p=P)).then_inc(sem("x_loaded"), 16)
            chunk(G_IN, w_in, 0, GW)
            with sp.Fori(1, 8) as c:
                chunk(G_IN + c, w_in, 0, c * 512 + GW)
            with sp.Fori(0, 8) as c:
                chunk(G_IN + 8 + c, w_in, 0, c * 512)
            with sp.Fori(0, 4) as n:
                for half in range(2):
                    chunk(G_OUT + 2 * n + half, w_out, 4 * half, n * 512)
            for (f0, nf), (gu, gd) in zip(FPARTS, G_FFN):
                with sp.Fori(0, nf) as f:
                    chunk(gu + 2 * f, w_up, 0, f * 512 + f0 * 512)
                    chunk(gu + 2 * f + 1, w_up, 0, f * 512 + (FF + f0 * 512))
                if nf == 4:
                    with sp.Fori(0, 4) as n:
                        chunk(gd + n, w_down, f0, n * 512)
                else:
                    for s in range(4 * nf):
                        slab(gd + s // 4, s % 4, w_down, f0 + s % nf, s // nf * 512)
            with sp.Fori(0, 4) as j:
                for i in range(3):
                    chunk(G_A + 3 * j + i, w_a, 0, j * 512 + i * D)
            with sp.Fori(0, 4) as j:
                chunk(G_GATE + j, w_a, 0, j * 512 + 3 * D)
            with sp.Fori(0, 4) as j:
                chunk(G_AOUT + j, w_ao, 0, j * 512)
            chunk(G_KV, w_kv, 0, 0)
            with sp.Fori(0, 4) as j:
                chunk(G_B + j, w_b, 0, j * 512)
            with sp.Fori(0, 4) as j:
                chunk(G_BG + j, w_b, 0, j * 512 + D)
            with sp.Fori(0, 4) as j:
                chunk(G_BOUT + j, w_bo, 0, j * 512)
            for b in range(2):
                sp.wait_ge(sem("result_ready"), b + 1)
                sp.dma_start(out[0, b * P:(b + 1) * P, :], h[:, b, :]).then_inc(sem("stored"), 16)
            sp.wait_ge(sem("stored"), 32)

        @block.gpsimd
        def _(pool):
            pool.memset(ident[:, :], 0.0).then_inc(sem("pool_own"), 1)
            pool.memset(ones[:, :], 1.0).then_inc(sem("const_ready"), 1)
            pool.memset(neghalf[:, :], -0.5).then_inc(sem("pool_own"), 1)
            pool.memset(st[:, :], 1.0).then_inc(sem("const_ready"), 1)
            pool.wait_ge(sem("pool_own"), 2)
            pool.affine_select(out=ident[:, :], in_=ident[:, :], compare_op=ALU.not_equal, fill=1.0, base=0,
                               pattern=[[-1, P]], channel_multiplier=1).then_inc(sem("const_ready"), 1)

            def acc_start(j, slot, n):
                pool.memset(acc[:, slot], 0.0).then_inc(sem("acc_zeroed"), 1)
                pool.wait_ge(sem("acc_zeroed"), n + 1)
                if n:
                    pool.wait_ge(sem("acc_started"), 16 * n)
                pool.dma_start(acc[0:1, slot], ada_b[:, j * D:(j + 1) * D]).then_inc(sem("acc_started"), 16)

            def stream_ada(j, k0, start=0, end=KT):
                for first, loop in (((0, False), (1, True)) if k0 == 0 else ((start, True),)):
                    def two(k):
                        for half in range(2):
                            if loop:
                                pool.wait_ge(ada_step, 2 * k + 2 * k0 - 1 + half)
                            src = ada_w[bass.ds(k * P, P), j * D + half * 1024:j * D + half * 1024 + 1024]
                            pool.dma_start(ada[:, half], src).then_inc(al[half], 16)
                    if loop:
                        with pool.Fori(first, end) as k:
                            two(k)
                    else:
                        two(first)

            def rsqrt(name, cin, cout, w, scale, eps, parts=P):
                x, y = st[0:parts, cin:cin + w], st[0:parts, cout:cout + w]
                pool.tensor_scalar(x, x, scale, eps, ALU.mult, ALU.add).then_inc(sem("rs1"), 1)
                pool.wait_ge(sem("rs1"), RS_AT[name] - (RS_AT[name] > RS_AT["a"]))
                pool.tensor_tensor(y, x, neghalf[0:parts, 0:w], ALU.pow).then_inc(sem("rs"), 1)

            pool.wait_ge(sem("ss_n1"), 2)
            rsqrt("n1", 0, 4, 2, 1.0 / D, EPS1)
            pool.wait_ge(sem("mred"), 1)
            acc_start(2, 0, 0)
            stream_ada(2, 0)
            pool.wait_ge(sem("mred"), 2)
            acc_start(3, 1, 1)
            stream_ada(3, 16, 0, 2)
            pool.wait_ge(sem("ssv_ready"), 1)
            rsqrt("v", 8, 12, 2, 1.0 / GW, EPS1)
            stream_ada(3, 16, 2)
            pool.wait_ge(sem("mred"), 3)
            acc_start(4, 1, 2)
            stream_ada(4, 32)
            pool.wait_ge(sem("ss_n2"), 1)
            rsqrt("n2", 16, 20, 2, 1.0 / D, EPS1)
            acc_start(5, 0, 3)
            stream_ada(5, 48)
            pool.wait_ge(sem("ss_f"), 1)
            rsqrt("f", 24, 28, 2, 1.0 / D, EPS1)
            pool.wait_ge(sem("ss_a"), 1)
            pool.wait_ge(sem("meta_squared"), 1)
            pool.wait_ge(sem("rs"), RS_AT["f"])
            own = Own(pool, sem("pool_own"), 2)
            rf = st[:, 28:30]
            own(pool.tensor_tensor(st[:, 44:46], rf, rf, ALU.mult))
            own(pool.tensor_tensor(st[:, 32:34], st[:, 32:34], st[:, 44:46], ALU.mult))
            own(pool.tensor_scalar(st[:, 32:35], st[:, 32:35], 1.0 / D, EPS2, ALU.mult, ALU.add))
            own(pool.tensor_tensor(st[:, 36:39], st[:, 32:35], neghalf[:, 0:3], ALU.pow))
            pool.tensor_tensor(st[:, 40:42], st[:, 36:38], rf, ALU.mult).then_inc(sem("rs"), 1)
            for i in range(ITEMS):
                pool.wait_ge(sem("oss"), i + 1)
                x, y = st[:, 100:101], st[:, 101:102]
                pool.tensor_scalar(x, x, 1.0 / 256, EPS2, ALU.mult, ALU.add).then_inc(sem("ors1"), 1)
                pool.wait_ge(sem("ors1"), i + 1)
                pool.tensor_tensor(y, x, neghalf[:, 0:1], ALU.pow).then_inc(sem("ors"), 1)
            pool.wait_ge(sem("ss_b"), 1)
            rsqrt("b", 48, 52, 3, 1.0 / D, EPS2)
            pool.wait_ge(sem("kk_ready"), 1)
            for e in range(2):
                for half in range(2):
                    pool.dma_start(kd[64 * half:64 * half + 64, e:4:2, :],
                                   kk[64 * e:64 * e + 64, 0:2, :]).then_inc(sem("kd_ready"), 16)
            pool.wait_ge(sem("ss_z"), 1)
            rsqrt("z", 56, 60, 2, 1.0 / D, EPS2)

        @block.scalar
        def _(act):
            def load(dst, src, name):
                act.dma_start(dst, src).then_inc(sem(name), 16)

            def cast(G, r, first=False):
                if r % 2 == 0:
                    act.wait_ge(ld[r // 2], G * 16 + 16)
                if not first:
                    act.wait_ge(unit_used, units_before(G) + (r - 3))
                act.activation(whi[:, r % 4], raw[:, r // 2, r % 2], ACT.Copy).then_inc(hi_ready, 1)

            def sums(name, srcs, cin):
                for b, src in enumerate(srcs):
                    w = src.shape[0]
                    if b:
                        act.wait_ge(sem("ss_" + name), b)
                    act.activation(junk[0:w, :], src, ACT.Square,
                                   accum_out=st[0:w, cin + b:cin + b + 1]).then_inc(sem("ss_" + name), 1)

            def part(name, n, srcs, i, col=64):
                nb = len(srcs)
                for b, src in enumerate(srcs):
                    w = src.shape[0]
                    if isinstance(i, int) and PART_AT[name] + i * nb + b == 0:
                        pass
                    else:
                        act.wait_ge(sem("part"), i * nb + (PART_AT[name] + b))
                    act.activation(ps[0:w, 7:8, :], src[:, bass.ds(n * 512, 512)].rearrange("p (o n) -> p o n", o=1),
                                   ACT.Square, accum_out=st[0:w, bass.ds(n * nb + (col + b), 1)])\
                       .then_inc(sem("part"), 1)

            def spread(name, t, dests, first=4):
                for k in tiles_at(t, first):
                    for e, (n, xh) in enumerate(dests):
                        i = k * len(dests) + e
                        act.wait_ge(sem("ntmp"), TILES0[name] + i + 1)
                        act.activation(xh[:, k, 0:n], ntmp[:, i % 2, 0:n], ACT.Copy).then_inc(sem("nh"), 1)

            act.wait_ge(sem("c_turned"), 1)
            act.activation(ccol[:, :], ps[:, 2, 0:KT], ACT.Silu).then_inc(sem("ccol_ready"), 1)
            load(brow[:, :, :], ada_b[:, 0:2 * D].rearrange("o (j n) -> o j n", n=D), "bias_loaded")
            vecs = (a["c"][0], a["norm_g"][0, 0], a["norm_g"][0, 1], a["a_norm_2"][0], a["kv_norm_2"], a["b_norm_2"][0])
            for i, src in enumerate(vecs):
                load(rows[16 * i:16 * i + 16, 0, :], src.rearrange("(r q) -> r q", q=P), "rows_loaded")
            load(rows[0:16, 1, :], a["a_b_s"][0], "rows_loaded")
            load(rows[16:18, 1, :], a["a_subln_2"][0].rearrange("(r q) -> r q", q=P), "rows_loaded")
            act.wait_ge(sem("x_loaded"), 16)
            act.wait_ge(sem("const_ready"), 3)
            sums("n1", [h[:, 0, :], h[:, 1, :]], 0)

            def v_out(c, par):
                act.wait_ge(unit_used, c * 8 + 8)
                for tok in range(2):
                    act.activation(v[:, bass.ds(c, 1), tok, :], ps[:, 2 * par + tok:2 * par + tok + 1, :],
                                   ACT.Gelu_apprx_tanh).then_inc(sem("v_ready"), 1)
                    act.wait_ge(sem("v_ready"), c * 2 + (tok + 1))
                    act.activation(utmp[:, None, :], v[:, bass.ds(c, 1), tok, :], ACT.Square,
                                   accum_out=st[:, bass.ds(c * 2 + (64 + tok), 1)]).then_inc(sem("ssv"), 1)

            def v_chunk(c, par, first=False):
                for r in range(8):
                    if isinstance(c, int):
                        spread("n1", c * 8 + r, [(T, xth)], 0)
                    if r == 3 and not first:
                        v_out(c - 1, 1 - par)
                    cast(G_IN + c, r, first and r < 4)

            def ws_load(c):
                load(wsr[:, :, :], a["a_w_s"][0].rearrange("g p q -> p g q")[:, bass.ds(c * 2, 2), :], "ws_loaded")

            def gv_load(c):
                load(gvb[:, :], a["a_g_v"][0:1, bass.ds(c * 512, 512)].broadcast_to([P, 512]), "gv_loaded")

            v_chunk(0, 0, True)
            v_chunk(1, 1)
            ws_load(0)
            gv_load(0)
            with act.Fori(1, 4) as i:
                v_chunk(i * 2, 0)
                v_chunk(i * 2 + 1, 1)

            def u_out(c, par):
                act.wait_ge(unit_used, c * 8 + 72)
                for tok in range(2):
                    act.activation(ut[:, tok], ps[:, 2 * par + tok, :], ACT.Gelu_apprx_tanh)\
                       .then_inc(sem("u_ready"), 1)

            def us_out(c):
                act.wait_ge(sem("us_turned"), c * 2 + 2)
                for tok in range(2):
                    act.activation(ush[:, bass.ds(c * 4, 4), tok * P:tok * P + P],
                                   ps[:, 6 + tok, :].rearrange("p (k q) -> p k q", q=P), ACT.Copy)\
                       .then_inc(sem("ush_ready"), 1)

            def u_chunk(c, par, first=False, last=False):
                for r in range(8):
                    if r == 3:
                        if first:
                            v_out(7, 1)
                            act.wait_ge(sem("m2_spread"), 4)
                            for n in range(4):
                                act.activation(acc[:, 0, n * 512:n * 512 + 512], ps[:, 4 + n, :], ACT.Copy)\
                                   .then_inc(sem("m2b_ready"), 1)
                        else:
                            u_out(c - 1, 1 - par)
                    if r == 7 and not first:
                        act.wait_ge(sem("us_done"), c * 2)
                        gv_load(c)
                    if r == 6:
                        act.wait_ge(sem("ws_turned"), c + 1)
                        act.wait_ge(sem("rs"), RS_AT["v"])
                        for tok in range(2):
                            act.activation(wsc[:, tok].rearrange("p g q -> p (g q)"), ps[:, 6, 0:256], ACT.Copy,
                                           scale=st[:, 12 + tok:13 + tok]).then_inc(sem("wsc_ready"), 1)
                        if not last:
                            ws_load(c + 1)
                    if r == 7 and not first:
                        us_out(c - 1)
                    cast(G_IN + 8 + c, r)

            u_chunk(0, 0, first=True)
            u_chunk(1, 1)
            with act.Fori(1, 3) as i:
                u_chunk(i * 2, 0)
                u_chunk(i * 2 + 1, 1)
            u_chunk(6, 0)
            u_chunk(7, 1, last=True)

            for t in range(16):
                if t == 3:
                    u_out(7, 1)
                if t == 7:
                    us_out(7)
                    act.wait_ge(sem("ws_loaded"), 16 * 8)
                    act.wait_ge(sem("gv_loaded"), 16 * 8)
                    load(h[:, :, :], a["x"][0].rearrange("(b p) n -> p b n", p=P), "x_loaded")
                cast(*at(G_OUT, t))
            def out_chunk(n):
                for t in range(16):
                    if t == 5:
                        act.wait_ge(sem("resid"), n * 2)
                        part("n2", n - 1, [h[:, 0], h[:, 1]], n - 1)
                    cast(*at(G_OUT + n * 2, t))

            out_chunk(1)
            with act.Fori(2, 4) as n:
                out_chunk(n)
            for t in range(4):
                cast(G_FFN[0][0], t)
            act.wait_ge(sem("resid"), 8)
            part("n2", 3, [h[:, 0], h[:, 1]], 3)
            act.wait_ge(unit_used, units_before(G_OUT + 8))
            for i in range(3):
                load(crow[:, i, :], a["ffn_conv_w"][0, i].rearrange("(r q) -> r q", q=P), "crow_loaded")
            load(crow[:, 3, :], a["ffn_conv_b"][0].rearrange("(r q) -> r q", q=P), "crow_loaded")

            def taps(y, bank, blk, fsem):
                for n in range(4):
                    act.activation(y[:, n], ps[:, bank + n, 0:T], ACT.Identity, bias=cw[:, 3, bass.ds(blk + n, 1)],
                                   scale=cw[:, 1, bass.ds(blk + n, 1)]).then_inc(sem(fsem), 1)

            def value_out(F):
                act.wait_ge(unit_used, units_of(F) + 16)
                taps(yv, 4, F * 4 + 44, "yv_ready")

            def h_out(F, f):
                act.wait_ge(sem("hs_done"), F + 1)
                act.activation(hth[:, bass.ds(f * 4, 4), :], hs[:, :, :], ACT.Copy).then_inc(sem("hth_ready"), 1)

            for p, ((f0, nf), (gu, gd)) in enumerate(zip(FPARTS, G_FFN)):
                ubase = units_before(gu) - 16 * f0
                units_of = lambda F, ub=ubase: F * 16 + ub

                def pair(f, first=False):
                    F = f + f0
                    for t in range(16):
                        if t == 3 and not first:
                            value_out(F - 1)
                        if t == 5 and not first:
                            h_out(F - 1, f - 1)
                        if t == 11:
                            act.wait_ge(unit_used, units_of(F) + 8)
                            act.wait_ge(sem("hs_done"), F)
                            taps(yg, 0, F * 4, "yg_ready")
                        if t == 13:
                            act.wait_ge(sem("yg_done"), F + 1)
                            act.activation(sg[:, :, :], yg[:, :, :], ACT.Silu).then_inc(sem("sg_ready"), 1)
                        if first and p == 0:
                            spread("n2", t, [(T, xth)])
                        if not (first and p == 0 and t < 4):
                            cast(*at(gu + f * 2, t))

                pair(0, True)
                with act.Fori(1, nf) as f:
                    pair(f)
                for t in range(8 * nf):
                    if p == 2 and t == 0:
                        load(bcast[:, :], a["final_g"].rearrange("(o n) -> o n", o=1).broadcast_to([P, D]), "bcast_loaded")
                        act.wait_ge(sem("mred"), 4)
                        load(hm[0:NM, :], a["meta_tokens_2"], "meta_loaded")
                    if p == 2 and t == 9:
                        act.wait_ge(sem("meta_loaded"), 16)
                        act.wait_ge(sem("yv_done"), NF)
                        act.activation(ps[0:NM, 4:8, :], hm[0:NM, :].rearrange("p (b n) -> p b n", n=512), ACT.Square,
                                       accum_out=st[0:NM, 34:35]).then_inc(sem("meta_squared"), 1)
                        act.wait_ge(sem("meta_squared"), 1)
                    if p == 2 and t in (10, 16, 22):
                        act.wait_ge(sem("resid_f"), 16 + 2 * (t // 6))
                        part("f", t // 6 - 1, [h[:, 0], h[:, 1]], 2 * (t // 6) - 2)
                    if p == 2 and t in (13, 19):
                        act.wait_ge(sem("gained"), t // 6 - 1)
                        part("f", t // 6 - 2, [h[:, 0], h[:, 1]], 2 * (t // 6) - 3, 80)
                    if t == 3:
                        value_out(f0 + nf - 1)
                    if t == 5:
                        h_out(f0 + nf - 1, nf - 1)
                    if p == 0 and t == 10:
                        act.wait_ge(sem("m5_spread"), 4)
                        for n in range(4):
                            act.activation(acc[:, 0, n * 512:n * 512 + 512], ps[:, 4 + n, :], ACT.Copy)\
                               .then_inc(sem("m5b_ready"), 1)
                    cast(*at(gd, t))
            for t in range(4):
                cast(G_A, t)
            act.wait_ge(sem("gained"), 3)
            part("f", 2, [h[:, 0], h[:, 1]], 5, 80)
            act.wait_ge(sem("resid_f"), 24)
            part("f", 3, [h[:, 0], h[:, 1]], 6)
            act.wait_ge(sem("gained"), 4)
            part("f", 3, [h[:, 0], h[:, 1]], 7, 80)

            for i, name in enumerate(("a_lambda_q1_2", "a_lambda_k1_2", "a_lambda_q2_2", "a_lambda_k2_2")):
                load(lamv[0:1, i, :], a[name], "lamv_loaded")
            load(tabA[:, :, :], a["tab_a"], "tabA_loaded")
            load(rotA[:, :], a["rot_a"], "tabA_loaded")
            act.wait_ge(sem("lam_sum"), 1)
            act.activation(st[0:1, 116:118], st[0:1, 114:116], ACT.Exp).then_inc(sem("lam_exp"), 1)

            def banks_out(n, G, func, dst, done):
                for c in range(4):
                    if c < 3:
                        act.wait_ge(bank_done, n * 3 + (c + 1))
                    else:
                        act.wait_ge(unit_used, units_before(G))
                    act.activation(dst[:, c, :], ps[:, c, 0:L], func, scale=0.5 if func == ACT.Tanh else 1.0)\
                       .then_inc(sem(done), 1)

            def item_act(t, j, items=True, before=True):
                for i, back in due(t, 4, items, before):
                    it, nk = (j - back) * 6 + i, ITEM_KEYS[i % 3][1]
                    act.wait_ge(sem("a_max"), it + 1)
                    for e in range(2):
                        act.activation(ex[:, e, 0:nk], sc[:, e, 0:nk], ACT.Exp, bias=st[:, 104 + e:105 + e],
                                       accum_out=st[:, 106 + e:107 + e]).then_inc(sem("a_exp"), 1)
                for i, back in due(t, 7, items, before):
                    it = (j - back) * 6 + i
                    act.wait_ge(sem("a_wturned"), it + 1)
                    for kb in ITEM_BLOCKS[i % 3]:
                        w = BLK[kb][1]
                        cp = act.activation(wt[0:w, kb, :], ps[0:w, 6, kb * P:kb * P + P], ACT.Copy)
                    cp.then_inc(sem("a_wt"), 1)
                for i, back in due(t, 8, items, before):
                    act.wait_ge(sem("a_pv"), (j - back) * 6 + (i + 1))
                    act.activation(ojunk[:, :], ps[:, 7, 0:256], ACT.Square,
                                   accum_out=st[:, 100:101]).then_inc(sem("oss"), 1)

            def group_act(j, t, before=True):
                if t == 1:
                    act.wait_ge(sem("rope_done"), j * 4)
                    if before:
                        act.wait_ge(sem("a_scores"), (j - 1) * 6)
                    act.activation(qt[:, :, :], qs[:, :, :], ACT.Copy).then_inc(sem("qk_moved"), 1)
                    act.activation(kt_[:, :, :], ks[:, :, :], ACT.Copy).then_inc(sem("qk_moved"), 1)
                if t == 3:
                    act.wait_ge(sem("qk_moved"), j * 2)
                    banks_out(3 * j - 1, G_A + 3 * j, ACT.Copy, qs, "bank_read")
                if t == 6:
                    act.wait_ge(sem("v_turned"), j)
                    for b, (c0, w) in enumerate(BLK):
                        cp = act.activation(vx[0:w, b, :], ps[0:w, 4 + b, :], ACT.Copy)
                    cp.then_inc(sem("vx_ready"), 1)

            def heads(j, items=True, before=True):
                for t in range(24):
                    if items:
                        group_act(j, t, before)
                    if t == 11:
                        banks_out(3 * j, G_A + (3 * j + 1), ACT.Copy, qs, "bank_read")
                    if t == 19:
                        banks_out(3 * j + 1, G_A + (3 * j + 2), ACT.Copy, ks, "bank_read")
                    item_act(t, j, items, before)
                    if not items:
                        spread("a", t, [(L, xmh)])
                    if items or t > 3:
                        cast(*at(G_A + j * 3, t))

            heads(0, False, False)
            heads(1, True, False)
            with act.Fori(2, 4) as j:
                heads(j)

            def gate_out(g):
                banks_out(12 + g, G_GATE + g + 1, ACT.Tanh, gth, "gth_ready")

            def oth_out(g):
                act.wait_ge(sem("g_prod"), g + 1)
                act.activation(oth[:, 4 * g:4 * g + 4, :], g2[:, :, :], ACT.Copy).then_inc(sem("oth_ready"), 1)

            for t in range(40):
                if t % 8 == 3 and t > 8:
                    gate_out(t // 8 - 1)
                if t < 24:
                    group_act(4, t)
                    item_act(t, 4)
                else:
                    item_act(t - 24, 5, items=False)
                if t % 8 == 6 and t > 8:
                    oth_out(t // 8 - 1)
                cast(*at(G_GATE, t))

            def y_out(j):
                banks_out(16 + j, G_AOUT + (j + 1), ACT.Copy, yt, "bank_read")

            with act.Fori(1, 4) as j:
                for r in range(8):
                    if r == 3:
                        y_out(j - 1)
                    if r == 7:
                        act.wait_ge(sem("y_added"), j * 3)
                        part("b", j - 1, [h[:, 0], hm[0:NM], h[:, 1]], j - 1)
                    cast(G_AOUT + j, r)
            y_out(3)

            for r in range(4):
                cast(G_KV, r)
            act.wait_ge(sem("y_added"), 12)
            part("b", 3, [h[:, 0], hm[0:NM], h[:, 1]], 3)
            load(tabB[:, :, :], a["tab_b"], "tabB_loaded")
            load(rotB[:, :], a["rot_b"], "tabB_loaded")
            for r in range(4, 8):
                spread("b", r, [(L, xmh), (T, bxh)])
                cast(G_KV, r)

            def quad_act(t):
                for n in quads(t, 4):
                    nk = (144, L)[n // 2 % 2]
                    act.wait_ge(sem("b_max"), n + 1)
                    act.activation(st[:, 136:140], st[:, 132:136], ACT.Exp).then_inc(sem("b_sexp"), 1)
                    for i in range(4):
                        act.activation(eb_[:, i, 0:nk], sb_[:, i, 0:nk], ACT.Exp, bias=st[:, 128 + i:129 + i],
                                       accum_out=st[:, 140 + i:141 + i]).then_inc(sem("b_exp"), 1)
                for n in quads(t, 6):
                    act.wait_ge(sem("b_wturned"), n + 1)
                    for kb in range(2 + n // 2 % 2):
                        w = BLK[kb][1]
                        cp = act.activation(wtb[0:w, kb], ps[0:w, TURN_BANK[kb], :].rearrange("p (i q) -> p i q", q=P),
                                            ACT.Copy)
                    cp.then_inc(sem("b_wt"), 1)

            def pair_out(n, func, dst, done):
                for tok in range(2):
                    if tok == 0:
                        act.wait_ge(sem("pair_done"), n + 1)
                    else:
                        act.wait_ge(unit_used, units_before(G_B + n + 1))
                    act.activation(dst[:, tok, :], ps[:, tok, :], func, scale=0.5 if func == ACT.Tanh else 1.0)\
                       .then_inc(sem(done), 1)

            for t in range(72):
                spread("b", t + 8, [(L, xmh), (T, bxh)])
                if t == 3:
                    act.wait_ge(unit_used, units_before(G_KV + 1))
                    act.activation(kk[:, :, :], ps[:, 0:4, 0:L], ACT.Copy).then_inc(sem("kk_raw"), 1)
                    load(tabq[:, :, :, :], a["tab_q"], "tabq_loaded")
                    load(sinkb[:, :], a["b_sinks_2"].broadcast_to([P, 32]), "tabq_loaded")
                if t == 4:
                    act.wait_ge(sem("vb_turned"), 1)
                    for b, (c0, w) in enumerate(BLK):
                        bank, col = ((6, 0), (6, 256), (7, 0))[b]
                        cp = act.activation(vb[0:w, b, :], ps[0:w, bank, col:col + 256], ACT.Copy)
                    cp.then_inc(sem("vb_ready"), 1)
                if t % 8 == 3 and t > 8:
                    n = t // 8 - 1
                    if n < 4:
                        act.wait_ge(sem("kd_ready"), 64)
                        pair_out(n, ACT.Copy, qx, "pair_read")
                    else:
                        pair_out(n, ACT.Tanh, gb1, "gb_ready")
                quad_act(t)
                if t - 4 in Q_TURN_AT:
                    j = Q_TURN_AT.index(t - 4)
                    act.wait_ge(sem("q_turned"), j + 1)
                    for tok in range(2):
                        cp = act.activation(qtb[:, j, :, tok * P:tok * P + P],
                                            ps[:, 5 + tok, :].rearrange("p (k q) -> p k q", q=P), ACT.Copy)
                    cp.then_inc(sem("qtb_ready"), 1)
                if t - 4 in O_TURN_AT:
                    j = O_TURN_AT.index(t - 4)
                    act.wait_ge(sem("ob_turned"), j + 1)
                    for tok in range(2):
                        cp = act.activation(obh[:, 4 * j:4 * j + 4, tok * P:tok * P + P],
                                            ps[:, 5 + tok, :].rearrange("p (k q) -> p k q", q=P), ACT.Copy, scale=0.5)
                    cp.then_inc(sem("obh_ready"), 1)
                cast(*at(G_B, t))
            load(bcast[:, :], a["final_norm_2"].rearrange("(o n) -> o n", o=1).broadcast_to([P, D]), "bcast_loaded")
            with act.Fori(1, 4) as j:
                for r in range(8):
                    if r == 5:
                        act.wait_ge(sem("resid_b"), j * 2)
                        part("z", j - 1, [h[:, 0], h[:, 1]], j - 1)
                    cast(G_BOUT + j, r)
            act.wait_ge(sem("resid_b"), 8)
            part("z", 3, [h[:, 0], h[:, 1]], 3)

        @block.vector
        def _(dve):
            def lo(G, r):
                dve.wait_ge(hi_ready, units_before(G) + (r + 1))
                dve.tensor_tensor(wlo[:, r % 4], raw[:, r // 2, r % 2], whi[:, r % 4].bitcast(F32),
                                  ALU.subtract).then_inc(lo_ready, 1)

            def ada_add(k, kt, half, slot):
                dve.wait_ge(al[half], k * 16 + 16)
                if not isinstance(k, int) or k:
                    dve.wait_ge(ada_step, k * 2 + (half - 1))
                y = acc[:, slot, half * 1024:half * 1024 + 1024]
                dve.scalar_tensor_tensor(out=y, in0=ada[:, half], scalar=ccol[:, bass.ds(kt, 1)], in1=y,
                                         op0=ALU.mult, op1=ALU.add).then_inc(ada_step, 1)

            def total(name, outs, col=64, end=None):
                nb = outs.shape[1]
                dve.wait_ge(sem("part"), PART_AT[name] + 4 * nb if end is None else end)
                dve.tensor_reduce(outs, st[:, col:col + 4 * nb].rearrange("p (n b) -> p b n", b=nb), AX.X,
                                  ALU.add).then_inc(sem("ss_" + ("a" if col == 80 else name)), 1)

            def diagonals(name, cols_widths):
                dve.wait_ge(sem("rs"), RS_AT[name])
                for i, (c, w) in enumerate(cols_widths):
                    d = dve.tensor_scalar(dg[0:w, i, 0:w], ident[0:w, 0:w], st[0:w, c:c + 1], None, ALU.mult)
                d.then_inc(sem("dg"), 1)

            def spread(name, t, dests, first=4):
                m = len(dests)

                def low(i):
                    n, xh, xl = dests[i % m][0:3]
                    k = i // m
                    dve.wait_ge(sem("nh"), TILES0[name] + i + 1)
                    dve.tensor_tensor(xl[:, k, 0:n], ntmp[:, i % 2, 0:n], xh[:, k, 0:n].bitcast(F32),
                                      ALU.subtract).then_inc(sem("nl"), 1)

                for k in tiles_at(t, first):
                    for e, (n, xh, xl, gain, shift) in enumerate(dests):
                        i = k * m + e
                        dve.wait_ge(sem("nt"), TILES0[name] + k + 1)
                        if i > 1:
                            dve.wait_ge(sem("nl"), TILES0[name] + i - 1)
                        src, dst = ps[:, 4 + k % 4, 0:n], ntmp[:, i % 2, 0:n]
                        if e:
                            src = ps[:, 4 + k % 4, 0:2 * (P + NM)].rearrange("p (b q) -> p b q", q=P + NM)[:, :, 0:P]
                            dst = dst.rearrange("p (b q) -> p b q", q=P)
                        if shift is None:
                            ins = dve.tensor_scalar(dst, src, gain[:, k:k + 1], None, ALU.mult)
                        else:
                            ins = dve.tensor_scalar(dst, src, gain[:, k:k + 1], shift[:, k:k + 1], ALU.mult, ALU.add)
                        ins.then_inc(sem("ntmp"), 1)
                        if i:
                            low(i - 1)
                if KT - 1 in tiles_at(t, first):
                    low(KT * m - 1)

            own = Own(dve, sem("dve_own"))

            dve.wait_ge(sem("ccol_ready"), 1)
            for j in range(2):
                def four(i, j):
                    for q in range(4):
                        dve.wait_ge(ld[q], i * 16 + (64 * j + 16))
                        if not isinstance(i, int) or i + j + q:
                            dve.wait_ge(ada_used, i * 4 + (16 * j + q))
                        if isinstance(i, int) and q == 0:
                            dve.tensor_scalar(acc[:, j], rawv[:, q], ccol[:, 0:1], None, ALU.mult).then_inc(ada_used, 1)
                        else:
                            dve.scalar_tensor_tensor(out=acc[:, j], in0=rawv[:, q], scalar=ccol[:, bass.ds(i * 4 + q, 1)],
                                                     in1=acc[:, j], op0=ALU.mult, op1=ALU.add).then_inc(ada_used, 1)

                four(0, j)
                dve.wait_ge(sem("bias_loaded"), 16)
                dve.wait_ge(ada_used, 16 * j + 4)
                own(dve.tensor_tensor(acc[0:1, j], acc[0:1, j], brow[0:1, j], ALU.add))
                with dve.Fori(1, 4) as i:
                    four(i, j)
                if j == 0:
                    dve.wait_ge(sem("cols_turned"), 1)
                    dve.tensor_copy(cols[:, :], ps[:, 0, 0:114]).then_inc(sem("cols_ready"), 1)
                    diagonals("n1", ((4, P), (5, P)))
            dve.wait_ge(sem("cols_ready"), 1)
            dve.wait_ge(sem("mred"), 2)
            own(dve.tensor_copy(mcol[:, 0:2], ps[:, 1, 0:32].rearrange("p (m k) -> p m k", k=KT)))
            dve.scalar_tensor_tensor(out=acol[:, :], in0=mcol[:, 1], scalar=1.0, in1=cols[:, C_G0],
                                     op0=ALU.add, op1=ALU.mult).then_inc(sem("gain_n1"), 1)
            dve.wait_ge(sem("gain_n1"), 1)
            n1_dests = [(T, xth, xtl, acol, mcol[:, 0])]

            def v_chunk(c):
                for r in range(8):
                    if isinstance(c, int):
                        spread("n1", c * 8 + r, n1_dests, 0)
                    if isinstance(c, int) and c + r == 0:
                        dve.wait_ge(sem("acc_started"), 16)
                    lo(G_IN + c, r)
                    if r % 2 == 0:
                        ada_add(c * 2 + r // 4, c * 2 + r // 4, r // 2 % 2, 0)

            v_chunk(0)
            v_chunk(1)
            with dve.Fori(2, 8) as c:
                v_chunk(c)

            def u_mix(c):
                for tok in range(2):
                    dve.wait_ge(sem("mixed"), c * 2 + (tok + 1))
                    dve.wait_ge(sem("gv_loaded"), c * 16 + 16)
                    dve.wait_ge(sem("us_done"), c * 2 + tok)
                    dve.tensor_tensor(utmp[:, :], ps[:, 4 + tok, :], gvb[:, :], ALU.mult).then_inc(sem("us_own"), 1)
                    dve.wait_ge(sem("us_own"), c * 2 + (tok + 1))
                    dve.wait_ge(sem("u_ready"), c * 2 + (tok + 1))
                    for g in range(2):
                        ins = dve.scalar_tensor_tensor(
                            out=us[:, tok, g * 256:g * 256 + 256], in0=utmp[:, g * 256:g * 256 + 256],
                            scalar=cols[:, bass.ds(c * 2 + (C_BS + g), 1)], in1=ut[:, tok, g * 256:g * 256 + 256],
                            op0=ALU.add, op1=ALU.mult)
                    ins.then_inc(sem("us_done"), 1)

            def us_lo(c):
                dve.wait_ge(sem("ush_ready"), c * 2 + 2)
                for tok in range(2):
                    dve.tensor_tensor(usl[:, bass.ds(c * 4, 4), tok * P:tok * P + P],
                                      ps[:, 6 + tok, :].rearrange("p (k q) -> p k q", q=P),
                                      ush[:, bass.ds(c * 4, 4), tok * P:tok * P + P].bitcast(F32),
                                      ALU.subtract).then_inc(sem("usl_ready"), 1)

            dve.wait_ge(sem("acc_started"), 32)

            def u_chunk(c, first=False):
                for r in range(8):
                    if first and r == 4:
                        dve.wait_ge(sem("ssv"), 16)
                        dve.tensor_reduce(st[:, 8:10], st[:, 64:80].rearrange("p (c t) -> p t c", t=2), AX.X,
                                          ALU.add).then_inc(sem("ssv_ready"), 1)
                    if not first and r == 4:
                        u_mix(c - 1)
                    if not first and r == 7:
                        us_lo(c - 1)
                    lo(G_IN + 8 + c, r)
                    if r % 2 == 0:
                        ada_add(c * 2 + (16 + r // 4), c * 2 + r // 4, r // 2 % 2, 1)

            u_chunk(0, True)
            u_chunk(1)
            with dve.Fori(2, 8) as c:
                u_chunk(c)

            def residual(n, par, gate, s, base):
                gy = gy1 if s == "resid" else gy2
                for tok in range(2):
                    y = ps[:, 2 * par + tok, :]
                    hc = h[:, tok, bass.ds(n * 512, 512)]
                    if gate is not None:
                        dve.tensor_tensor(gy[:, tok], y, gate[:, bass.ds(n * 512, 512)], ALU.mult)\
                           .then_inc(sem("gated_" + s), 1)
                        dve.wait_ge(sem("gated_" + s), n * 2 + (base + tok + 1))
                        y = gy[:, tok]
                    dve.tensor_tensor(hc, hc, y, ALU.add).then_inc(sem(s), 1)

            for n in range(4):
                for t in range(16):
                    if n == 0 and t == 5:
                        u_mix(7)
                    if n == 0 and t == 7:
                        us_lo(7)
                    if n == 0 and t == 12:
                        dve.wait_ge(sem("mred"), 3)
                        dve.tensor_copy(mcol[:, 2], ps[:, 4, 0:KT]).then_inc(sem("mcol3"), 1)
                    if n and t == 3:
                        dve.wait_ge(unit_used, units_before(G_OUT) + 16 * n)
                        dve.wait_ge(sem("x_loaded"), 32)
                        if n == 1:
                            dve.wait_ge(sem("m2b_ready"), 4)
                        residual(n - 1, (n - 1) % 2, acc[:, 0], "resid", 0)
                    lo(*at(G_OUT, 16 * n + t))
                    step = t - t // 4
                    if n == 1 and t == 0:
                        dve.wait_ge(sem("acc_started"), 48)
                    if n in (1, 2) and t % 4 != 3:
                        ada_add(32 + 6 * (n - 1) + step // 2, 6 * (n - 1) + step // 2, step % 2, 1)
                    if n == 3 and t < 8:
                        ada_add(32 + 12 + t // 2, 12 + t // 2, t % 2, 1)
            dve.wait_ge(unit_used, units_before(G_OUT + 8))
            residual(3, 1, acc[:, 0], "resid", 0)

            for t in range(4):
                if t == 2:
                    total("n2", st[:, 16:18])
                lo(G_FFN[0][0], t)
            dve.wait_ge(sem("conv_turned"), 1)
            dve.tensor_copy(cw[:, :, :].rearrange("p i b -> p (i b)"), ps[:, 0, 0:352]).then_inc(sem("cw_ready"), 1)
            diagonals("n2", ((20, P), (21, P)))
            dve.wait_ge(sem("mred"), 4)
            own(dve.tensor_copy(mcol[:, 3], ps[:, 1, 0:KT]))
            dve.scalar_tensor_tensor(out=acol[:, :], in0=mcol[:, 3], scalar=1.0, in1=cols[:, C_G1],
                                     op0=ALU.add, op1=ALU.mult).then_inc(sem("gain_n2"), 1)
            dve.wait_ge(sem("gain_n2"), 1)
            dve.wait_ge(sem("mcol3"), 1)
            dve.wait_ge(sem("acc_started"), 64)

            def side_taps(y, bank, blk, ysem, F, done):
                dve.wait_ge(sem(ysem), F * 4 + 4)
                for n in range(4):
                    dve.scalar_tensor_tensor(out=y[:, n, 1:T], in0=ps[:, bank + n, 0:T - 1],
                                             scalar=cw[:, 0, bass.ds(blk + n, 1)], in1=y[:, n, 1:T],
                                             op0=ALU.mult, op1=ALU.add).then_inc(sem("tap_" + ysem), 1)
                for n in range(4):
                    dve.wait_ge(sem("tap_" + ysem), F * 4 + (n + 1))
                    ins = dve.scalar_tensor_tensor(out=y[:, n, 0:T - 1], in0=ps[:, bank + n, 1:T],
                                                   scalar=cw[:, 2, bass.ds(blk + n, 1)], in1=y[:, n, 0:T - 1],
                                                   op0=ALU.mult, op1=ALU.add)
                ins.then_inc(sem(done), 1)

            def value_done(F):
                side_taps(yv, 4, F * 4 + 44, "yv_ready", F, "yv_done")
                dve.wait_ge(sem("yv_done"), F + 1)
                dve.wait_ge(sem("sg_ready"), F + 1)
                dve.tensor_tensor(hs[:, :, :], sg[:, :, :], yv[:, :, :], ALU.mult).then_inc(sem("hs_done"), 1)

            def h_lo(F, f):
                dve.wait_ge(sem("hth_ready"), F + 1)
                dve.tensor_tensor(htl[:, bass.ds(f * 4, 4), :], hs[:, :, :], hth[:, bass.ds(f * 4, 4), :].bitcast(F32),
                                  ALU.subtract).then_inc(sem("htl_ready"), 1)

            def gained(n):
                dve.wait_ge(sem("part"), PART_AT["f"] + 4 * n + 2)
                hc = h[:, :, n * 512:n * 512 + 512]
                dve.tensor_tensor(hc, hc, bcast[:, None, n * 512:n * 512 + 512].broadcast_to([P, 2, 512]),
                                  ALU.mult).then_inc(sem("gained"), 1)

            for p, ((f0, nf), (gu, gd)) in enumerate(zip(FPARTS, G_FFN)):
                def pair(f, first=False):
                    F = f + f0
                    for t in range(16):
                        if first and p and t == 3:
                            dve.wait_ge(unit_used, units_before(gu))
                            residual(3, 1, acc[:, 0], "resid_f", 8 * (p - 1))
                        if t == 3 and not first:
                            value_done(F - 1)
                        if t == 6 and not first:
                            h_lo(F - 1, f - 1)
                        if t == 11:
                            side_taps(yg, 0, F * 4, "yg_ready", F, "yg_done")
                        if first and p == 0:
                            spread("n2", t, [(T, xth, xtl, acol, mcol[:, 2])])
                        if not (first and p == 0 and t < 4):
                            lo(*at(gu + f * 2, t))
                        if p == 0 and t % 2 == 0:
                            ada_add(f * 4 + (48 + t // 4), f * 4 + t // 4, t // 2 % 2, 0)

                pair(0, True)
                with dve.Fori(1, nf) as f:
                    pair(f)
                for t in range(8 * nf):
                    n, r = t // (2 * nf), t % (2 * nf)
                    if t == 3:
                        value_done(f0 + nf - 1)
                    if t == 6 and nf > 3 or t == 5 and nf == 3:
                        h_lo(f0 + nf - 1, nf - 1)
                    if n and r == 3:
                        dve.wait_ge(unit_used, units_before(gd) + 2 * nf * n)
                        if p == 0 and n == 1:
                            dve.wait_ge(sem("m5b_ready"), 4)
                        residual(n - 1, (n - 1) % 2, acc[:, 0], "resid_f", 8 * p)
                    if p == 2 and t in (11, 17, 23):
                        if t == 11:
                            dve.wait_ge(sem("bcast_loaded"), 16)
                        gained(t // 6 - 1)
                    lo(*at(gd, t))
            dve.wait_ge(unit_used, units_before(G_A))
            residual(3, 1, acc[:, 0], "resid_f", 16)
            lo(G_A, 0)
            lo(G_A, 1)
            gained(3)
            total("f", st[:, 24:26], 64, PART_AT["f"] + 14)
            lo(G_A, 2)
            total("f", st[:, 32:34], 80, PART_AT["f"] + 16)
            lo(G_A, 3)

            for t, rects in ((maskA, ((0, 64, 64, 128, 0), (0, 64, 208, L, 1))),):
                own(dve.memset(t[:, :, :], 0.0))
                for p0, p1, c0, c1, b in rects:
                    own(dve.memset(t[p0:p1, b, c0:c1], NEG))
            dve.wait_ge(sem("lamv_loaded"), 64)
            for i in range(2):
                own(dve.tensor_tensor(lamv[0:1, 4, :], lamv[0:1, 2 * i, :], lamv[0:1, 2 * i + 1, :], ALU.mult))
                own(dve.tensor_reduce(st[0:1, 114 + i:115 + i], lamv[0:1, 4, :], AX.X, ALU.add))
            dve.tensor_scalar(st[:, 112:114], cols[:, C_SUB:C_SUB + 2], 0.4, None, ALU.mult).then_inc(sem("lam_sum"), 1)
            diagonals("a", ((40, P), (38, NM), (41, P)))
            dve.wait_ge(sem("lam_exp"), 1)
            dve.wait_ge(sem("lam_sum"), 1)
            own(dve.tensor_tensor(st[0:1, 118:119], st[0:1, 117:118], st[0:1, 116:117], ALU.subtract))
            dve.tensor_scalar(st[0:1, 119:120], st[0:1, 118:119], -0.2, None, ALU.add).then_inc(sem("nlam"), 1)

            def rope(j, q):
                x = (qs, ks)[q // 2][0:32, q % 2 * 2:q % 2 * 2 + 2, :]
                n = j * 4 + q
                dve.wait_ge(sem("rot"), n + 1)
                if not isinstance(n, int) or n:
                    dve.wait_ge(sem("rope_done"), n)
                dve.tensor_tensor(rt2[:, :, :], ps[0:32, 4:6, 0:L], tabA[:, 1:2, :].broadcast_to([32, 2, L]),
                                  ALU.mult).then_inc(sem("rope_read"), 1)
                dve.tensor_tensor(x, x, tabA[:, 0:1, :].broadcast_to([32, 2, L]), ALU.mult).then_inc(sem("rope_own"), 1)
                dve.wait_ge(sem("rope_read"), n + 1)
                dve.wait_ge(sem("rope_own"), n + 1)
                dve.tensor_tensor(x, x, rt2[:, :, :], ALU.add).then_inc(sem("rope_done"), 1)

            def item_dve(t, j, items=True, before=True):
                for i, back in due(t, 4, items, before):
                    it, b = (j - back) * 6 + i, i % 3
                    own3 = Own(dve, sem("item_own"), it * 5)
                    nk = ITEM_KEYS[b][1]
                    dve.wait_ge(sem("a_scores"), it + 1)
                    s = sc[:, :, 0:nk]
                    if b == 1:
                        own3(dve.tensor_scalar(s, ps[:, 4:6, 0:nk], AH ** -0.5, None, ALU.mult))
                    else:
                        own3(dve.scalar_tensor_tensor(out=s, in0=ps[:, 4:6, 0:nk], scalar=AH ** -0.5,
                                                      in1=maskA[:, b // 2:b // 2 + 1, 0:nk].broadcast_to([P, 2, nk]),
                                                      op0=ALU.mult, op1=ALU.add))
                    own3(dve.tensor_reduce(st[:, 102:104], s, AX.X, ALU.max))
                    dve.tensor_scalar(st[:, 104:106], st[:, 102:104], -1.0, None, ALU.mult).then_inc(sem("a_max"), 1)
                for i, back in due(t, 4, items, before):
                    it, nk = (j - back) * 6 + i, ITEM_KEYS[i % 3][1]
                    own3 = Own(dve, sem("item_own"), it * 5 + 2)
                    dve.wait_ge(sem("a_exp"), it * 2 + 2)
                    if not isinstance(it, int) or it:
                        dve.wait_ge(sem("a_wturned"), it)
                    own3(dve.reciprocal(st[:, 108:110], st[:, 106:108]))
                    own3(dve.tensor_scalar(st[:, 110:111], st[:, 109:110], st[:, 111:112], None, ALU.mult))
                    own3(dve.tensor_scalar(wd[:, 0:nk], ex[:, 0, 0:nk], st[:, 108:109], None, ALU.mult))
                    dve.scalar_tensor_tensor(out=wd[:, 0:nk], in0=ex[:, 1, 0:nk], scalar=st[:, 110:111],
                                             in1=wd[:, 0:nk], op0=ALU.mult, op1=ALU.add).then_inc(sem("a_w"), 1)
                for i, back in due(t, 9, items, before):
                    dve.wait_ge(sem("ors"), (j - back) * 6 + (i + 1))
                    dve.tensor_scalar(on[:, :], ps[:, 7, 0:256], st[:, 101:102], None, ALU.mult).then_inc(sem("a_on"), 1)
                for i, back in due(t, 10, items, before):
                    c0, w = BLK[i % 3]
                    dve.wait_ge(sem("a_oturned"), (j - back) * 6 + (i + 1))
                    for d in range(2):
                        dve.tensor_scalar(ot[:, bass.ds((j - back) * 4 + (2 * (i // 3) + d), 1), c0:c0 + w],
                                          ps[:, 7:8, 256 + d * P:256 + d * P + w], st[:, 112 + d:113 + d], None,
                                          ALU.mult).then_inc(sem("a_ot"), 1)

            def heads(j, items=True, before=True):
                for t in range(24):
                    if t == 0 and items:
                        rope(j - 1, 3)
                    if isinstance(j, int) and j == 1 and t in (2, 3):
                        hb = h[:, t - 2, :]
                        dve.tensor_scalar(hb, hb, st[:, 26 + t:27 + t], None, ALU.mult).then_inc(sem("x2_ready"), 1)
                    item_dve(t, j, items, before)
                    if not items and t == 12:
                        dve.wait_ge(sem("nlam_ps"), 1)
                        own(dve.tensor_copy(st[:, 111:112], ps[:, 4, 0:1]))
                        dve.tensor_copy(st[:, 119:120], st[:, 111:112]).then_inc(sem("lam_read"), 1)
                    if t - 4 in ROPE_AT:
                        rope(j, ROPE_AT.index(t - 4))
                    if not items:
                        spread("a", t, [(L, xmh, xml, cols[:, C_AN], None)])
                    if items or t > 3:
                        lo(*at(G_A + j * 3, t))

            heads(0, False, False)
            heads(1, True, False)
            with dve.Fori(2, 4) as j:
                heads(j)

            def gate(g):
                for c in range(4):
                    dve.wait_ge(sem("gth_ready"), g * 4 + c + 1)
                    dve.scalar_tensor_tensor(out=g2[:, c, :], in0=gth[:, c, :], scalar=1.0, in1=ps[:, c, 0:L],
                                             op0=ALU.add, op1=ALU.mult).then_inc(sem("bank_read"), 1)

            def gate_times(g):
                dve.wait_ge(sem("bank_read"), (12 + g) * 4 + 4)
                dve.tensor_tensor(g2[:, :, :], g2[:, :, :], ot[:, 4 * g:4 * g + 4, :], ALU.mult).then_inc(sem("g_prod"), 1)

            def otl_out(g):
                dve.wait_ge(sem("oth_ready"), g + 1)
                dve.tensor_tensor(otl[:, 4 * g:4 * g + 4, :], g2[:, :, :], oth[:, 4 * g:4 * g + 4, :].bitcast(F32),
                                  ALU.subtract).then_inc(sem("g_done"), 1)

            for t in range(40):
                if t == 0:
                    rope(3, 3)
                if t % 8 == 3 and t > 8:
                    if t > 11:
                        dve.wait_ge(sem("g_done"), t // 8 - 1)
                    gate(t // 8 - 1)
                if t < 24:
                    item_dve(t, 4)
                else:
                    item_dve(t - 24, 5, items=False)
                if t % 8 == 4 and t > 8:
                    gate_times(t // 8 - 1)
                if t % 8 == 7 and t > 8:
                    otl_out(t // 8 - 1)
                lo(*at(G_GATE, t))

            dve.wait_ge(sem("x2_ready"), 2)

            def y_add(j):
                dve.wait_ge(sem("y_turned"), j + 1)
                for b, (c0, w) in enumerate(BLK):
                    hb = (h[:, 0], hm[0:NM], h[:, 1])[b]
                    hc = hb[:, bass.ds(j * 512, 512)]
                    dve.tensor_tensor(hc, hc, ps[0:w, 4 + b, :], ALU.add).then_inc(sem("y_added"), 1)

            with dve.Fori(1, 4) as j:
                for r in range(8):
                    if r == 6:
                        y_add(j - 1)
                    lo(G_AOUT + j, r)
            y_add(3)

            own4 = Own(dve, sem("dve_own_b"))
            for r in range(4):
                if r == 2:
                    total("b", st[:, 48:51])
                lo(G_KV, r)
            diagonals("b", ((52, P), (53, NM), (54, P)))
            b_dests = [(L, xmh, xml, cols[:, C_KVN], None), (T, bxh, bxl, cols[:, C_BN], None)]
            own4(dve.memset(maskB[:, :, :], 0.0))
            for p0, p1, c0, c1, b in ((0, 64, 64, 128, 0), (0, 64, 208, L, 1), (64, 128, 0, 64, 1)):
                own4(dve.memset(maskB[p0:p1, b, c0:c1], NEG))
            for r in range(4, 8):
                spread("b", r, b_dests)
                lo(G_KV, r)

            def rope_k():
                dve.wait_ge(sem("kk_raw"), 1)
                dve.wait_ge(sem("tabB_loaded"), 32)
                own4(dve.tensor_tensor(kt1[:, :, :], kk[:, 0:2, :], tabB[:, 0:1, :].broadcast_to([P, 2, L]), ALU.mult))
                dve.wait_ge(sem("rotb"), 1)
                own4(dve.tensor_tensor(kt2[:, :, :], ps[:, 4:6, 0:L], tabB[:, 1:2, :].broadcast_to([P, 2, L]), ALU.mult))
                dve.tensor_tensor(kk[:, 0:2, :], kt1[:, :, :], kt2[:, :, :], ALU.add).then_inc(sem("kk_ready"), 1)
                dve.wait_ge(sem("tabq_loaded"), 32)

            qv = qx[:, :, :].rearrange("p t (h d) -> p t h d", d=BH)

            def quad_dve(t):
                for n in quads(t, 4):
                    j, tok, half = n // 4, n // 2 % 2, n % 2
                    own6 = Own(dve, sem("quad_own"), n * 6)
                    nk = (144, L)[tok]
                    dve.wait_ge(sem("b_scores"), n + 1)
                    s = sb_[:, :, 0:nk]
                    sink = sinkb[:, j * 8 + 4 * half:j * 8 + 4 * half + 4]
                    own6(dve.scalar_tensor_tensor(out=s, in0=ps[:, 4:8, 0:nk], scalar=BH ** -0.5,
                                                  in1=maskB[:, tok:tok + 1, 0:nk].broadcast_to([P, 4, nk]),
                                                  op0=ALU.mult, op1=ALU.add))
                    own6(dve.tensor_reduce(st[:, 120:124], s, AX.X, ALU.max))
                    own6(dve.tensor_tensor(st[:, 124:128], st[:, 120:124], sink, ALU.max))
                    own6(dve.tensor_scalar(st[:, 128:132], st[:, 124:128], -1.0, None, ALU.mult))
                    dve.tensor_tensor(st[:, 132:136], sink, st[:, 124:128], ALU.subtract).then_inc(sem("b_max"), 1)
                for n in quads(t, 5):
                    own6 = Own(dve, sem("quad_own"), n * 6 + 4)
                    dve.wait_ge(sem("b_sexp"), n + 1)
                    dve.wait_ge(sem("b_exp"), n * 4 + 4)
                    own6(dve.tensor_tensor(st[:, 144:148], st[:, 140:144], st[:, 136:140], ALU.add))
                    if n:
                        dve.wait_ge(sem("b_o"), n)
                    own6(dve.reciprocal(st[:, 148:152], st[:, 144:148]))
                for n in quads(t, 7):
                    j, tok, half = n // 4, n // 2 % 2, n % 2
                    dve.wait_ge(sem("b_pv"), n + 1)
                    dve.tensor_tensor(ob[:, j, tok, half * 256:half * 256 + 256].rearrange("p (i d) -> p i d", d=BH),
                                      ps[:, 2, 0:256].rearrange("p (i d) -> p i d", d=BH),
                                      st[:, 148:152].unsqueeze(2).broadcast_to([P, 4, BH]), ALU.mult)\
                       .then_inc(sem("b_o"), 1)

            def rope_q(j, tok):
                own5 = Own(dve, sem("qrope_own"), j * 6 + tok * 3)
                own5(dve.tensor_tensor(rta[:, :, :], qv[:, tok, :, 0:16],
                                       tabq[:, tok, 0:1, :].broadcast_to([P, 8, 16]), ALU.mult))
                dve.tensor_tensor(rtb[:, :, 0:8], qv[:, tok, :, 8:16],
                                  tabq[:, tok, 1:2, 0:8].broadcast_to([P, 8, 8]), ALU.mult)
                own5(dve.tensor_tensor(rtb[:, :, 8:16], qv[:, tok, :, 0:8],
                                       tabq[:, tok, 1:2, 8:16].broadcast_to([P, 8, 8]), ALU.mult))
                own5(dve.tensor_tensor(qv[:, tok, :, 0:16], rta[:, :, :], rtb[:, :, :], ALU.add))

            def gb(j):
                for tok in range(2):
                    dve.wait_ge(sem("gb_ready"), j * 2 + tok + 1)
                    dve.scalar_tensor_tensor(out=gb2[:, tok, :], in0=gb1[:, tok, :], scalar=1.0, in1=ps[:, tok, :],
                                             op0=ALU.add, op1=ALU.mult).then_inc(sem("pair_read"), 1)

            def gb_times(j):
                dve.wait_ge(sem("pair_read"), j * 2 + 10)
                dve.tensor_tensor(gb2[:, :, :], gb2[:, :, :], ob[:, j, :, :], ALU.mult).then_inc(sem("gb_prod"), 1)

            def ob_lo(j):
                dve.wait_ge(sem("obh_ready"), j + 1)
                for tok in range(2):
                    ins = dve.scalar_tensor_tensor(
                        out=obl[:, 4 * j:4 * j + 4, tok * P:tok * P + P],
                        in0=ps[:, 5 + tok, :].rearrange("p (k q) -> p k q", q=P), scalar=0.5,
                        in1=obh[:, 4 * j:4 * j + 4, tok * P:tok * P + P].bitcast(F32), op0=ALU.mult, op1=ALU.subtract)
                ins.then_inc(sem("obl_ready"), 1)

            for t in range(72):
                spread("b", t + 8, b_dests)
                if t == 4:
                    rope_k()
                n = t // 8 - 1
                if n < 4:
                    quad_dve(t)
                if n >= 0 and n < 4 and t % 8 in (4, 5):
                    tok = t % 8 - 4
                    dve.wait_ge(sem("pair_read"), n * 2 + tok + 1)
                    rope_q(n, tok)
                if n >= 4 and t % 8 == 3:
                    gb(n - 4)
                if n >= 4:
                    quad_dve(t)
                if n >= 4 and t % 8 == 3:
                    gb_times(n - 4)
                if t - 4 in O_TURN_AT:
                    ob_lo(O_TURN_AT.index(t - 4))
                lo(*at(G_B, t))
            for j in range(1, 4):
                for r in range(8):
                    if r == 3:
                        dve.wait_ge(unit_used, units_before(G_BOUT + j))
                        residual(j - 1, (j - 1) % 2, None, "resid_b", 0)
                    lo(G_BOUT + j, r)
            dve.wait_ge(unit_used, units_before(G_BOUT + 4))
            residual(3, 1, None, "resid_b", 0)
            total("z", st[:, 56:58])
            dve.wait_ge(sem("rs"), RS_AT["z"])
            dve.wait_ge(sem("bcast_loaded"), 32)
            for b in range(2):
                dve.scalar_tensor_tensor(out=h[:, b, :], in0=h[:, b, :], scalar=st[:, 60 + b:61 + b], in1=bcast[:, :],
                                         op0=ALU.mult, op1=ALU.mult).then_inc(sem("result_ready"), 1)

        @block.tensor
        def _(pe):
            def tok_unit(G, r, xh, xl, k0, bank, first, last, chunk=None):
                pe.wait_ge(lo_ready, units_before(G) + (r + 1))
                for tok in range(2):
                    if first and chunk:
                        pe.wait_ge(sem("pair_read"), chunk * 2 + tok - 1)
                    for i in range(2):
                        xs = [x[:, k0 + i, tok * P:tok * P + P] for x in (xh, xl)]
                        for n, (x, w) in enumerate(((0, whi), (0, wlo), (1, whi))):
                            mm = pe.matmul(ps[:, bank + tok, :], xs[x], w[:, r % 4, i, :],
                                           start=first and i == 0 and n == 0, stop=last and i == 1 and n == 2)
                    if last and tok == 0 and chunk is not None:
                        mm.then_inc(sem("pair_done"), 1)
                mm.then_inc(unit_used, 1)

            def chan_unit(G, r, xh, xl, n_tok, bank, first, last, chunk=None, counted=False, resid=None):
                pe.wait_ge(lo_ready, units_before(G) + (r + 1))
                for c in range(4):
                    if first and chunk is not None:
                        pe.wait_ge(sem("bank_read"), chunk * 4 + (c - 3))
                    if first and resid is not None and c > 1:
                        pe.wait_ge(sem("resid_f"), resid + (c - 3))
                    for i in range(2):
                        ws = [w[:, r % 4, i, c * P:c * P + P] for w in (whi, wlo)]
                        for n, (w, x) in enumerate(((0, xh), (0, xl), (1, xh))):
                            mm = pe.matmul(ps[:, bank + c, 0:n_tok], ws[w], x[:, 2 * r + i, 0:n_tok],
                                           start=first and i == 0 and n == 0, stop=last and i == 1 and n == 2)
                    if last and c < 3 and counted:
                        mm.then_inc(bank_done, 1)
                mm.then_inc(unit_used, 1)

            def turned_tile(name, k):
                if k == 0:
                    pe.wait_ge(sem("dg"), DG_AT[name])
                steps = 1 + (name == "b")
                if k >= 4:
                    pe.wait_ge(sem("ntmp"), TILES0[name] + steps * (k - 3))
                srcs = ((h[:, 0], 0, P), (h[:, 1], P, P))
                if name in "ab":
                    srcs = ((h[:, 0], 0, P), (hm[:, :], P, NM), (h[:, 1], P + NM, P))
                for d, (src, c0, w) in enumerate(srcs):
                    mm = pe.matmul(ps[:, 4 + k % 4, c0:c0 + w], src[0:w, k * P:k * P + P], dg[0:w, d, 0:w],
                                   start=True, stop=True)
                mm.then_inc(sem("nt"), 1)

            def normed(name, r):
                if r < 6:
                    turned_tile(name, 2 * r + 4)
                    turned_tile(name, 2 * r + 5)
                pe.wait_ge(sem("nl"), TILES0[name] + (1 + (name == "b")) * (2 * r + 2))

            def column(slot, bank, c0):
                for b in range(KT):
                    mm = pe.matmul(ps[:, bank, c0 + b:c0 + b + 1], acc[:, slot, b * P:b * P + P], ones[:, 0:1],
                                   start=True, stop=True)
                mm.then_inc(sem("mred"), 1)

            def row_all(slot, done):
                for n in range(4):
                    pe.matmul(ps[:, 4 + n, :], ones[:, :], acc[:, slot, n * 512:n * 512 + 512],
                              start=True, stop=True).then_inc(sem(done), 1)

            pe.wait_ge(sem("const_ready"), 3)
            pe.wait_ge(sem("c_loaded"), 16)
            pe.transpose(ps[:, 2, 0:16], crows[:, :], ident[0:16, 0:16]).then_inc(sem("c_turned"), 1)
            pe.wait_ge(sem("rows_loaded"), 16 * 8)
            pe.transpose(ps[:, 0, 0:96], rows[0:96, 0, :], ident[0:96, 0:96])
            pe.transpose(ps[:, 0, 96:114], rows[0:18, 1, :], ident[0:18, 0:18]).then_inc(sem("cols_turned"), 1)
            pe.wait_ge(ada_used, 16)
            column(0, 1, 0)
            for k in range(4):
                turned_tile("n1", k)
            pe.wait_ge(ada_used, 32)
            column(1, 1, 16)

            def v_chunk(c, par, first=False):
                if not first:
                    pe.wait_ge(sem("v_ready"), c * 2 - 2)
                for r in range(8):
                    if first and par == 0:
                        normed("n1", r)
                    tok_unit(G_IN + c, r, xth, xtl, 2 * r, 2 * par, r == 0, r == 7)

            v_chunk(0, 0, True)
            v_chunk(1, 1, True)
            with pe.Fori(1, 4) as i:
                v_chunk(i * 2, 0)
                v_chunk(i * 2 + 1, 1)

            def mix(c):
                pe.wait_ge(sem("wsc_ready"), c * 2 + 2)
                pe.wait_ge(sem("v_ready"), 16)
                for tok in range(2):
                    for g in range(2):
                        mm = pe.matmul(ps[:, 4 + tok, g * 256:g * 256 + 256], wsc[:, tok, g, :],
                                       v[:, bass.ds(c, 1), tok, g * 256:g * 256 + 256].rearrange("p o n -> p (o n)"),
                                       start=True, stop=True)
                    mm.then_inc(sem("mixed"), 1)

            def us_turn(c):
                for tok in range(2):
                    pe.wait_ge(sem("us_done"), c * 2 + (tok + 1))
                    for k in range(4):
                        mm = pe.transpose(ps[:, 6 + tok, k * P:k * P + P], us[:, tok, k * P:k * P + P], ident[:, :])
                    mm.then_inc(sem("us_turned"), 1)

            def u_chunk(c, par, first=False):
                if first:
                    pe.wait_ge(sem("v_ready"), 14)
                    pe.wait_ge(ada_step, 32)
                    row_all(0, "m2_spread")
                else:
                    pe.wait_ge(sem("u_ready"), c * 2 - 2)
                for r in range(8):
                    if r == 1:
                        pe.wait_ge(sem("ws_loaded"), c * 16 + 16)
                        if first:
                            pe.wait_ge(sem("m2b_ready"), 4)
                        else:
                            pe.wait_ge(sem("usl_ready"), c * 2 - 2)
                        for g in range(2):
                            mm = pe.transpose(ps[:, 6, g * P:g * P + P], wsr[:, g, :], ident[:, :])
                        mm.then_inc(sem("ws_turned"), 1)
                    if r == 4 and not first:
                        pe.wait_ge(sem("wsc_ready"), c * 2 + 2)
                        us_turn(c - 1)
                    if r == 5:
                        mix(c)
                    tok_unit(G_IN + 8 + c, r, xth, xtl, 2 * r, 2 * par, r == 0, r == 7)

            u_chunk(0, 0, True)
            pe.wait_ge(sem("v_ready"), 16)
            u_chunk(1, 1)
            with pe.Fori(1, 4) as i:
                u_chunk(i * 2, 0)
                u_chunk(i * 2 + 1, 1)

            for n in range(4):
                if n == 0:
                    pe.wait_ge(sem("u_ready"), 14)
                elif n == 1:
                    pe.wait_ge(sem("u_ready"), 16)
                else:
                    pe.wait_ge(sem("resid"), 2 * n - 2)
                for t in range(16):
                    if n == 0 and t == 4:
                        pe.wait_ge(sem("wsc_ready"), 16)
                        us_turn(7)
                    if n == 0 and t == 8:
                        pe.wait_ge(ada_step, 64)
                        column(1, 4, 0)
                    if n == 0 and t % 2 == 0:
                        pe.wait_ge(sem("usl_ready"), t + 2)
                    tok_unit(*at(G_OUT, 16 * n + t), ush, usl, 2 * t, 2 * (n % 2), t == 0, t == 15)

            pe.wait_ge(sem("crow_loaded"), 64)
            for i in range(4):
                mm = pe.transpose(ps[:, 0, 88 * i:88 * i + 88], crow[:, i, :], ident[0:88, 0:88])
            mm.then_inc(sem("conv_turned"), 1)
            pe.wait_ge(ada_step, 96)
            column(1, 1, 0)
            for k in range(4):
                turned_tile("n2", k)
            pe.wait_ge(sem("cw_ready"), 1)
            for p, ((f0, nf), (gu, gd)) in enumerate(zip(FPARTS, G_FFN)):
                def pair(f, first=False):
                    F = f + f0
                    if first:
                        if p == 0:
                            pe.wait_ge(sem("gain_n2"), 1)
                        else:
                            pe.wait_ge(sem("resid_f"), 8 * p - 2)
                    else:
                        pe.wait_ge(sem("yg_done"), F)
                    for r in range(8):
                        if first and p == 0:
                            normed("n2", r)
                        chan_unit(gu + f * 2, r, xth, xtl, T, 0, r == 0, r == 7,
                                  resid=8 * p if first and p else None)
                    if first and p == 0:
                        pass
                    elif first and p == 1:
                        pe.wait_ge(sem("m5b_ready"), 4)
                        pe.wait_ge(sem("yv_done"), F)
                    else:
                        pe.wait_ge(sem("yv_done"), F)
                    for r in range(8):
                        chan_unit(gu + f * 2 + 1, r, xth, xtl, T, 4, r == 0, r == 7)

                pair(0, True)
                with pe.Fori(1, nf) as f:
                    pair(f)
                for t in range(8 * nf):
                    n, r = t // (2 * nf), t % (2 * nf)
                    if r == 0 and n < 2:
                        pe.wait_ge(sem("yg_done"), f0 + nf)
                    elif r == 0:
                        pe.wait_ge(sem("resid_f"), 8 * p + 2 * n - 2)
                    if p == 0 and t == 6:
                        pe.wait_ge(sem("yv_done"), nf)
                        pe.wait_ge(ada_step, 128)
                        row_all(0, "m5_spread")
                    if n == 0 and r % 2 == 0:
                        pe.wait_ge(sem("htl_ready"), f0 + r // 2 + 1)
                    tok_unit(*at(gd, t), hth, htl, 2 * r, 2 * (n % 2), r == 0, r == 2 * nf - 1)

            pe.wait_ge(sem("gained"), 4)
            pe.wait_ge(sem("meta_loaded"), 16)
            for k in range(4):
                turned_tile("a", k)

            def item_pe(t, j, items=True, before=True):
                for i, back in due(t, 3, items, before):
                    it, b = (j - back) * 6 + i, i % 3
                    pe.wait_ge(sem("a_w"), it + 1)
                    for kb in ITEM_BLOCKS[b]:
                        kc, w = BLK[kb]
                        k0 = ITEM_KEYS[b][0]
                        mm = pe.transpose(ps[0:w, 6, kb * P:kb * P + P], wd[:, kc - k0:kc - k0 + w], ident[:, :])
                    mm.then_inc(sem("a_wturned"), 1)
                for i, back in due(t, 6, items, before):
                    pe.wait_ge(sem("a_on"), (j - back) * 6 + (i + 1))
                    for d in range(2):
                        mm = pe.transpose(ps[:, 7, 256 + d * P:256 + d * P + P], on[:, d * P:d * P + P], ident[:, :])
                    mm.then_inc(sem("a_oturned"), 1)
                for i, back in due(t, 4, items, before):
                    it, blocks = (j - back) * 6 + i, ITEM_BLOCKS[i % 3]
                    if not isinstance(it, int) or it:
                        pe.wait_ge(sem("a_ot"), it * 2)
                    pe.wait_ge(sem("a_wt"), it + 1)
                    for kb in blocks:
                        w = BLK[kb][1]
                        mm = pe.matmul(ps[:, 7, 0:256], wt[0:w, kb, :], vx[0:w, kb, i // 3 * 256:i // 3 * 256 + 256],
                                       start=kb == blocks[0], stop=kb == blocks[-1])
                    mm.then_inc(sem("a_pv"), 1)
                if items and t == 1:
                    pe.wait_ge(sem("bank_read"), j * 12)
                    pe.wait_ge(sem("rope_read"), j * 4)
                    for b, (c0, w) in enumerate(BLK):
                        for i in range(4):
                            mm = pe.transpose(ps[0:w, 4 + b, i * P:i * P + P], qs[:, i, c0:c0 + w], ident[:, :])
                    mm.then_inc(sem("v_turned"), 1)
                for i, back in due(t, 0, items, before):
                    c0, pair, (k0, nk) = BLK[i % 3][0], i // 3, ITEM_KEYS[i % 3]
                    if i == 0:
                        pe.wait_ge(sem("qk_moved"), j * 2)
                        pe.wait_ge(sem("vx_ready"), j)
                    for q in range(4):
                        if t > ROPE_AT[q] and ITEM_AT[i - 1] <= ROPE_AT[q] and rotates(j):
                            pe.wait_ge(sem("rope_read"), j * 4 + (q + 1))
                    for e in range(2):
                        mm = pe.matmul(ps[:, 4 + e, 0:nk], qt[:, 2 * pair + e, c0:c0 + P],
                                       kt_[:, 2 * pair + e, k0:k0 + nk], start=True, stop=True)
                    mm.then_inc(sem("a_scores"), 1)

            def rotates(j):
                return not isinstance(j, int) or j < 4

            def swap_halves(j, q):
                if not isinstance(j, int) or j:
                    done = len([x for x in ITEM_AT if x < ROPE_AT[q]])
                    pe.wait_ge(sem("a_max"), (j - 1) * 6 + done)
                pe.wait_ge(sem("bank_read"), j * 12 + 4 * (q // 2 + 1))
                if not isinstance(j, int) or j * 4 + q:
                    pe.wait_ge(sem("rope_read"), j * 4 + q)
                else:
                    pe.wait_ge(sem("lam_read"), 1)
                for i in range(2):
                    mm = pe.matmul(ps[:, 4 + i, 0:L], rotA[:, :], (qs, ks)[q // 2][0:32, q % 2 * 2 + i, :],
                                   start=True, stop=True)
                mm.then_inc(sem("rot"), 1)

            def heads(j, items=True, before=True):
                for t in range(24):
                    item_pe(t, j, items, before)
                    if not items and t < 8:
                        normed("a", t)
                    if not items and t == 8:
                        pe.wait_ge(sem("nlam"), 1)
                        pe.matmul(ps[:, 4, 0:1], ones[0:1, :], st[0:1, 119:120], start=True, stop=True)\
                          .then_inc(sem("nlam_ps"), 1)
                        pe.wait_ge(sem("tabA_loaded"), 32)
                    if t in ROPE_AT:
                        swap_halves(j, ROPE_AT.index(t))
                    chunk = None if isinstance(j, int) and j * 3 + t // 8 == 0 else j * 3 + t // 8
                    chan_unit(*at(G_A + j * 3, t), xmh, xml, L, 0, t % 8 == 0, t % 8 == 7, chunk, True)

            pe.wait_ge(sem("resid_f"), 24)
            heads(0, False, False)
            heads(1, True, False)
            with pe.Fori(2, 4) as j:
                heads(j)

            for t in range(40):
                if t < 24:
                    item_pe(t, 4)
                else:
                    item_pe(t - 24, 5, items=False)
                if t < 32:
                    chan_unit(*at(G_GATE, t), xmh, xml, L, 0, t % 8 == 0, t % 8 == 7, 12 + t // 8, True)
                else:
                    if t % 2 == 0:
                        pe.wait_ge(sem("g_done"), (t - 32) // 2 + 1)
                    chan_unit(*at(G_GATE, t), oth, otl, L, 0, t % 8 == 0, t % 8 == 7, 12 + t // 8, True)

            def y_turn(j):
                if not isinstance(j, int) or j:
                    pe.wait_ge(sem("y_added"), j * 3)
                pe.wait_ge(sem("bank_read"), j * 4 + 68)
                for b, (c0, w) in enumerate(BLK):
                    for i in range(4):
                        mm = pe.transpose(ps[0:w, 4 + b, i * P:i * P + P], yt[:, i, c0:c0 + w], ident[:, :])
                mm.then_inc(sem("y_turned"), 1)

            def out_chunk(j):
                for r in range(8):
                    if r == 3:
                        y_turn(j - 1)
                    chan_unit(G_AOUT + j, r, oth, otl, L, 0, r == 0, r == 7, j + 16, True)

            out_chunk(1)
            with pe.Fori(2, 4) as j:
                out_chunk(j)
            y_turn(3)

            pe.wait_ge(sem("y_added"), 12)
            for k in range(4):
                turned_tile("b", k)
            for r in range(8):
                normed("b", r)
                chan_unit(G_KV, r, xmh, xml, L, 0, r == 0, r == 7)
            pe.wait_ge(sem("kk_raw"), 1)
            pe.wait_ge(sem("tabB_loaded"), 32)
            for i in range(2):
                mm = pe.matmul(ps[:, 4 + i, 0:L], rotB[:, :], kk[:, i, :], start=True, stop=True)
            mm.then_inc(sem("rotb"), 1)
            for b, (c0, w) in enumerate(BLK):
                bank, col = ((6, 0), (6, 256), (7, 0))[b]
                for i in range(2):
                    mm = pe.transpose(ps[0:w, bank, col + i * P:col + i * P + P], kk[:, 2 + i, c0:c0 + w], ident[:, :])
            mm.then_inc(sem("vb_turned"), 1)

            def quad_pe(t):
                for n in quads(t, 2):
                    tok = n // 2 % 2
                    if n:
                        pe.wait_ge(sem("b_o"), n)
                    pe.wait_ge(sem("b_exp"), n * 4 + 4)
                    for kb in range(2 + tok):
                        kc, w = BLK[kb]
                        for i in range(4):
                            mm = pe.transpose(ps[0:w, TURN_BANK[kb], i * P:i * P + P], eb_[:, i, kc:kc + w], ident[:, :])
                    mm.then_inc(sem("b_wturned"), 1)
                for n in quads(t, 3):
                    j, tok = n // 4, n // 2 % 2
                    pe.wait_ge(sem("b_wt"), n + 1)
                    for i in range(4):
                        for kb in range(2 + tok):
                            w = BLK[kb][1]
                            mm = pe.matmul(ps[:, 2, i * BH:i * BH + BH], wtb[0:w, kb, i, :],
                                           vb[0:w, kb, j * BH:j * BH + BH], start=kb == 0, stop=kb == 1 + tok)
                    mm.then_inc(sem("b_pv"), 1)
                for n in quads(t, 0):
                    j, tok, half = n // 4, n // 2 % 2, n % 2
                    nk = (144, L)[tok]
                    pe.wait_ge(sem("qtb_ready"), len([x for x in Q_TURN_AT if x < t]))
                    if t > O_TURN_AT[0]:
                        pe.wait_ge(sem("obl_ready"), len([x for x in O_TURN_AT if x < t]))
                    for i in range(4):
                        p0 = 64 * (i % 2)
                        mm = pe.matmul(ps[:, 4 + i, 0:nk], qtb[p0:p0 + 64, j, 2 * half + i // 2, tok * P:tok * P + P],
                                       kd[p0:p0 + 64, j, 0:nk], start=True, stop=True)
                    mm.then_inc(sem("b_scores"), 1)

            def turn(src, done):
                for tok in range(2):
                    for i in range(4):
                        mm = pe.transpose(ps[:, 5 + tok, i * P:i * P + P], src[:, tok, i * P:i * P + P], ident[:, :])
                mm.then_inc(sem(done), 1)

            for t in range(72):
                if t == QUAD_AT[0]:
                    pe.wait_ge(sem("vb_ready"), 1)
                    pe.wait_ge(sem("kd_ready"), 64)
                if t == Q_TURN_AT[0]:
                    pe.wait_ge(sem("kk_ready"), 1)
                    pe.wait_ge(sem("vb_ready"), 1)
                quad_pe(t)
                if t in Q_TURN_AT:
                    pe.wait_ge(sem("qrope_own"), Q_TURN_AT.index(t) * 6 + 6)
                    turn(qx, "q_turned")
                if t in O_TURN_AT:
                    pe.wait_ge(sem("gb_prod"), O_TURN_AT.index(t) + 1)
                    turn(gb2, "ob_turned")
                if t < 64:
                    tok_unit(*at(G_B, t), bxh, bxl, 2 * (t % 8), 0, t % 8 == 0, t % 8 == 7, t // 8)
                else:
                    if t % 2 == 0:
                        pe.wait_ge(sem("obl_ready"), t % 8 // 2 + 1)
                    tok_unit(*at(G_B, t), obh, obl, 2 * (t % 8), 0, t % 8 == 0, t % 8 == 7, t // 8)
            for j in range(1, 4):
                if j > 1:
                    pe.wait_ge(sem("resid_b"), 2 * j - 2)
                for r in range(8):
                    tok_unit(G_BOUT + j, r, obh, obl, 2 * r, 2 * (j % 2), r == 0, r == 7)


USED = ("x", "c", "ada_w", "ada_b", "norm_g", "ffn_w_up", "ffn_conv_w", "ffn_conv_b", "ffn_w_down", "a_w_in",
        "a_g_v", "a_w_s", "a_b_s", "a_w_out", "final_g", "meta_tokens_2", "a_norm_2", "a_w_in_2", "a_w_out_2",
        "a_lambda_q1_2", "a_lambda_k1_2", "a_lambda_q2_2", "a_lambda_k2_2", "a_subln_2", "kv_norm_2", "w_kv_2",
        "b_norm_2", "b_w_in_2", "b_w_out_2", "b_sinks_2", "final_norm_2")


def rope_constants():
    import numpy as np

    pos = np.concatenate([NM + np.arange(P), np.arange(NM), NM + P + np.arange(P)])
    out = {}

    def angles(rot):
        inv = (500000.0 ** (-np.arange(0, rot, 2, dtype=np.float32) / rot)).astype(np.float32)
        return pos.astype(np.float32)[None, :] * inv[:, None]

    ang = angles(AH // 4)
    half = AH // 8
    out["tab_a"] = np.stack([np.concatenate([np.cos(ang)] * 2), np.concatenate([-np.sin(ang), np.sin(ang)])], 1)
    out["rot_a"] = np.pad(np.roll(np.eye(2 * half), half, 1), ((0, 0), (0, P - 2 * half)))
    ang = angles(BH // 4)
    half = BH // 8
    tab = np.zeros((P, 2, L))
    tab[:, 0] = 1.0
    rot = np.zeros((P, P))
    for h0 in (0, BH):
        tab[h0:h0 + 2 * half, 0] = np.concatenate([np.cos(ang)] * 2)
        tab[h0:h0 + 2 * half, 1] = np.concatenate([-np.sin(ang), np.sin(ang)])
        rot[h0:h0 + 2 * half, h0:h0 + 2 * half] = np.roll(np.eye(2 * half), half, 1)
    out["tab_b"], out["rot_b"] = tab, rot
    tabq = np.zeros((P, 2, 2, 2 * half))
    for i, b in enumerate(XB):
        c0 = BLK[b][0]
        tabq[:, i] = tab[0:2 * half, :, c0:c0 + P].transpose(2, 1, 0)
    out["tab_q"] = tabq
    return {k: np.ascontiguousarray(x.astype(np.float32)) for k, x in out.items()}


def kernel(**inputs):
    import numpy as np
    import concourse.bacc as bacc
    from concourse.bass_utils import run_bass_kernel_spmd

    nc = bacc.Bacc("TRN2", target_bir_lowering=False, num_devices=1)
    arrays, aps = {}, {}
    for name, x in [(n, inputs[n]) for n in USED] + list(rope_constants().items()):
        x = np.ascontiguousarray(x)
        arrays[f"in_{name}"] = x
        aps[name] = nc.dram_tensor(f"in_{name}", x.shape, mybir.dt.from_np(x.dtype), kind="ExternalInput").ap()
    out = nc.dram_tensor("out", (1, T, D), F32, kind="ExternalOutput").ap()
    program(nc, aps, out)
    r = run_bass_kernel_spmd(nc, [arrays], core_ids=[0])
    return r.results[0]["out"]
```
